# Optimizing a Trainium2 kernel written in Bass

```python
import math
import jax, jax.numpy as jnp
from jax import lax
import numpy as np

D_MODEL = 1024
BATCH = 1
SEQ = 512
DEPTH = 2

N_A_LAYERS = DEPTH // 2
N_B_LAYERS = DEPTH - N_A_LAYERS
MEM_TOKENS = 256
D_FF = 2816
HEAD_DIM = 64
MEM_HEADS = 4
MEM_WIDTH = MEM_HEADS * HEAD_DIM
MLSTM_HEADS = 4
MLSTM_HEAD_DIM = 192
MLSTM_WIDTH = MLSTM_HEADS * MLSTM_HEAD_DIM
MLSTM_CHUNK = 128
CONV_WIDTH = 4
DILATED_GROUPS = ((128, 1), (512, 4), (2048, 16))
HEADS_PER_GROUP = 4
N_DIL_HEADS = HEADS_PER_GROUP * len(DILATED_GROUPS)
DIL_WIDTH = N_DIL_HEADS * HEAD_DIM
A_IN_WIDTH = 4 * MLSTM_WIDTH + 2 * MLSTM_HEADS + MEM_WIDTH
B_IN_WIDTH = DIL_WIDTH + MEM_WIDTH
NUM_BUCKETS = 32
MAX_DISTANCE = 2048
RMS_EPS = 1e-6
NEG_INF = -1e30
ATTN_SCALE = HEAD_DIM ** -0.5


def rms_norm(x, gain):
    xf = x.astype(jnp.float32)
    y = xf * lax.rsqrt(jnp.mean(xf * xf, axis=-1, keepdims=True) + RMS_EPS)
    return (y * gain.astype(jnp.float32)).astype(x.dtype)

def swiglu(h, w_gate, w_up, w_down):
    return (jax.nn.silu(h @ w_gate) * (h @ w_up)) @ w_down

def causal_conv(x, w):
    C = x.shape[-1]
    return lax.conv_general_dilated(x, w[:, None, :].astype(x.dtype), window_strides=(1,),
                                    padding=[(w.shape[0] - 1, 0)],
                                    dimension_numbers=('NWC', 'WIO', 'NWC'),
                                    feature_group_count=C)

def t5_causal_bucket(dist):
    max_exact = NUM_BUCKETS // 2
    d_f = jnp.maximum(dist, 1).astype(jnp.float32)
    large = max_exact + (jnp.log(d_f / max_exact) / math.log(MAX_DISTANCE / max_exact)
                         * (NUM_BUCKETS - max_exact)).astype(jnp.int32)
    large = jnp.minimum(large, NUM_BUCKETS - 1)
    return jnp.where(dist < max_exact, dist, large)

def mlstm_chunkwise(q, k, v, i_pre, f_pre):
    B, S, H, DK = q.shape
    DV = v.shape[-1]
    L = MLSTM_CHUNK
    NC = S // L
    f32 = jnp.float32

    def chunks(t):
        t = t.astype(f32).reshape(B, NC, L, H, *t.shape[3:])
        return jnp.moveaxis(t, 3, 2)

    qc = chunks(q)
    kc = chunks(k) * (DK ** -0.5)
    vc = chunks(v)
    ic = chunks(i_pre)
    logf = jax.nn.log_sigmoid(chunks(f_pre))
    b = jnp.cumsum(logf, axis=-1)
    b_last = b[..., -1]
    a = b_last[..., None] - b + ic

    def step(carry, xs):
        C, n, m = carry
        k_j, v_j, a_j, bl_j = xs
        m_new = jnp.maximum(bl_j + m, jnp.max(a_j, axis=-1))
        w = jnp.exp(a_j - m_new[..., None])
        decay = jnp.exp(bl_j + m - m_new)
        C_new = decay[..., None, None] * C + jnp.einsum('bhl,bhlk,bhlv->bhkv', w, k_j, v_j)
        n_new = decay[..., None] * n + jnp.einsum('bhl,bhlk->bhk', w, k_j)
        return (C_new, n_new, m_new), (C, n, m)

    init = (jnp.zeros((B, H, DK, DV), f32), jnp.zeros((B, H, DK), f32), jnp.zeros((B, H), f32))
    xs = (jnp.moveaxis(kc, 1, 0), jnp.moveaxis(vc, 1, 0), jnp.moveaxis(a, 1, 0), jnp.moveaxis(b_last, 1, 0))
    _, (C0, n0, m0) = lax.scan(step, init, xs)
    C0 = jnp.moveaxis(C0, 0, 1)
    n0 = jnp.moveaxis(n0, 0, 1)
    m0 = jnp.moveaxis(m0, 0, 1)

    causal = jnp.tril(jnp.ones((L, L), dtype=bool))
    Dlog = jnp.where(causal, b[..., :, None] - b[..., None, :] + ic[..., None, :], NEG_INF)
    g = b + m0[..., None]
    m_t = jnp.maximum(g, jnp.max(Dlog, axis=-1))
    W = jnp.exp(Dlog - m_t[..., None]) * jnp.einsum('bchtk,bchsk->bchts', qc, kc)
    inter = jnp.exp(g - m_t)
    num = jnp.einsum('bchts,bchsv->bchtv', W, vc) + inter[..., None] * jnp.einsum('bchtk,bchkv->bchtv', qc, C0)
    den = jnp.sum(W, axis=-1) + inter * jnp.einsum('bchtk,bchk->bcht', qc, n0)
    h = num / jnp.maximum(jnp.abs(den), jnp.exp(-m_t))[..., None]
    return jnp.moveaxis(h, 2, 3).reshape(B, S, H, DV)

def dilated_group_attention(q, k, v, bias_table, window, dilation):
    B, S, H, E = q.shape
    blk = window // dilation
    span = window
    Lp = -(-S // span) * span
    nb = Lp // span
    pad = ((0, 0), (0, Lp - S), (0, 0), (0, 0))

    def to_blocks(t):
        t = jnp.pad(t.astype(jnp.float32), pad).reshape(B, Lp // dilation, dilation, H, E)
        return jnp.transpose(t, (0, 2, 1, 3, 4)).reshape(B, dilation, nb, blk, H, E)

    qb = to_blocks(q)
    kb = to_blocks(k)
    vb = to_blocks(v)
    prev = lambda t: jnp.pad(t, ((0, 0), (0, 0), (1, 0), (0, 0), (0, 0), (0, 0)))[:, :, :-1]
    kk = jnp.concatenate([prev(kb), kb], axis=3)
    vv = jnp.concatenate([prev(vb), vb], axis=3)

    qi = jnp.arange(blk)[:, None]
    kj = jnp.arange(2 * blk)[None, :]
    m_off = qi + blk - kj
    band = (m_off >= 0) & (m_off <= blk)
    bucket = t5_causal_bucket(jnp.clip(m_off, 0, blk) * dilation)
    bias = jnp.transpose(bias_table.astype(jnp.float32)[bucket], (2, 0, 1))
    n_idx = jnp.arange(nb)[:, None, None]
    allowed = band[None] & ~((n_idx == 0) & (kj[None] < blk))

    s = jnp.einsum('brnqhe,brnkhe->brnhqk', qb, kk) * ATTN_SCALE + bias
    s = jnp.where(allowed[:, None], s, NEG_INF)
    mx = jnp.max(s, axis=-1, keepdims=True)
    p = jnp.exp(s - mx)
    den = jnp.sum(p, axis=-1)
    out = jnp.einsum('brnhqk,brnkhe->brnqhe', p, vv) / jnp.moveaxis(den, 3, 4)[..., None]
    lse = mx[..., 0] + jnp.log(den)

    out = jnp.transpose(out.reshape(B, dilation, Lp // dilation, H, E), (0, 2, 1, 3, 4)).reshape(B, Lp, H, E)[:, :S]
    lse = jnp.moveaxis(lse, 3, 4).reshape(B, dilation, Lp // dilation, H)
    lse = jnp.transpose(lse, (0, 2, 1, 3)).reshape(B, Lp, H)[:, :S]
    return out, lse

def memory_cross_attention(q_mem, mem_n, w_mem_kv, q_gain, k_gain):
    B, S, _ = q_mem.shape
    M = mem_n.shape[1]
    q = rms_norm(q_mem.reshape(B, S, MEM_HEADS, HEAD_DIM), q_gain)
    kv = mem_n @ w_mem_kv
    k = rms_norm(kv[..., :MEM_WIDTH].reshape(B, M, MEM_HEADS, HEAD_DIM), k_gain)
    v = kv[..., MEM_WIDTH:].reshape(B, M, MEM_HEADS, HEAD_DIM)
    s = jnp.einsum('bshe,bmhe->bhsm', q.astype(jnp.float32), k.astype(jnp.float32)) * ATTN_SCALE
    p = jax.nn.softmax(s, axis=-1)
    out = jnp.einsum('bhsm,bmhe->bshe', p, v.astype(jnp.float32))
    return out.reshape(B, S, MEM_WIDTH).astype(q_mem.dtype)

def mlstm_mixer(h, mem_n, w_in, conv_w, gate_bias, h_gain, w_out, w_mem_kv, mq_gain, mk_gain):
    B, S, _ = h.shape
    W = MLSTM_WIDTH
    p = h @ w_in
    qk = jax.nn.silu(causal_conv(p[..., :2 * W], conv_w))
    v = p[..., 2 * W:3 * W]
    o = p[..., 3 * W:4 * W]
    gates = p[..., 4 * W:4 * W + 2 * MLSTM_HEADS].astype(jnp.float32) + gate_bias.astype(jnp.float32)
    q_mem = p[..., 4 * W + 2 * MLSTM_HEADS:]
    heads = lambda t: t.reshape(B, S, MLSTM_HEADS, MLSTM_HEAD_DIM)
    cell = mlstm_chunkwise(heads(qk[..., :W]), heads(qk[..., W:]), heads(v),
                           gates[..., :MLSTM_HEADS], gates[..., MLSTM_HEADS:])
    cell = rms_norm(cell, h_gain).reshape(B, S, W)
    h_a = (jax.nn.sigmoid(o.astype(jnp.float32)) * cell).astype(h.dtype)
    h_m = memory_cross_attention(q_mem, mem_n, w_mem_kv, mq_gain, mk_gain)
    return jnp.concatenate([h_a, h_m], axis=-1) @ w_out

def dilated_mixer(h, mem_n, k_sh, v_sh, w_q, q_gain, w_out, rel_bias, w_mem_kv, mq_gain, mk_gain):
    B, S, _ = h.shape
    p = h @ w_q
    q_d = rms_norm(p[..., :DIL_WIDTH].reshape(B, S, len(DILATED_GROUPS), HEADS_PER_GROUP, HEAD_DIM), q_gain)
    outs, lses = [], []
    for g, (window, dilation) in enumerate(DILATED_GROUPS):
        table = rel_bias[:, g * HEADS_PER_GROUP:(g + 1) * HEADS_PER_GROUP]
        o_g, l_g = dilated_group_attention(q_d[:, :, g], k_sh[:, :, g], v_sh[:, :, g], table, window, dilation)
        outs.append(o_g)
        lses.append(l_g)
    outs = jnp.stack(outs, axis=2)
    alpha = jax.nn.softmax(jnp.stack(lses, axis=2), axis=2)
    h_d = (outs * alpha[..., None]).reshape(B, S, DIL_WIDTH).astype(h.dtype)
    h_m = memory_cross_attention(p[..., DIL_WIDTH:], mem_n, w_mem_kv, mq_gain, mk_gain)
    return jnp.concatenate([h_d, h_m], axis=-1) @ w_out

def first_inputs(seed: int = 0) -> dict:
    key = jax.random.key(seed)
    ks = iter(jax.random.split(key, 40))
    nrm = lambda shape, scale: jax.random.normal(next(ks), shape, jnp.float32) * scale
    gain = lambda shape: 1.0 + nrm(shape, 0.02)
    D, F = D_MODEL, D_FF
    return {
        'x': nrm((BATCH, SEQ, D), 1.0),
        'mem': nrm((BATCH, MEM_TOKENS, D), 1.0),
        'ffn1_norm': gain((DEPTH, D)),
        'ffn1_w_gate': nrm((DEPTH, D, F), D ** -0.5),
        'ffn1_w_up': nrm((DEPTH, D, F), D ** -0.5),
        'ffn1_w_down': nrm((DEPTH, F, D), F ** -0.5),
        'ffn2_norm': gain((DEPTH, D)),
        'ffn2_w_gate': nrm((DEPTH, D, F), D ** -0.5),
        'ffn2_w_up': nrm((DEPTH, D, F), D ** -0.5),
        'ffn2_w_down': nrm((DEPTH, F, D), F ** -0.5),
        'mix_norm': gain((DEPTH, D)),
        'mem_norm': gain((DEPTH, D)),
        'w_mem_kv': nrm((DEPTH, D, 2 * MEM_WIDTH), D ** -0.5),
        'mem_q_norm': gain((DEPTH, HEAD_DIM)),
        'mem_k_norm': gain((DEPTH, HEAD_DIM)),
        'a_w_in': nrm((N_A_LAYERS, D, A_IN_WIDTH), D ** -0.5),
        'a_conv': nrm((N_A_LAYERS, CONV_WIDTH, 2 * MLSTM_WIDTH), CONV_WIDTH ** -0.5),
        'a_gate_bias': jnp.concatenate([nrm((N_A_LAYERS, MLSTM_HEADS), 0.1),
                                        3.0 + nrm((N_A_LAYERS, MLSTM_HEADS), 0.5)], axis=-1),
        'a_h_norm': gain((N_A_LAYERS, MLSTM_HEADS, MLSTM_HEAD_DIM)),
        'a_w_out': nrm((N_A_LAYERS, MLSTM_WIDTH + MEM_WIDTH, D), (MLSTM_WIDTH + MEM_WIDTH) ** -0.5),
        'b_w_q': nrm((N_B_LAYERS, D, B_IN_WIDTH), D ** -0.5),
        'b_q_norm': gain((N_B_LAYERS, HEAD_DIM)),
        'b_w_out': nrm((N_B_LAYERS, DIL_WIDTH + MEM_WIDTH, D), (DIL_WIDTH + MEM_WIDTH) ** -0.5),
        'kv_norm': gain((D,)),
        'w_kv': nrm((D, 2 * DIL_WIDTH), D ** -0.5),
        'kv_k_norm': gain((HEAD_DIM,)),
        'rel_bias': nrm((NUM_BUCKETS, N_DIL_HEADS), 0.3),
    }

def first_block(x, mem, ffn1_norm, ffn1_w_gate, ffn1_w_up, ffn1_w_down,
              ffn2_norm, ffn2_w_gate, ffn2_w_up, ffn2_w_down,
              mix_norm, mem_norm, w_mem_kv, mem_q_norm, mem_k_norm,
              a_w_in, a_conv, a_gate_bias, a_h_norm, a_w_out,
              b_w_q, b_q_norm, b_w_out, kv_norm, w_kv, kv_k_norm, rel_bias):
    B, S, _ = x.shape
    n_groups = len(DILATED_GROUPS)
    k_sh = None
    v_sh = None
    for layer in range(DEPTH):
        x = x + 0.5 * swiglu(rms_norm(x, ffn1_norm[layer]), ffn1_w_gate[layer], ffn1_w_up[layer], ffn1_w_down[layer])
        h = rms_norm(x, mix_norm[layer])
        mem_n = rms_norm(mem, mem_norm[layer])
        if layer < N_A_LAYERS:
            ia = layer
            mix = mlstm_mixer(h, mem_n, a_w_in[ia], a_conv[ia], a_gate_bias[ia], a_h_norm[ia], a_w_out[ia],
                              w_mem_kv[layer], mem_q_norm[layer], mem_k_norm[layer])
        else:
            ib = layer - N_A_LAYERS
            mix = dilated_mixer(h, mem_n, k_sh, v_sh, b_w_q[ib], b_q_norm[ib], b_w_out[ib], rel_bias,
                                w_mem_kv[layer], mem_q_norm[layer], mem_k_norm[layer])
        x = x + mix
        x = x + 0.5 * swiglu(rms_norm(x, ffn2_norm[layer]), ffn2_w_gate[layer], ffn2_w_up[layer], ffn2_w_down[layer])
        if layer == N_A_LAYERS - 1:
            kv = rms_norm(x, kv_norm) @ w_kv
            k_sh = rms_norm(kv[..., :DIL_WIDTH].reshape(B, S, N_DIL_HEADS, HEAD_DIM), kv_k_norm)
            k_sh = k_sh.reshape(B, S, n_groups, HEADS_PER_GROUP, HEAD_DIM)
            v_sh = kv[..., DIL_WIDTH:].reshape(B, S, n_groups, HEADS_PER_GROUP, HEAD_DIM)
    return x


GRID_W = 64
CTX_LEN = 256
RWKV_HEADS = 6
GQA_Q_HEADS = 6
GQA_KV_HEADS = 2
GQA_REP = GQA_Q_HEADS // GQA_KV_HEADS
NA_HEADS = 4
RWKV_W = RWKV_HEADS * HEAD_DIM
GQA_W = GQA_Q_HEADS * HEAD_DIM
GQA_KV_W = GQA_KV_HEADS * HEAD_DIM
NA_W = NA_HEADS * HEAD_DIM
D_MIX = RWKV_W + GQA_W + NA_W
DECAY_RANK = 32
ICLR_RANK = 32
RWKV_CONV_W = 3 * RWKV_W + 2 * DECAY_RANK + 2 * ICLR_RANK
RWKV_SPLIT = (RWKV_W, 2 * RWKV_W, 3 * RWKV_W, 3 * RWKV_W + 2 * DECAY_RANK)
_SPLIT_SIZES = (RWKV_CONV_W, RWKV_W, GQA_W, GQA_KV_W, GQA_KV_W, GQA_W, NA_W, NA_W, NA_W, NA_W)
D_IN = sum(_SPLIT_SIZES)
SPLIT_POINTS = tuple(int(s) for s in np.cumsum(_SPLIT_SIZES)[:-1])
Q_BLOCK = 128
NA_WIN_ROWS = 8
NA_WIN_COLS = 16
ROPE_THETA = 10000.0
DEEPNORM_ALPHA = (2 * DEPTH) ** 0.25
DEEPNORM_BETA = (8 * DEPTH) ** -0.25
LN_EPS = 1e-5
GN_EPS = 64e-5


def _layer_norm(x, g, b):
    xf = x.astype(jnp.float32)
    mu = jnp.mean(xf, axis=-1, keepdims=True)
    var = jnp.mean(jnp.square(xf - mu), axis=-1, keepdims=True)
    return ((xf - mu) * lax.rsqrt(var + LN_EPS) * g + b).astype(x.dtype)

def _rms_norm(x, g):
    xf = x.astype(jnp.float32)
    return (xf * lax.rsqrt(jnp.mean(xf * xf, axis=-1, keepdims=True) + RMS_EPS) * g).astype(x.dtype)

def _centred_conv3(x, w):
    xp = jnp.pad(x, ((0, 0), (1, 1), (0, 0)))
    return w[0] * xp[:, :-2] + w[1] * xp[:, 1:-1] + w[2] * xp[:, 2:]

def _axial_rope_tables(n_tokens):
    t = jnp.arange(n_tokens, dtype=jnp.int32)
    row = (t // GRID_W).astype(jnp.float32)
    col = (t % GRID_W).astype(jnp.float32)
    n_freq = HEAD_DIM // 4
    inv_freq = ROPE_THETA ** (-jnp.arange(n_freq, dtype=jnp.float32) / n_freq)
    ang_r = row[:, None] * inv_freq
    ang_c = col[:, None] * inv_freq
    ang = jnp.concatenate([ang_r, ang_r, ang_c, ang_c], axis=-1)
    return jnp.cos(ang), jnp.sin(ang)

def _apply_axial_rope(x, cos, sin):
    x1, x2, x3, x4 = jnp.split(x, 4, axis=-1)
    rotated = jnp.concatenate([-x2, x1, -x4, x3], axis=-1)
    return (x * cos[:, None] + rotated * sin[:, None]).astype(x.dtype)

def _rwkv_inputs(u, conv_w, decay_w0, decay_w2, iclr_a0, iclr_a2, k_k, k_a):
    u = _centred_conv3(u, conv_w).astype(jnp.float32)
    B, T, _ = u.shape
    r, k, v, dd, ad = jnp.split(u, RWKV_SPLIT, axis=-1)
    dd = jnp.tanh(dd.reshape(B, T, 2, DECAY_RANK))
    ad = ad.reshape(B, T, 2, ICLR_RANK)
    w_log = -jax.nn.softplus(-(decay_w0 + jnp.einsum('btdr,drc->btdc', dd, decay_w2))) - 0.5
    decay = jnp.exp(-jnp.exp(w_log))
    iclr = jax.nn.sigmoid(iclr_a0 + jnp.einsum('btdr,drc->btdc', ad, iclr_a2))
    kk = (k * k_k).reshape(B, T, RWKV_HEADS, HEAD_DIM)
    kk = kk * lax.rsqrt(jnp.maximum(jnp.sum(kk * kk, axis=-1, keepdims=True), 1e-12))
    kk = kk.reshape(B, T, RWKV_W)
    kd = k[:, :, None] * (1.0 + (iclr - 1.0) * k_a)
    bd = kk[:, :, None] * iclr

    def heads_t(z):
        return jnp.moveaxis(z.reshape(z.shape[:-1] + (RWKV_HEADS, HEAD_DIM)), 1, 0)

    return (heads_t(r), heads_t(decay), heads_t(kd), heads_t(v), heads_t(kk), heads_t(bd))

def _rwkv7_step(S, inp):
    r, w, k, v, kk, b = inp
    sa = jnp.einsum('bhvk,bhk->bhv', S, kk)
    S = S * w[:, :, None, :] - sa[..., None] * b[:, :, None, :] + v[..., None] * k[:, :, None, :]
    return S, jnp.einsum('bhvk,bhk->bhv', S, r)

def _rwkv_bidir(rin, S0_f, S0_b):
    r, decay, kd, v, kk, bd = rin
    S_f, y_f = lax.scan(_rwkv7_step, S0_f, (r, decay[:, :, 0], kd[:, :, 0], v, kk, bd[:, :, 0]))
    S_b, y_b = lax.scan(_rwkv7_step, S0_b, (r, decay[:, :, 1], kd[:, :, 1], v, kk, bd[:, :, 1]),
                        reverse=True)
    return S_f, S_b, y_f + y_b

def _rwkv_output(ys, rin, r_k, gn_g, gn_b, dtype):
    r, _, kd, v, _, _ = rin
    T, B = ys.shape[:2]
    mu = jnp.mean(ys, axis=-1, keepdims=True)
    var = jnp.mean(jnp.square(ys - mu), axis=-1, keepdims=True)
    yn = ((ys - mu) * lax.rsqrt(var + GN_EPS)).reshape(T, B, RWKV_W) * gn_g + gn_b
    bonus = jnp.sum(jnp.sum(r[:, :, None] * kd * r_k, axis=-1, keepdims=True), axis=2) * v
    return jnp.moveaxis(yn + bonus.reshape(T, B, RWKV_W), 0, 1).astype(dtype)

def _block_attention(q, keys, vals):
    B, T, G, R, D = q.shape
    qb = jnp.moveaxis(q.reshape(B, T // Q_BLOCK, Q_BLOCK, G, R, D), 1, 0) * (D ** -0.5)

    def one_block(qi):
        s = jnp.einsum('bqgrd,bsgd->bgrqs', qi, keys).astype(jnp.float32)
        p = jax.nn.softmax(s, axis=-1).astype(vals.dtype)
        return jnp.einsum('bgrqs,bsgd->bqgrd', p, vals)

    o = lax.map(one_block, qb)
    return jnp.moveaxis(o, 0, 1).reshape(B, T, G * R * D)

def _neighbourhood_attention(q, k, v, k_ctx, v_ctx, rpb):
    B, L, H, D = q.shape
    rows = L // GRID_W
    win_r = min(NA_WIN_ROWS, rows)
    n_nb = win_r * NA_WIN_COLS
    qg = q.reshape(B, rows, GRID_W, H, D) * (D ** -0.5)
    kg = k.reshape(B, rows, GRID_W, H, D)
    vg = v.reshape(B, rows, GRID_W, H, D)
    cols = jnp.arange(GRID_W, dtype=jnp.int32)
    c_start = jnp.clip(cols - NA_WIN_COLS // 2, 0, GRID_W - NA_WIN_COLS)
    c_idx = c_start[:, None] + jnp.arange(NA_WIN_COLS, dtype=jnp.int32)[None, :]
    dc = c_idx - cols[:, None] + (NA_WIN_COLS - 1)

    def row_block(r):
        r_start = jnp.clip(r - win_r // 2, 0, rows - win_r)
        q_r = lax.dynamic_index_in_dim(qg, r, axis=1, keepdims=False)
        k_nb = lax.dynamic_slice_in_dim(kg, r_start, win_r, axis=1)[:, :, c_idx]
        v_nb = lax.dynamic_slice_in_dim(vg, r_start, win_r, axis=1)[:, :, c_idx]
        dr = r_start + jnp.arange(win_r, dtype=jnp.int32) - r + (NA_WIN_ROWS - 1)
        bias = rpb[:, dr[None, :, None], dc[:, None, :]]
        s_nb = jnp.einsum('bqhd,bpqjhd->bhqpj', q_r, k_nb).astype(jnp.float32) + bias
        s_ctx = jnp.einsum('bqhd,bchd->bhqc', q_r, k_ctx).astype(jnp.float32)
        s = jnp.concatenate([s_nb.reshape(B, H, GRID_W, n_nb), s_ctx], axis=-1)
        p = jax.nn.softmax(s, axis=-1).astype(v.dtype)
        p_nb = p[..., :n_nb].reshape(B, H, GRID_W, win_r, NA_WIN_COLS)
        return (jnp.einsum('bhqpj,bpqjhd->bqhd', p_nb, v_nb)
                + jnp.einsum('bhqc,bchd->bqhd', p[..., n_nb:], v_ctx))

    o = lax.map(row_block, jnp.arange(rows, dtype=jnp.int32))
    return jnp.moveaxis(o, 0, 1).reshape(B, L, H * D)

def _layer(x, ctx, c, c_ctx, rope, w_mod, b_mod, w_in, w_out, rwkv_conv, decay_w0, decay_w2,
           iclr_a0, iclr_a2, k_k, k_a, r_k, gn_g, gn_b, q_norm, k_norm, rpb, ln_g, ln_b, update_ctx):
    B, L, _ = x.shape
    cos, sin = rope
    shift, scale, gate = jnp.split(jax.nn.silu(c) @ w_mod + b_mod, 3, axis=-1)
    shift_c, scale_c, gate_c = jnp.split(jax.nn.silu(c_ctx) @ w_mod + b_mod, 3, axis=-1)
    h_lat = x * (1.0 + scale[:, None]) + shift[:, None]
    h_ctx = ctx * (1.0 + scale_c) + shift_c
    ru_l, rg_l, aq_l, ak_l, av_l, ag_l, nq_l, nk_l, nv_l, ng_l = jnp.split(h_lat @ w_in, SPLIT_POINTS, axis=-1)
    ru_c, rg_c, aq_c, ak_c, av_c, ag_c, nq_c, nk_c, nv_c, ng_c = jnp.split(h_ctx @ w_in, SPLIT_POINTS, axis=-1)

    rwkv_params = (rwkv_conv, decay_w0, decay_w2, iclr_a0, iclr_a2, k_k, k_a)
    rin_c = _rwkv_inputs(ru_c, *rwkv_params)
    rin_l = _rwkv_inputs(ru_l, *rwkv_params)
    S0 = jnp.zeros((B, RWKV_HEADS, HEAD_DIM, HEAD_DIM), jnp.float32)
    S_f, S_b, ys_c = _rwkv_bidir(rin_c, S0, S0)
    _, _, ys_l = _rwkv_bidir(rin_l, S_f, S_b)
    yr_l = _rwkv_output(ys_l, rin_l, r_k, gn_g, gn_b, x.dtype)

    def gqa_kv(kx, vx):
        T = kx.shape[1]
        return (_rms_norm(kx.reshape(B, T, GQA_KV_HEADS, HEAD_DIM), k_norm),
                vx.reshape(B, T, GQA_KV_HEADS, HEAD_DIM))

    def gqa_q(qx):
        return _rms_norm(qx.reshape(B, qx.shape[1], GQA_Q_HEADS, HEAD_DIM), q_norm)

    gk_l, gv_l = gqa_kv(ak_l, av_l)
    gk_l = _apply_axial_rope(gk_l, cos, sin)
    gq_l = _apply_axial_rope(gqa_q(aq_l), cos, sin)
    gk_c, gv_c = gqa_kv(ak_c, av_c)
    ya_l = _block_attention(gq_l.reshape(B, L, GQA_KV_HEADS, GQA_REP, HEAD_DIM),
                            jnp.concatenate([gk_c, gk_l], axis=1), jnp.concatenate([gv_c, gv_l], axis=1))

    def na_heads(u):
        return u.reshape(B, u.shape[1], NA_HEADS, HEAD_DIM)

    nk_c, nv_c = na_heads(nk_c), na_heads(nv_c)
    yn_l = _neighbourhood_attention(na_heads(nq_l), na_heads(nk_l), na_heads(nv_l), nk_c, nv_c, rpb)

    y_l = jnp.concatenate([yr_l * jax.nn.silu(rg_l), ya_l * jax.nn.silu(ag_l),
                           yn_l * jax.nn.silu(ng_l)], axis=-1) @ w_out
    x = _layer_norm(DEEPNORM_ALPHA * x + gate[:, None] * y_l, ln_g, ln_b)

    if update_ctx:
        n_ctx = ctx.shape[1]
        yr_c = _rwkv_output(ys_c, rin_c, r_k, gn_g, gn_b, ctx.dtype)
        ya_c = _block_attention(gqa_q(aq_c).reshape(B, n_ctx, GQA_KV_HEADS, GQA_REP, HEAD_DIM), gk_c, gv_c)
        yn_c = _block_attention(na_heads(nq_c)[:, :, :, None], nk_c, nv_c)
        y_c = jnp.concatenate([yr_c * jax.nn.silu(rg_c), ya_c * jax.nn.silu(ag_c),
                               yn_c * jax.nn.silu(ng_c)], axis=-1) @ w_out
        ctx = _layer_norm(DEEPNORM_ALPHA * ctx + gate_c * y_c, ln_g, ln_b)
    else:
        ctx = None
    return x, ctx

def second_inputs(seed: int = 0) -> dict:
    key = jax.random.key(seed)
    ks = jax.random.split(key, 24)

    def n(k, shape):
        return jax.random.normal(k, shape, jnp.float32)

    inv_d = D_MODEL ** -0.5
    return {
        'x': n(ks[0], (BATCH, SEQ, D_MODEL)),
        'c': n(ks[1], (BATCH, D_MODEL)),
        'ctx': n(ks[2], (BATCH, CTX_LEN, D_MODEL)),
        'c_ctx': n(ks[3], (D_MODEL,)),
        'w_mod': n(ks[4], (DEPTH, D_MODEL, 3 * D_MODEL)) * (0.5 * inv_d),
        'b_mod': 0.01 * n(ks[5], (DEPTH, 3 * D_MODEL)),
        'w_in': n(ks[6], (DEPTH, D_MODEL, D_IN)) * inv_d,
        'w_out': n(ks[7], (DEPTH, D_MIX, D_MODEL)) * (DEEPNORM_BETA * D_MIX ** -0.5),
        'rwkv_conv': jnp.array([0.25, 0.5, 0.25], jnp.float32)[None, :, None]
                     + 0.05 * n(ks[8], (DEPTH, 3, RWKV_CONV_W)),
        'decay_w0': n(ks[9], (DEPTH, 2, RWKV_W)),
        'decay_w2': 0.1 * n(ks[10], (DEPTH, 2, DECAY_RANK, RWKV_W)),
        'iclr_a0': 0.5 * n(ks[11], (DEPTH, 2, RWKV_W)),
        'iclr_a2': 0.1 * n(ks[12], (DEPTH, 2, ICLR_RANK, RWKV_W)),
        'rwkv_k_k': 0.85 + 0.05 * n(ks[13], (DEPTH, RWKV_W)),
        'rwkv_k_a': 1.0 + 0.05 * n(ks[14], (DEPTH, RWKV_W)),
        'rwkv_r_k': 0.1 * n(ks[15], (DEPTH, RWKV_HEADS, HEAD_DIM)),
        'rwkv_gn_g': 1.0 + 0.05 * n(ks[16], (DEPTH, RWKV_W)),
        'rwkv_gn_b': 0.01 * n(ks[17], (DEPTH, RWKV_W)),
        'gqa_q_norm': 1.0 + 0.05 * n(ks[18], (DEPTH, HEAD_DIM)),
        'gqa_k_norm': 1.0 + 0.05 * n(ks[19], (DEPTH, HEAD_DIM)),
        'na_rpb': 0.1 * n(ks[20], (DEPTH, NA_HEADS, 2 * NA_WIN_ROWS - 1, 2 * NA_WIN_COLS - 1)),
        'ln_g': 1.0 + 0.05 * n(ks[21], (DEPTH, D_MODEL)),
        'ln_b': 0.01 * n(ks[22], (DEPTH, D_MODEL)),
    }

def second_block(x, c, ctx, c_ctx, w_mod, b_mod, w_in, w_out, rwkv_conv, decay_w0, decay_w2,
              iclr_a0, iclr_a2, rwkv_k_k, rwkv_k_a, rwkv_r_k, rwkv_gn_g, rwkv_gn_b,
              gqa_q_norm, gqa_k_norm, na_rpb, ln_g, ln_b):
    rope = _axial_rope_tables(x.shape[1])
    for l in range(DEPTH):
        x, ctx = _layer(x, ctx, c, c_ctx, rope, w_mod[l], b_mod[l], w_in[l], w_out[l], rwkv_conv[l],
                        decay_w0[l], decay_w2[l], iclr_a0[l], iclr_a2[l], rwkv_k_k[l], rwkv_k_a[l],
                        rwkv_r_k[l], rwkv_gn_g[l], rwkv_gn_b[l], gqa_q_norm[l], gqa_k_norm[l],
                        na_rpb[l], ln_g[l], ln_b[l], l < DEPTH - 1)
    return x


def setup_inputs(seed=0):
    out = dict(first_inputs(seed))
    for name, value in second_inputs(seed + 1).items():
        if name != "x":
            out[name + "_2"] = value
    return out


def reference(
    x, mem, ffn1_norm, ffn1_w_gate, ffn1_w_up, ffn1_w_down, ffn2_norm, ffn2_w_gate, ffn2_w_up,
    ffn2_w_down, mix_norm, mem_norm, w_mem_kv, mem_q_norm, mem_k_norm, a_w_in, a_conv,
    a_gate_bias, a_h_norm, a_w_out, b_w_q, b_q_norm, b_w_out, kv_norm, w_kv, kv_k_norm,
    rel_bias, c_2, ctx_2, c_ctx_2, w_mod_2, b_mod_2, w_in_2, w_out_2, rwkv_conv_2, decay_w0_2,
    decay_w2_2, iclr_a0_2, iclr_a2_2, rwkv_k_k_2, rwkv_k_a_2, rwkv_r_k_2, rwkv_gn_g_2,
    rwkv_gn_b_2, gqa_q_norm_2, gqa_k_norm_2, na_rpb_2, ln_g_2, ln_b_2,
):
    x = first_block(
        x, mem, ffn1_norm, ffn1_w_gate, ffn1_w_up, ffn1_w_down, ffn2_norm, ffn2_w_gate,
        ffn2_w_up, ffn2_w_down, mix_norm, mem_norm, w_mem_kv, mem_q_norm, mem_k_norm, a_w_in,
        a_conv, a_gate_bias, a_h_norm, a_w_out, b_w_q, b_q_norm, b_w_out, kv_norm, w_kv,
        kv_k_norm, rel_bias,
    )
    return second_block(
        x, c_2, ctx_2, c_ctx_2, w_mod_2, b_mod_2, w_in_2, w_out_2, rwkv_conv_2, decay_w0_2,
        decay_w2_2, iclr_a0_2, iclr_a2_2, rwkv_k_k_2, rwkv_k_a_2, rwkv_r_k_2, rwkv_gn_g_2,
        rwkv_gn_b_2, gqa_q_norm_2, gqa_k_norm_2, na_rpb_2, ln_g_2, ln_b_2,
    )


_drawn_inputs = setup_inputs


def setup_inputs(seed=0):
    import zlib

    import numpy as np

    out = dict(_drawn_inputs(seed))
    spreads = {}
    factors = {'ffn1_norm': 4.398,
     'ffn2_norm': 5.363,
     'mix_norm': 3.845,
     'mem_norm': 8.0,
     'mem_q_norm': 8.0,
     'mem_k_norm': 8.0,
     'a_h_norm': 6.356,
     'b_q_norm': 8.0,
     'kv_norm': 8.0,
     'kv_k_norm': 8.0,
     'rel_bias': 3.361,
     'ctx_2': 8.0,
     'c_ctx_2': 4.748,
     'b_mod_2': 8.0,
     'decay_w2_2': 8.0,
     'iclr_a0_2': 3.599,
     'iclr_a2_2': 3.911,
     'rwkv_k_k_2': 38.381,
     'rwkv_k_a_2': 8.0,
     'rwkv_gn_g_2': 24.691,
     'rwkv_gn_b_2': 190.705,
     'gqa_q_norm_2': 109.091,
     'gqa_k_norm_2': 130.481,
     'na_rpb_2': 64.0,
     'ln_b_2': 4.156}
    for name, (base, spread) in spreads.items():
        noise = np.random.default_rng([zlib.crc32(name.encode()), seed]).standard_normal(out[name].shape)
        drawn = base * np.exp(spread * noise) if base else spread * noise
        out[name] = __import__('jax').numpy.asarray(drawn.astype(out[name].dtype))
    for name, factor in factors.items():
        out[name] = (out[name] * factor).astype(out[name].dtype)
    return out
```

```python
from contextlib import ExitStack

import concourse.bass as bass
from concourse import mybir
from concourse.alu_op_type import AluOpType as ALU

F32 = mybir.dt.float32
ACT = mybir.ActivationFunctionType
AX_X = mybir.AxisListType.X

P = 128
D = 1024
KT = D // P
S = 512
M = 256
CTX = 256
F = 2816
FT = F // P
HD = 64
SCALE = HD ** -0.5
RMS_EPS = 1e-6
LN_EPS = 1e-5
GN_EPS = 64e-5
ALPHA = 4 ** 0.25

ML_H, ML_D = 4, 192
RING = 4
CHUNK = 2048
DOWN = FT // 2 * P
ARENA = 53000


class Core:

    def __init__(self, nc, ctx, dram, cols, consts, plan):
        self.nc, self.ctx, self.dram, self.plan = nc, ctx, dram, plan
        self.arena = ctx.enter_context(nc.sbuf_tensor("arena", [P, ARENA], F32))
        self.psum = ctx.enter_context(nc.psum_tensor("psum", [P, 8, 512], F32))
        self.top = 0
        self.sems, self.count, self.base = {}, {}, {}
        self.col_at, self.const_at = cols, consts
        self.used = 0
        self.issued = 0
        self.free_at = {}
        self.ring = self.alloc(RING, CHUNK)

    def alloc(self, *shape):
        n = 1
        for x in shape:
            n *= x
        flat = self.arena[:, self.top:self.top + n]
        self.top += n
        assert self.top <= ARENA, self.top
        if len(shape) == 1:
            return flat
        names = "abcd"[:len(shape)]
        text = "p (" + " ".join(names) + ") -> p " + " ".join(names)
        return flat.rearrange(text, **dict(zip(names, shape)))

    def up(self, name, n=1):
        if name not in self.sems:
            self.sems[name] = self.ctx.enter_context(self.nc.semaphore(name))
            self.count[name] = 0
            self.base.setdefault(name, 0)
        self.count[name] += n
        return self.sems[name], n

    def at(self, name, i, step=1):
        if name not in self.sems:
            self.sems[name] = self.ctx.enter_context(self.nc.semaphore(name))
            self.count[name] = 0
            self.base[name] = 0
        assert i >= 0
        return self.sems[name], self.base.get(name, 0) + (i + 1) * step

    def now(self, name):
        return self.sems[name], self.count[name]

    def stage(self):
        self.base = dict(self.count)
        return self.nc.Block()

    def link(self, eng, ins, name):
        sem, n = self.up(name)
        ins.then_inc(sem, n)
        eng.wait_ge(sem, self.count[name])

    def const(self, name):
        a, n = self.const_at[name]
        return self.consts_sb[:, a:a + n]

    def col(self, name):
        a, n = self.col_at[name]
        return self.cols_sb[:, a:a + n]

    def take(self, n):
        first = self.used
        self.used += n
        return first

    def slot(self, c):
        return self.ring[:, c % RING, :]

    def landed(self, c):
        sem, n = self.up(f"chunk_landed_{c % RING}", 0)
        return sem, 16 * (c // RING + 1)

    def frees(self, c, name):
        self.free_at[c] = (self.sems[name], self.count[name])

    def stream(self, sp):
        while self.issued < min(self.used + RING, len(self.plan)):
            c = self.issued
            name, row, n = self.plan[c]
            if c - RING in self.free_at:
                sp.wait_ge(*self.free_at[c - RING])
            sp.dma_start(self.slot(c)[:, 0:n], self.dram[name][row, :, 0:n]).then_inc(
                *self.up(f"chunk_landed_{c % RING}", 16))
            self.issued += 1


def rms_norm(K, src, n, gain, dst):
    top = K.top
    sq, std, rstd = K.alloc(2, 512), K.alloc(512), K.alloc(512)
    total = K.psum[:, 0, 0:n]
    with K.stage() as block:
        @block.scalar
        def _(act):
            for k in range(KT):
                if k >= 2:
                    act.wait_ge(*K.at("square_summed", k - 2))
                act.activation(sq[:, k % 2, 0:n], src[:, k, :], ACT.Square).then_inc(*K.up("square_ready"))
            act.wait_ge(*K.at("square_summed", KT - 1))
            act.activation(std[:, 0:n], total, ACT.Sqrt, scale=1.0 / D,
                           bias=K.const("eps_rms")).then_inc(*K.up("std_ready"))

        @block.tensor
        def _(pe):
            for k in range(KT):
                pe.wait_ge(*K.at("square_ready", k))
                pe.matmul(total, K.const("ones"), sq[:, k % 2, 0:n], start=k == 0,
                          stop=k == KT - 1).then_inc(*K.up("square_summed"))

        @block.vector
        def _(dve):
            dve.wait_ge(*K.at("std_ready", 0))
            K.link(dve, dve.reciprocal(rstd[:, 0:n], std[:, 0:n]), "dve_step")
            for k in range(KT):
                dve.scalar_tensor_tensor(dst[:, k, :], src[:, k, :], gain[:, k:k + 1], rstd[:, 0:n],
                                         ALU.mult, ALU.mult)
    K.top = top


def ffn(K, x_T, gain):
    top = K.top
    h_T = K.alloc(KT, S)
    rms_norm(K, x_T, S, gain, h_T)
    act_T, gate = K.alloc(FT, S), K.alloc(2, S)
    up0 = K.take(FT)
    down0 = K.take(KT * 2)
    with K.stage() as block:
        @block.tensor
        def _(pe):
            for f in range(FT):
                pe.wait_ge(*K.landed(up0 + f))
                if f >= 2:
                    pe.wait_ge(*K.at("hidden_ready", f - 2))
                w = K.slot(up0 + f).rearrange("p (k n) -> p k n", k=KT)
                for part in range(2):
                    for k in range(KT):
                        mm = pe.matmul(K.psum[:, 2 * (f % 2) + part, :], w[:, k, part * P:(part + 1) * P],
                                       h_T[:, k, :], start=k == 0, stop=k == KT - 1)
                mm.then_inc(*K.up("gate_up_ready"))
                K.frees(up0 + f, "gate_up_ready")
            for d in range(KT):
                if d >= 4:
                    pe.wait_ge(*K.at("x_updated", d - 4))
                for half in range(2):
                    pe.wait_ge(*K.landed(down0 + 2 * d + half))
                    if d == 0 and half == 0:
                        pe.wait_ge(*K.at("hidden_ready", FT - 1))
                    w = K.slot(down0 + 2 * d + half)[:, 0:DOWN].rearrange("p (f n) -> p f n", f=FT // 2)
                    for f in range(FT // 2):
                        mm = pe.matmul(K.psum[:, 4 + d % 4, :], w[:, f, :], act_T[:, half * (FT // 2) + f, :],
                                       start=half + f == 0, stop=half == 1 and f == FT // 2 - 1)
                    mm.then_inc(*K.up("half_summed"))
                    K.frees(down0 + 2 * d + half, "half_summed")

        @block.sync
        def _(sp):
            K.stream(sp)

        @block.scalar
        def _(act):
            for f in range(FT):
                act.wait_ge(*K.at("gate_up_ready", f))
                if f >= 2:
                    act.wait_ge(*K.at("hidden_ready", f - 2))
                act.activation(gate[:, f % 2, :], K.psum[:, 2 * (f % 2), :], ACT.Silu).then_inc(*K.up("gate_ready"))

        @block.vector
        def _(dve):
            for f in range(FT):
                dve.wait_ge(*K.at("gate_ready", f))
                dve.tensor_tensor(act_T[:, f, :], gate[:, f % 2, :], K.psum[:, 2 * (f % 2) + 1, :],
                                  ALU.mult).then_inc(*K.up("hidden_ready"))
            for d in range(KT):
                dve.wait_ge(*K.at("half_summed", 2 * d + 1))
                dve.scalar_tensor_tensor(x_T[:, d, :], K.psum[:, 4 + d % 4, :], 0.5, x_T[:, d, :],
                                         ALU.mult, ALU.add).then_inc(*K.up("x_updated"))
    K.top = top


class Job:

    def __init__(self, chunk, c0, cn, width, src, n, engine, evacuate, tokens=None):
        self.chunk, self.c0, self.cn, self.width = chunk, c0, cn, width
        self.src, self.n, self.engine, self.evacuate, self.tokens = src, n, engine, evacuate, tokens


def copy_to(out):
    def evacuate(K, eng, ps):
        if eng is K.nc.scalar:
            return eng.copy(out, ps)
        return eng.tensor_copy(out, ps)
    return evacuate


def act_to(out, func):
    def evacuate(K, eng, ps):
        return eng.activation(out, ps, func)
    return evacuate


def project(K, jobs, n_chunks, also=None):
    c0 = K.take(n_chunks)
    order = {"act": [j for j, job in enumerate(jobs) if job.engine == "act"],
             "dve": [j for j, job in enumerate(jobs) if job.engine == "dve"]}
    with K.stage() as block:
        @block.tensor
        def _(pe):
            for j, job in enumerate(jobs):
                c = c0 + job.chunk
                if j == 0 or jobs[j - 1].chunk != job.chunk:
                    pe.wait_ge(*K.landed(c))
                if j >= 4:
                    e = jobs[j - 4].engine
                    pe.wait_ge(*K.at(f"{e}_evacuated", order[e].index(j - 4)))
                w = K.slot(c)[:, 0:len(job.src) * job.width].rearrange("p (k n) -> p k n", k=len(job.src))
                ps = K.psum[:, 2 * (j % 4):2 * (j % 4) + 2, :].rearrange("p a b -> p (a b)")
                for k, s in enumerate(job.src):
                    rows = s.shape[0]
                    cols = w[0:rows, k, job.c0:job.c0 + job.cn]
                    flags = dict(start=k == 0, stop=k == len(job.src) - 1)
                    if job.tokens is not None:
                        mm = pe.matmul(ps[0:P, 0:job.cn], job.tokens(s), cols, **flags)
                    else:
                        for a in range(0, job.n, 512):
                            b = min(job.n, a + 512)
                            mm = pe.matmul(ps[0:job.cn, a:b], cols, s[:, a:b], **flags)
                last = j == len(jobs) - 1 or jobs[j + 1].chunk != job.chunk
                mm.then_inc(*K.up("product_ready"))
                if last:
                    K.frees(c, "product_ready")

        @block.sync
        def _(sp):
            K.stream(sp)

        def evacuation(eng, name):
            for j in order[name]:
                job = jobs[j]
                rows, n = (P, job.cn) if job.tokens is not None else (job.cn, job.n)
                ps = K.psum[:, 2 * (j % 4):2 * (j % 4) + 2, :].rearrange("p a b -> p (a b)")[0:rows, 0:n]
                eng.wait_ge(*K.at("product_ready", j))
                job.evacuate(K, eng, ps).then_inc(*K.up(f"{name}_evacuated"))

        @block.scalar
        def _(act):
            evacuation(act, "act")

        @block.vector
        def _(dve):
            evacuation(dve, "dve")


def head_norm(K, tiles, n, gain, eps=RMS_EPS):
    top = K.top
    sq, std = K.alloc(2, 1024), K.alloc(2, 1024)
    with K.stage() as block:
        @block.scalar
        def _(act):
            for i, x in enumerate(tiles):
                if i >= 2:
                    act.wait_ge(*K.at("square_summed", i - 2))
                act.activation(sq[:, i % 2, 0:n], x, ACT.Square).then_inc(*K.up("square_ready"))
                act.wait_ge(*K.at("square_summed", i))
                if i >= 2:
                    act.wait_ge(*K.at("head_normed", i - 2))
                ps = K.psum[:, 2 * (i % 2):2 * (i % 2) + 2, :].rearrange("p a b -> p (a b)")
                act.activation(std[:, i % 2, 0:n], ps[:, 0:n], ACT.Sqrt, scale=1.0 / HD,
                               bias=K.const("eps_rms")).then_inc(*K.up("std_ready"))

        @block.tensor
        def _(pe):
            for i in range(len(tiles)):
                pe.wait_ge(*K.at("square_ready", i))
                if i >= 2:
                    pe.wait_ge(*K.at("std_ready", i - 2))
                ps = K.psum[:, 2 * (i % 2):2 * (i % 2) + 2, :].rearrange("p a b -> p (a b)")
                for a in range(0, n, 512):
                    b = min(n, a + 512)
                    mm = pe.matmul(ps[:, a:b], K.const("head_ones"), sq[:, i % 2, a:b], start=True, stop=True)
                mm.then_inc(*K.up("square_summed"))

        @block.vector
        def _(dve):
            for i, x in enumerate(tiles):
                dve.wait_ge(*K.at("std_ready", i))
                r = std[:, i % 2, 0:n]
                K.link(dve, dve.reciprocal(r, r), "dve_step")
                dve.scalar_tensor_tensor(x, x, gain, r, ALU.mult, ALU.mult).then_inc(*K.up("head_normed"))
    K.top = top


def block_of(t):
    return lambda x: x[:, t * P:(t + 1) * P]


def as_shape(x, like):
    if len(like.shape) == 2:
        return x
    return x.rearrange("p (a b) -> p a b", a=like.shape[1])


class Unit:

    def __init__(self, half, q, keys, values, out, bias=None, lse=None):
        self.half, self.q, self.keys, self.values = half, q, keys, values
        self.out, self.bias, self.lse = out, bias, lse
        self.n = P * len(values)


def attention(K, units):
    top = K.top
    width = max(u.n for u in units)
    probs, probs_T = K.alloc(2, width), K.alloc(2, width)
    scored = K.alloc(2, width)
    peak, bound, total, inverse = (K.alloc(len(units)) for _ in range(4))

    def scores_ps(u):
        return K.psum[:, 2 * (u % 2):2 * (u % 2) + 2, :].rearrange("p a b -> p (a b)")
    turned_ps = K.psum[:, 4:6, :].rearrange("p a b -> p (a b)")
    with K.stage() as block:
        @block.tensor
        def _(pe):
            def scores(u):
                unit = units[u]
                n = unit.n
                rows = slice(64 * unit.half, 64 * unit.half + 64)
                if u >= 2:
                    pe.wait_ge(*K.at("probs_ready", u - 2))
                if n <= 512:
                    mm = pe.matmul(scores_ps(u)[:, 0:n], unit.q, unit.keys, start=True, stop=True)
                else:
                    for a in range(0, n, 512):
                        b = min(n, a + 512)
                        mm = pe.matmul(scores_ps(u)[:, a:b], unit.q, unit.keys[:, a:b], start=True, stop=True)
                mm.then_inc(*K.up("scores_ready"))

            def outputs(u):
                unit = units[u]
                blocks = len(unit.values)
                pe.wait_ge(*K.at("probs_scaled", u))
                if u >= 1:
                    pe.wait_ge(*K.at("turned_copied", u - 1))
                for b in range(blocks):
                    mm = pe.transpose(turned_ps[:, b * P:(b + 1) * P], probs[:, u % 2, b * P:(b + 1) * P],
                                      K.const("identity"))
                mm.then_inc(*K.up("turned_ready"))
                pe.wait_ge(*K.at("turned_copied", u))
                if u >= 2:
                    pe.wait_ge(*K.at("output_copied", u - 2))
                for b in range(blocks):
                    mm = pe.matmul(K.psum[:, 6 + u % 2, 0:P], unit.values[b], probs_T[:, u % 2, b * P:(b + 1) * P],
                                   start=b == 0, stop=b == blocks - 1)
                mm.then_inc(*K.up("output_ready"))

            for u in range(len(units) + 1):
                if u < len(units):
                    scores(u)
                if u >= 1:
                    outputs(u - 1)

        @block.vector
        def _(dve):
            def find_peak(u):
                unit = units[u]
                n = unit.n
                dve.wait_ge(*K.at("scores_ready", u))
                source = scores_ps(u)[:, 0:n]
                factor = -SCALE
                if unit.bias is not None:
                    dve_in = source
                    source = scored[:, u % 2, 0:n]
                    if u >= 2:
                        dve.wait_ge(*K.at("probs_ready", u - 2))
                    free = n - unit.bias.shape[1]
                    if free:
                        dve.tensor_scalar(source[:, 0:free], dve_in[:, 0:free], SCALE, None, ALU.mult)
                    K.link(dve, dve.scalar_tensor_tensor(source[:, free:n], dve_in[:, free:n], SCALE, unit.bias,
                                                         ALU.mult, ALU.add), "dve_step")
                    factor = -1.0
                K.link(dve, dve.tensor_reduce(peak[:, u:u + 1], source, AX_X, ALU.max), "dve_step")
                dve.tensor_scalar(bound[:, u:u + 1], peak[:, u:u + 1], factor, None,
                                  ALU.mult).then_inc(*K.up("bound_ready"))

            def finish(u):
                unit = units[u]
                n = unit.n
                dve.wait_ge(*K.at("probs_ready", u))
                K.link(dve, dve.reciprocal(inverse[:, u:u + 1], total[:, u:u + 1]), "dve_step")
                dve.tensor_scalar(probs[:, u % 2, 0:n], probs[:, u % 2, 0:n], inverse[:, u:u + 1], None,
                                  ALU.mult).then_inc(*K.up("probs_scaled"))

            def copy_out(u):
                unit = units[u]
                rows = slice(64 * unit.half, 64 * unit.half + 64)
                dve.wait_ge(*K.at("output_ready", u))
                dve.tensor_copy(unit.out, as_shape(K.psum[rows, 6 + u % 2, 0:P], unit.out)).then_inc(*K.up("output_copied"))

            for u in range(len(units) + 2):
                if u < len(units):
                    find_peak(u)
                if 1 <= u <= len(units):
                    finish(u - 1)
                if u >= 2:
                    copy_out(u - 2)

        @block.scalar
        def _(act):
            def exponentials(u):
                unit = units[u]
                n = unit.n
                act.wait_ge(*K.at("bound_ready", u))
                if u >= 2:
                    act.wait_ge(*K.at("turned_ready", u - 2))
                source, scale = (scores_ps(u)[:, 0:n], SCALE) if unit.bias is None else (scored[:, u % 2, 0:n], 1.0)
                act.activation(probs[:, u % 2, 0:n], source, ACT.Exp, scale=scale, bias=bound[:, u:u + 1],
                               accum_out=total[:, u:u + 1]).then_inc(*K.up("probs_ready"))

            def turn(u):
                n = units[u].n
                act.wait_ge(*K.at("turned_ready", u))
                if u >= 2:
                    act.wait_ge(*K.at("output_ready", u - 2))
                act.copy(probs_T[:, u % 2, 0:n], turned_ps[:, 0:n]).then_inc(*K.up("turned_copied"))

            for u in range(len(units) + 1):
                if u < len(units):
                    exponentials(u)
                if u >= 1:
                    turn(u - 1)
    if units[0].lse is not None:
        logs = K.alloc(len(units))
        with K.stage() as block:
            @block.scalar
            def _(act):
                act.activation(logs[:, :], total[:, :], ACT.Ln).then_inc(*K.up("log_ready"))

            @block.vector
            def _(dve):
                dve.wait_ge(*K.at("log_ready", 0))
                dve.tensor_tensor(units[0].lse, logs[:, :], bound[:, :], ALU.subtract)
    K.top = top


def memory_attention(K, layer, mem_T, q_mem):
    top = K.top
    mem_n = K.alloc(KT, M)
    rms_norm(K, mem_T, M, K.col(f"mem_norm{layer}"), mem_n)
    k_T, v = K.alloc(2, M), K.alloc(2, 256)
    src = [mem_n[:, k, :] for k in range(KT)]
    jobs = [Job(0, P * i, P, 256, src, M, "act" if i else "dve", copy_to(k_T[:, i, :])) for i in range(2)]
    jobs += [Job(1, 0, 256, 256, src, M, "act" if t else "dve", copy_to(v[:, t, :]), tokens=block_of(t))
             for t in range(2)]
    project(K, jobs, 2)
    head_norm(K, [k_T[:, i, :] for i in range(2)], M, K.col(f"mem_k_norm{layer}"))
    head_norm(K, q_mem, S, K.col(f"mem_q_norm{layer}"))
    units = []
    for t in range(S // P):
        for pair in range(2):
            for half in range(2):
                rows = slice(64 * half, 64 * half + 64)
                q = q_mem[pair][rows, t * P:(t + 1) * P]
                units.append(Unit(half, q, k_T[rows, pair, :],
                                  [v[:, b, pair * P:(pair + 1) * P] for b in range(2)], q))
    attention(K, units)
    K.top = top


def conv_evacuation(out, taps):
    def evacuate(K, eng, ps):
        n = ps.shape[1]
        K.link(eng, eng.tensor_scalar(out, ps, taps[:, 3:4], None, ALU.mult), "dve_step")
        for shift in (1, 2, 3):
            ins = eng.scalar_tensor_tensor(out[:, shift:n], ps[:, 0:n - shift], taps[:, 3 - shift:4 - shift],
                                           out[:, shift:n], ALU.mult, ALU.add)
            if shift < 3:
                K.link(eng, ins, "dve_step")
        return ins
    return evacuate


def add_to(out, row):
    def evacuate(K, eng, ps):
        return eng.tensor_tensor(out, ps, row, ALU.add)
    return evacuate


def residual(x, factor=None):
    def evacuate(K, eng, ps):
        return eng.tensor_tensor(x, ps, x, ALU.add)
    return evacuate


def mlstm_gates(K, gates):
    H, N = ML_H, (S // P) * ML_H
    tiny = lambda: K.alloc(S // P, H)
    b, c, tot, cmax, upto, m0, m1, u, neg_u, inter, wgt, decay, floor, tmp = (tiny() for _ in range(14))
    flat = lambda x: x.rearrange("p a b -> p (a b)")
    masked = K.alloc(N, P)
    top = K.top
    size, soft, logf = tiny(), tiny(), tiny()
    f = gates[:, :, H:2 * H]
    with K.stage() as block:
        @block.vector
        def _(dve):
            dve.scalar_tensor_tensor(size, f, -1.0, f, ALU.mult, ALU.max).then_inc(*K.up("size_ready"))
            dve.wait_ge(*K.at("softplus_ready", 1))
            K.link(dve, dve.tensor_scalar(logf, f, 0.0, None, ALU.min), "dve_step")
            dve.tensor_tensor(logf, logf, soft, ALU.subtract).then_inc(*K.up("logf_ready"))
            dve.wait_ge(*K.at("sums_ready", 0))
            dve.tensor_copy(flat(b), K.psum[:, 0, 0:N])
            K.link(dve, dve.tensor_copy(flat(tot), K.psum[:, 1, 0:N]), "dve_step")
            dve.tensor_tensor(c, gates[:, :, 0:H], b, ALU.subtract).then_inc(*K.up("c_ready"))
            for q in range(4):
                dve.wait_ge(*K.at("c_spread", q))
                rows = K.psum[:, 2 + q, :].rearrange("p (a b) -> p a b", a=4)
                mask = K.const("causal_add").rearrange("p (a b) -> p a b", a=1).to_broadcast([P, 4, P])
                dve.tensor_reduce(cmax[:, q, :], rows, AX_X, ALU.max)
                K.link(dve, dve.tensor_tensor(masked[:, 4 * q:4 * q + 4, :], rows, mask, ALU.add), "dve_step")
                dve.tensor_reduce(upto[:, q, :], masked[:, 4 * q:4 * q + 4, :], AX_X, ALU.max)
            K.link(dve, dve.memset(m0[:, 0, :], 0.0), "dve_step")
            for q in range(S // P):
                K.link(dve, dve.tensor_tensor(m1[:, q, :], m0[:, q, :], cmax[:, q, :], ALU.max), "dve_step")
                if q + 1 < S // P:
                    K.link(dve, dve.tensor_tensor(m0[:, q + 1, :], m1[:, q, :], tot[:, q, :], ALU.add), "dve_step")
            K.link(dve, dve.tensor_tensor(u, m0, upto, ALU.max), "dve_step")
            dve.tensor_scalar(neg_u, u, -1.0, None, ALU.mult)
            dve.tensor_tensor(inter, m0, u, ALU.subtract)
            dve.tensor_tensor(wgt, c, m1, ALU.subtract)
            dve.tensor_tensor(decay, m0, m1, ALU.subtract)
            dve.tensor_tensor(floor, b, u, ALU.add).then_inc(*K.up("exponents_ready"))

        @block.scalar
        def _(act):
            act.wait_ge(*K.at("size_ready", 0))
            act.activation(soft, size, ACT.Exp, scale=-1.0).then_inc(*K.up("softplus_ready"))
            act.wait_ge(*K.at("softplus_ready", 0))
            act.activation(soft, soft, ACT.Ln, bias=1.0).then_inc(*K.up("softplus_ready"))
            act.wait_ge(*K.at("exponents_ready", 0))
            for x in (inter, wgt, decay):
                act.activation(x, x, ACT.Exp)
            act.activation(floor, floor, ACT.Exp, scale=-1.0)
            for j in range(N):
                act.activation(masked[:, j, :], masked[:, j, :], ACT.Exp, bias=flat(neg_u)[:, j:j + 1])

        @block.tensor
        def _(pe):
            pe.wait_ge(*K.at("logf_ready", 0))
            pe.matmul(K.psum[:, 0, 0:N], K.const("upto"), flat(logf), start=True, stop=True)
            pe.matmul(K.psum[:, 1, 0:N], K.const("ones"), flat(logf), start=True, stop=True
                      ).then_inc(*K.up("sums_ready"))
            pe.wait_ge(*K.at("c_ready", 0))
            for j in range(N):
                mm = pe.matmul(K.psum[:, 2 + j // 4, (j % 4) * P:(j % 4 + 1) * P],
                               flat(c)[:, j:j + 1].to_broadcast([P, P]), K.const("identity"), start=True, stop=True)
                if j % 4 == 3:
                    mm.then_inc(*K.up("c_spread"))
    K.top = top
    return masked, inter, wgt, decay, floor


def mlstm_cell(K, q_T, k_T, v1, o_T, gates, h_gain, h_aT):
    top = K.top
    H, C = ML_H, S // P
    weight, inter, wgt, decay, floor = mlstm_gates(K, gates)
    k_tok = K.alloc(2, H, 2, 96)
    memory = K.alloc(H, 2, 193)
    w, w_T = K.alloc(2, H, P), K.alloc(2, H, P)
    num = K.alloc(H, 193)
    square = K.alloc(192)
    den, ss = K.alloc(H), K.alloc(2, H)
    h = K.alloc(2, H, 192)
    bank = lambda i: K.psum[:, i, :]
    s_ps = bank(0).rearrange("p (h t) -> p h t", h=H)
    wt_ps = bank(1).rearrange("p (h t) -> p h t", h=H)
    local_ps = lambda hd: K.psum[:, 2 + hd // 2, (hd % 2) * 193:(hd % 2) * 193 + 193]
    carried_ps = lambda hd: K.psum[:, 4 + hd // 2, (hd % 2) * 193:(hd % 2) * 193 + 193]
    update_ps = lambda hd: K.psum[0:96, 6 + hd % 2, 0:386].rearrange("p (a b) -> p a b", a=2)
    pair_ps = lambda base, g: K.psum[:, base + g, 0:386].rearrange("p (a b) -> p a b", a=2)
    with K.stage() as block:
        @block.tensor
        def _(pe):
            for c in range(C):
                tok = slice(c * P, (c + 1) * P)
                if c >= 1:
                    pe.wait_ge(*K.at("h_gated", c - 1))
                for hd in range(H):
                    for part in range(2):
                        mm = pe.matmul(s_ps[:, hd, :], q_T[0:96, 2 * hd + part, tok], k_T[0:96, 2 * hd + part, tok],
                                       start=part == 0, stop=part == 1)
                mm.then_inc(*K.up("qk_ready"))
                for hd in range(H):
                    if c >= 1:
                        pe.wait_ge(*K.at("memory_updated", 4 * c - 1))
                    for part in range(2):
                        mm = pe.transpose(K.psum[:, 6 + hd // 2, (2 * (hd % 2) + part) * 96:(2 * (hd % 2) + part) * 96 + 96],
                                          k_T[0:96, 2 * hd + part, tok], K.const("identity")[0:96, 0:96])
                mm.then_inc(*K.up("k_turned"))
                pe.wait_ge(*K.at("w_ready", c))
                for hd in range(H):
                    mm = pe.transpose(wt_ps[:, hd, :], w[:, c % 2, hd, :], K.const("identity"))
                mm.then_inc(*K.up("w_turned"))
                if c >= 1:
                    pe.wait_ge(*K.at("memory_updated", 4 * c - 1))
                else:
                    pe.wait_ge(*K.at("memory_cleared", 0))
                for hd in range(H):
                    for part in range(2):
                        mm = pe.matmul(carried_ps(hd), q_T[0:96, 2 * hd + part, tok], memory[0:96, hd, part, :],
                                       start=part == 0, stop=part == 1)
                mm.then_inc(*K.up("carried_ready"))
                pe.wait_ge(*K.at("w_T_ready", c))
                for hd in range(H):
                    mm = pe.matmul(local_ps(hd), w_T[:, c % 2, hd, :], v1[:, c, hd, :], start=True, stop=True)
                mm.then_inc(*K.up("local_ready"))
                pe.wait_ge(*K.at("k_copied", c))
                for hd in range(H):
                    if hd >= 2:
                        pe.wait_ge(*K.at("memory_updated", 4 * c + hd - 2))
                    for part in range(2):
                        mm = pe.matmul(update_ps(hd)[:, part, :], k_tok[:, c % 2, hd, part, :], v1[:, c, hd, :],
                                       start=True, stop=True)
                    mm.then_inc(*K.up("update_ready"))
                pe.wait_ge(*K.at("h_ready", c))
                for hd in range(H):
                    for part in range(2):
                        mm = pe.transpose(K.psum[0:96, hd // 2, (2 * (hd % 2) + part) * P:(2 * (hd % 2) + part) * P + P],
                                          h[:, c % 2, hd, part * 96:(part + 1) * 96], K.const("identity"))
                mm.then_inc(*K.up("h_turned"))

        @block.vector
        def _(dve):
            dve.memset(memory[:, :, :, :], 0.0).then_inc(*K.up("memory_cleared"))
            dve.wait_ge(*K.at("memory_cleared", 0))
            for c in range(C):
                tok = slice(c * P, (c + 1) * P)
                dve.wait_ge(*K.at("qk_ready", c))
                dve.scalar_tensor_tensor(w[:, c % 2, :, :], s_ps, ML_D ** -0.5, weight[:, 4 * c:4 * c + 4, :],
                                         ALU.mult, ALU.mult).then_inc(*K.up("w_ready"))
                dve.wait_ge(*K.at("k_turned", c))
                for hd in range(H):
                    out = k_tok[:, c % 2, hd, :, :].rearrange("p a b -> p (a b)")
                    ins = dve.tensor_scalar(out, K.psum[:, 6 + hd // 2, (hd % 2) * 192:(hd % 2) * 192 + 192],
                                            wgt[:, c, hd:hd + 1], ML_D ** -0.5, ALU.mult, ALU.mult)
                ins.then_inc(*K.up("k_copied"))
                dve.wait_ge(*K.at("local_ready", c))
                dve.wait_ge(*K.at("carried_scaled", c))
                for g in range(2):
                    ins = dve.tensor_tensor(num[:, 2 * g:2 * g + 2, :], num[:, 2 * g:2 * g + 2, :], pair_ps(2, g), ALU.add)
                K.link(dve, ins, "dve_step")
                last = num[:, :, 192]
                K.link(dve, dve.scalar_tensor_tensor(den, last, -1.0, last, ALU.mult, ALU.max), "dve_step")
                K.link(dve, dve.tensor_tensor(den, den, floor[:, c, :], ALU.max), "dve_step")
                K.link(dve, dve.reciprocal(den, den), "dve_step")
                for hd in range(H):
                    ins = dve.tensor_scalar(h[:, c % 2, hd, :], num[:, hd, 0:192], den[:, hd:hd + 1], None, ALU.mult)
                ins.then_inc(*K.up("h_raw"))
                for hd in range(H):
                    dve.wait_ge(*K.at("update_ready", 4 * c + hd))
                    dve.scalar_tensor_tensor(memory[0:96, hd, :, :], memory[0:96, hd, :, :], decay[0:96, c, hd:hd + 1],
                                             update_ps(hd), ALU.mult, ALU.add).then_inc(*K.up("memory_updated"))
                dve.wait_ge(*K.at("h_deviation", c))
                K.link(dve, dve.reciprocal(ss[:, 1, :], ss[:, 1, :]), "dve_step")
                for hd in range(H):
                    ins = dve.tensor_scalar(h[:, c % 2, hd, :], h[:, c % 2, hd, :], ss[:, 1, hd:hd + 1], None, ALU.mult)
                ins.then_inc(*K.up("h_ready"))
                dve.wait_ge(*K.at("h_turned", c))
                for j in range(8):
                    ins = dve.scalar_tensor_tensor(h_aT[0:96, j, tok], K.psum[0:96, j // 4, (j % 4) * P:(j % 4 + 1) * P],
                                                   h_gain[0:96, j:j + 1], o_T[0:96, j, tok], ALU.mult, ALU.mult)
                ins.then_inc(*K.up("h_gated"))

        @block.scalar
        def _(act):
            for c in range(C):
                act.wait_ge(*K.at("w_turned", c))
                act.copy(w_T[:, c % 2, :, :], wt_ps).then_inc(*K.up("w_T_ready"))
                act.wait_ge(*K.at("carried_ready", c))
                if c >= 1:
                    act.wait_ge(*K.at("h_raw", c - 1))
                for hd in range(H):
                    ins = act.mul(num[:, hd, :], carried_ps(hd), inter[:, c, hd:hd + 1])
                ins.then_inc(*K.up("carried_scaled"))
                act.wait_ge(*K.at("h_raw", c))
                if c >= 1:
                    act.wait_ge(*K.at("h_ready", c - 1))
                for hd in range(H):
                    ins = act.activation(square, h[:, c % 2, hd, :], ACT.Square, accum_out=ss[:, 0, hd:hd + 1])
                    ins.then_inc(*K.up("h_squares"))
                    act.wait_ge(*K.at("h_squares", 4 * c + hd))
                act.activation(ss[:, 1, :], ss[:, 0, :], ACT.Sqrt, scale=1.0 / ML_D,
                               bias=K.const("eps_rms")).then_inc(*K.up("h_deviation"))
    K.top = top


def mlstm_layer(K, x_T, mem_T):
    top = K.top
    h_T = K.alloc(KT, S)
    rms_norm(K, x_T, S, K.col("mix_norm0"), h_T)
    qk_T, o_T = K.alloc(16, S), K.alloc(8, S)
    v1 = K.alloc(S // P, ML_H, 193)
    q_mem = K.alloc(2, S)
    gates = K.alloc(S // P, 2 * ML_H)
    h_aT = K.alloc(8, S)
    src = [h_T[:, k, :] for k in range(KT)]
    taps = K.col("a_conv")
    jobs = []
    for j in range(16):
        jobs.append(Job(j // 2, 96 * (j % 2), 96, 192, src, S, "dve",
                        conv_evacuation(qk_T[0:96, j, :], taps[0:96, 4 * j:4 * j + 4])))
    for j in range(8):
        jobs.append(Job(8 + j // 2, 96 * (j % 2), 96, 192, src, S, "act", act_to(o_T[0:96, j, :], ACT.Sigmoid)))
    for hd in range(ML_H):
        for t in range(S // P):
            jobs.append(Job(12 + hd, 0, 192, 192, src, S, "act" if t % 2 else "dve",
                            copy_to(v1[:, t, hd, 0:192]), tokens=block_of(t)))
    for i in range(2):
        jobs.append(Job(16, P * i, P, 256, src, S, "act", copy_to(q_mem[:, i, :])))
    for t in range(S // P):
        jobs.append(Job(17, 0, 8, 8, src, S, "dve", add_to(gates[:, t, :], K.col("a_gate_bias")),
                        tokens=block_of(t)))
    project(K, jobs, 18)
    with K.stage() as block:
        @block.scalar
        def _(act):
            for half in range(2):
                x = qk_T[0:96, 8 * half:8 * half + 8, :]
                act.activation(x, x, ACT.Silu)

        @block.vector
        def _(dve):
            dve.memset(v1[:, :, :, 192:193], 1.0)
    mlstm_cell(K, qk_T[:, 0:8, :], qk_T[:, 8:16, :], v1, o_T, gates, K.col("a_h_norm"), h_aT)
    memory_attention(K, 0, mem_T, [q_mem[:, i, :] for i in range(2)])
    src = [h_aT[0:96, j, :] for j in range(8)] + [q_mem[:, i, :] for i in range(2)]
    jobs = [Job(d, 0, P, P, src, S, "dve", residual(x_T[:, d, :])) for d in range(KT)]
    project(K, jobs, 8)
    K.top = top


def strided_tokens(group, t):
    if group == 0:
        return block_of(t)
    return lambda x: x[:, t:S:4]


def shared_keys(K, x_T, k_T, v):
    top = K.top
    h_T = K.alloc(KT, S)
    rms_norm(K, x_T, S, K.col("kv_norm"), h_T)
    src = [h_T[:, k, :] for k in range(KT)]
    jobs = [Job(i // 2, P * (i % 2), P, 256, src, S, "act" if i % 2 else "dve", copy_to(k_T[:, i, :])) for i in range(6)]
    for g in range(3):
        for t in range(S // P):
            jobs.append(Job(3 + g, 0, 256, 256, src, S, "act" if t % 2 else "dve", copy_to(v[:, g, t, :]),
                            tokens=strided_tokens(g, t)))
    project(K, jobs, 6)
    head_norm(K, [k_T[:, i, :] for i in range(6)], S, K.col("kv_k_norm"))
    K.top = top


def load(K, pairs):
    with K.stage() as block:
        @block.sync
        def _(sp):
            for dst, src in pairs:
                sp.dma_start(dst, src).then_inc(*K.up("array_landed", 16))
            sp.wait_ge(*K.at("array_landed", len(pairs) - 1, 16))


def merge_groups(K, lse, out_T):
    top = K.top
    spread = K.alloc(3, 2, S)
    peak, total = K.alloc(2, S), K.alloc(2, S)
    wide = K.alloc(48, 64)
    with K.stage() as block:
        @block.tensor
        def _(pe):
            pe.wait_ge(*K.at("lse_widened", 0))
            for i in range(24):
                g, pair, t = i // 8, i // 4 % 2, i % 4
                c = (g * 4 + t) * 4 + 2 * pair
                two = wide[:, c:c + 2, :].rearrange("p a b -> p (a b)")
                mm = pe.matmul(K.psum[:, i // 4, t * P:(t + 1) * P], two, K.const("identity"), start=True, stop=True)
                if t == 3:
                    mm.then_inc(*K.up("lse_spread"))

        @block.vector
        def _(dve):
            dve.tensor_copy(wide, lse.rearrange("p (a b) -> p a b", b=1).to_broadcast([P, 48, 64])
                            ).then_inc(*K.up("lse_widened"))
            for i in range(24):
                g, pair, t = i // 8, i // 4 % 2, i % 4
                if t == 0:
                    dve.wait_ge(*K.at("lse_spread", i // 4))
                out = strided_tokens(g, t)(spread[:, g, pair, :])
                ins = dve.tensor_copy(out, as_shape(K.psum[:, i // 4, t * P:(t + 1) * P], out))
            K.link(dve, ins, "dve_step")
            K.link(dve, dve.tensor_tensor(peak, spread[:, 0], spread[:, 1], ALU.max), "dve_step")
            K.link(dve, dve.tensor_tensor(peak, peak, spread[:, 2], ALU.max), "dve_step")
            for g in range(3):
                dve.tensor_tensor(spread[:, g], spread[:, g], peak, ALU.subtract).then_inc(*K.up("lse_shifted"))
            for g in range(3):
                dve.wait_ge(*K.at("weight_ready", g))
            K.link(dve, dve.tensor_tensor(total, spread[:, 0], spread[:, 1], ALU.add), "dve_step")
            K.link(dve, dve.tensor_tensor(total, total, spread[:, 2], ALU.add), "dve_step")
            K.link(dve, dve.reciprocal(total, total), "dve_step")
            for g in range(3):
                K.link(dve, dve.tensor_tensor(spread[:, g], spread[:, g], total, ALU.mult), "dve_step")
                out = out_T[:, 2 * g:2 * g + 2, :]
                dve.tensor_tensor(out, out, spread[:, g], ALU.mult)

        @block.scalar
        def _(act):
            for g in range(3):
                act.wait_ge(*K.at("lse_shifted", g))
                act.activation(spread[:, g], spread[:, g], ACT.Exp).then_inc(*K.up("weight_ready"))
    K.top = top


def dilated_layer(K, x_T, mem_T, k_T, v):
    top = K.top
    bias = K.alloc(4, 512)
    mask = K.alloc(512)
    load(K, [(bias.rearrange("p a b -> p (a b)"), K.dram["dilated_bias"]), (mask, K.dram["dilated_mask"])])
    h_T = K.alloc(KT, S)
    rms_norm(K, x_T, S, K.col("mix_norm1"), h_T)
    q_T = K.alloc(KT, S)
    src = [h_T[:, k, :] for k in range(KT)]
    jobs = [Job(i // 2, P * (i % 2), P, 256, src, S, "act" if i % 2 else "dve", copy_to(q_T[:, i, :]))
            for i in range(KT)]
    project(K, jobs, 4)
    head_norm(K, [q_T[:, i, :] for i in range(6)], S, K.col("b_q_norm"))
    with K.stage() as block:
        @block.vector
        def _(dve):
            every = mask.rearrange("p (a b) -> p a b", a=1).to_broadcast([P, 4, 512])
            dve.tensor_tensor(bias, bias, every, ALU.add)
    lse = K.alloc(48)
    units = []
    for g in range(3):
        for t in range(S // P):
            for head in range(4):
                pair, half = 2 * g + head // 2, head % 2
                rows = slice(64 * half, 64 * half + 64)
                own = strided_tokens(g, t)
                q = own(q_T[rows, pair, :])
                features = slice(P * (head // 2), P * (head // 2) + P)
                if g == 0 and t > 0:
                    keys, blocks, where = k_T[rows, pair, (t - 1) * P:(t + 1) * P], (t - 1, t), slice(0, 256)
                else:
                    keys, blocks = own(k_T[rows, pair, :]), (t,)
                    where = slice((1, 2, 3)[g] * P, (2, 3, 4)[g] * P)
                units.append(Unit(half, q, keys, [v[:, g, b, features] for b in blocks], q,
                                  bias=bias[:, head, where], lse=lse))
    attention(K, units)
    merge_groups(K, lse, q_T[:, 0:6, :])
    memory_attention(K, 1, mem_T, [q_T[:, 6 + i, :] for i in range(2)])
    src = [q_T[:, i, :] for i in range(KT)]
    jobs = [Job(d // 2, P * (d % 2), P, 256, src, S, "dve", residual(x_T[:, d, :])) for d in range(KT)]
    project(K, jobs, 4)
    K.top = top



T2 = CTX + S
LAT = slice(CTX, T2)
RH, CH = 3, 64
NCH, TILES = T2 // CH, T2 // P
LEVELS = (4, 8, 16, 32, 64)
DECAY_SCALE = 0.6065306597126334


def modulation(K, layer, cond, mod):
    bias = K.col(f"b_mod{layer}")

    def shifted(tile):
        def evacuate(K, eng, ps):
            if 8 <= tile < 16:
                return eng.tensor_scalar(mod[:, tile, :], ps, bias[:, tile:tile + 1], 1.0, ALU.add, ALU.add)
            return eng.tensor_scalar(mod[:, tile, :], ps, bias[:, tile:tile + 1], None, ALU.add)
        return evacuate
    src = [cond[:, k, :] for k in range(KT)]
    project(K, [Job(i // 2, P * (i % 2), P, 256, src, 2, "dve", shifted(i)) for i in range(24)], 12)


def centred_evacuation(out, taps):
    def evacuate(K, eng, ps):
        K.link(eng, eng.tensor_scalar(out, ps, taps[:, 1:2], None, ALU.mult), "dve_step")
        for a, b in ((0, CTX), (CTX, T2)):
            ins = eng.scalar_tensor_tensor(out[:, a + 1:b], ps[:, a:b - 1], taps[:, 0:1], out[:, a + 1:b],
                                           ALU.mult, ALU.add)
        K.link(eng, ins, "dve_step")
        for a, b in ((0, CTX), (CTX, T2)):
            ins = eng.scalar_tensor_tensor(out[:, a:b - 1], ps[:, a + 1:b], taps[:, 2:3], out[:, a:b - 1],
                                           ALU.mult, ALU.add)
        return ins
    return evacuate


def rope(K, tiles, cos, sin, turn):
    top = K.top
    straight = K.alloc(2, S)
    with K.stage() as block:
        @block.tensor
        def _(pe):
            for i, x in enumerate(tiles):
                if i >= 2:
                    pe.wait_ge(*K.at("rotated", i - 2))
                pe.matmul(K.psum[:, i % 2, :], turn, x[:, LAT], start=True, stop=True).then_inc(*K.up("turned"))

        @block.vector
        def _(dve):
            for i, x in enumerate(tiles):
                if i >= 2:
                    dve.wait_ge(*K.at("rotated", i - 2))
                K.link(dve, dve.tensor_tensor(straight[:, i % 2, :], x[:, LAT], cos, ALU.mult), "dve_step")
                dve.wait_ge(*K.at("turned", i))
                K.link(dve, dve.tensor_tensor(x[:, LAT], K.psum[:, i % 2, :], sin, ALU.mult), "dve_step")
                dve.tensor_tensor(x[:, LAT], x[:, LAT], straight[:, i % 2, :], ALU.add).then_inc(*K.up("rotated"))
    K.top = top


def rwkv_prepare(K, layer, pair, r, k, ddad, lora, kr, bk, pc, bonus, scratch):
    top = K.top
    ld, L = K.alloc(2, T2), K.alloc(2, T2)
    iclr, decay_before = (scratch[:, i * 2 * T2:(i + 1) * 2 * T2].rearrange("p (d n) -> p d n", d=2) for i in range(2))
    kk, norm = K.alloc(T2), K.alloc(T2)
    less = K.alloc(1)
    col = lambda name, i=pair: K.col(f"{name}{layer}")[:, i:i + 1]
    banks = lambda i: K.psum[:, 2 * i:2 * i + 2, :].rearrange("p a b -> p (a b)")[:, 0:T2]
    parts = ((0, 512), (512, T2))
    tiled = lambda x: x.rearrange("p (t n) -> p t n", n=P)
    with K.stage() as block:
        @block.tensor
        def _(pe):
            for i in range(4):
                rows = slice(32 * i, 32 * i + 32)
                for a, b in parts:
                    mm = pe.matmul(banks(i)[:, a:b], lora[rows, pair * P:(pair + 1) * P], ddad[rows, a:b],
                                   start=True, stop=True)
                mm.then_inc(*K.up("logits_ready"))
            pe.wait_ge(*K.at("kk_squared", 0))
            pe.wait_ge(*K.at("sigmoid_ready", 0))
            for a, b in parts:
                mm = pe.matmul(banks(0)[:, a:b], K.const("head_ones"), norm[:, a:b], start=True, stop=True)
            mm.then_inc(*K.up("kk_summed"))
            pe.wait_ge(*K.at("bonus_terms", 0))
            pe.wait_ge(*K.at("sigmoid_ready", 1))
            for a, b in parts:
                mm = pe.matmul(banks(1)[:, a:b], K.const("head_ones"), bonus[:, a:b], start=True, stop=True)
            mm.then_inc(*K.up("bonus_summed"))

        @block.scalar
        def _(act):
            for i in range(4):
                d, out, bias = i % 2, (ld, iclr)[i // 2], ("decay_w0", "iclr_a0")[i // 2]
                act.wait_ge(*K.at("logits_ready", i))
                act.activation(out[:, d, :], banks(i), ACT.Sigmoid, bias=col(bias, 3 * d + pair)
                               ).then_inc(*K.up("sigmoid_ready"))
            act.wait_ge(*K.at("kk_raw", 0))
            act.activation(norm, kk, ACT.Square).then_inc(*K.up("kk_squared"))
            act.wait_ge(*K.at("norm_bounded", 0))
            act.activation(norm, norm, ACT.Sqrt).then_inc(*K.up("norm_ready"))
            for d in range(2):
                act.wait_ge(*K.at("sum_before", d))
                act.activation(decay_before[:, d, :], decay_before[:, d, :], ACT.Exp).then_inc(*K.up("before_ready"))
                act.activation(ld[:, d, :], L[:, d, :], ACT.Exp, scale=-1.0).then_inc(*K.up("inverse_ready"))
            for d in range(2):
                act.wait_ge(*K.at("inverse_ready", d))
                act.activation(L[:, d, :], L[:, d, :], ACT.Exp).then_inc(*K.up("decay_ready"))

        @block.vector
        def _(dve):
            dve.tensor_scalar(kk, k, col("k_k"), None, ALU.mult).then_inc(*K.up("kk_raw"))
            for d in range(2):
                dve.wait_ge(*K.at("sigmoid_ready", d))
                K.link(dve, dve.tensor_scalar(ld[:, d, :], ld[:, d, :], -DECAY_SCALE, None, ALU.mult), "dve_step")
                turn = slice(None) if d == 0 else slice(None, None, -1)
                K.link(dve, dve.tensor_tensor_scan(L[:, d, turn], K.reset[:, :], ld[:, d, turn], 0.0,
                                                   ALU.mult, ALU.add), "dve_step")
                dve.tensor_tensor(decay_before[:, d, :], L[:, d, :], ld[:, d, :], ALU.subtract
                                  ).then_inc(*K.up("sum_before"))
            dve.wait_ge(*K.at("kk_summed", 0))
            dve.wait_ge(*K.at("kk_squared", 0))
            dve.tensor_scalar(norm, banks(0), 1e-12, None, ALU.max).then_inc(*K.up("norm_bounded"))
            dve.wait_ge(*K.at("norm_ready", 0))
            K.link(dve, dve.reciprocal(norm, norm), "dve_step")
            K.link(dve, dve.tensor_tensor(kk, kk, norm, ALU.mult), "dve_step")
            for d in range(2):
                dve.wait_ge(*K.at("before_ready", d))
                dve.tensor_tensor(kr[:, d, :, 0, :], tiled(kk), tiled(decay_before[:, d, :]), ALU.mult)
            for d in range(2):
                dve.wait_ge(*K.at("sigmoid_ready", 2 + d))
                K.link(dve, dve.tensor_tensor(bk[:, d, 0, :], kk, iclr[:, d, :], ALU.mult), "iclr_used")
                dve.wait_ge(*K.at("inverse_ready", d))
                dve.tensor_tensor(bk[:, d, 0, :], bk[:, d, 0, :], ld[:, d, :], ALU.mult)
            for d in range(2):
                dve.wait_ge(*K.at("keys_ready", d))
                dve.tensor_tensor(bk[:, d, 1, :], iclr[:, d, :], ld[:, d, :], ALU.mult)
                dve.wait_ge(*K.at("decay_ready", d))
                dve.tensor_tensor(kr[:, d, :, 1, :], tiled(r), tiled(L[:, d, :]), ALU.mult)
                first = CH - 1 if d == 0 else 0
                dve.tensor_copy(pc[:, d, :], L[:, d, first:T2:CH])
            dve.wait_ge(*K.at("bonus_summed", 0))
            dve.tensor_copy(bonus, banks(1))

        @block.gpsimd
        def _(pool):
            pool.tensor_scalar(less, col("k_a"), -1.0, 1.0, ALU.mult, ALU.add).then_inc(*K.up("less_ready"))
            pool.wait_ge(*K.at("less_ready", 0))
            for d in range(2):
                pool.wait_ge(*K.at("sigmoid_ready", 2 + d))
                pool.wait_ge(*K.at("iclr_used", d))
                K.link(pool, pool.tensor_scalar(iclr[:, d, :], iclr[:, d, :], col("k_a"), less, ALU.mult, ALU.add),
                       "pool_step")
                pool.tensor_tensor(iclr[:, d, :], iclr[:, d, :], k, ALU.mult).then_inc(*K.up("keys_ready"))
            for d in range(2):
                pool.wait_ge(*K.at("keys_ready", d))
            K.link(pool, pool.tensor_tensor(bonus, iclr[:, 0, :], iclr[:, 1, :], ALU.add), "pool_step")
            K.link(pool, pool.tensor_tensor(bonus, bonus, r, ALU.mult), "pool_step")
            pool.tensor_scalar(bonus, bonus, col("r_k"), None, ALU.mult).then_inc(*K.up("bonus_terms"))
    K.top = top


def rwkv_chunks(K, kr, bk, pc, v, step, carry, y):
    top = K.top
    ab, bd = K.alloc(2, 2, 2, P), K.alloc(2, 2, 2, P)
    corner = K.alloc(2, 4, P)
    T, TT, prod = K.alloc(4, P), K.alloc(4, P), K.alloc(4, P)
    x = K.alloc(4, P)
    b_tok, k_tok, v_tok = K.alloc(2, P), K.alloc(2, P), K.alloc(P)
    kp, nu = K.alloc(2, P), K.alloc(2, P)
    bank = lambda i: K.psum[:, i, :]
    four = lambda i: bank(i).rearrange("p (u t) -> p u t", u=4)
    ident4 = K.const("identity").rearrange("p (a b) -> p a b", a=1).to_broadcast([P, 4, P])
    ident2 = K.const("identity").rearrange("p (a b) -> p a b", a=1).to_broadcast([P, 2, P])
    units = [(d, e) for d in range(2) for e in range(2)]

    def level_mask(d, i):
        return K.level_masks[:, i, d, :].rearrange("p (a b) -> p a b", a=1).to_broadcast([P, 2, P])

    NL = len(LEVELS)
    with K.stage() as block:
        @block.tensor
        def _(pe):
            for t in range(TILES):
                tok = slice(t * P, (t + 1) * P)
                if t >= 1:
                    pe.wait_ge(*K.at("steps_copied", t - 1))
                    pe.wait_ge(*K.at("own_copied", t - 1))
                for d in range(2):
                    pe.transpose(bank(6)[:, d * P:(d + 1) * P], bk[:, d, 0, tok], K.const("identity"))
                    pe.transpose(bank(6)[:, (2 + d) * P:(3 + d) * P], bk[:, d, 1, tok], K.const("identity"))
                    pe.transpose(bank(7)[:, d * P:(d + 1) * P], kr[:, d, t, 0, :], K.const("identity"))
                pe.transpose(bank(7)[:, 2 * P:3 * P], v[:, tok], K.const("identity")).then_inc(*K.up("tokens_turned"))
                for d, e in units:
                    rows = slice(64 * e, 64 * e + 64)
                    rhs = kr[rows, d, t, :, :].rearrange("p a b -> p (a b)")
                    pe.matmul(bank(e)[:, 256 * d:256 * d + 256], bk[rows, d, 0, tok], rhs, start=True, stop=True)
                    pe.matmul(bank(2 + e)[:, 256 * d:256 * d + 256], bk[rows, d, 1, tok], rhs, start=True, stop=True)
                    mm = pe.matmul(bank(4 + e)[:, P * d:P * d + P], kr[rows, d, t, 0, :], bk[rows, d, 0, tok],
                                   start=True, stop=True)
                mm.then_inc(*K.up("scores_done"))
                pe.wait_ge(*K.at("masked", t))
                pe.wait_ge(*K.at("tokens_copied", t))
                for u, (d, e) in enumerate(units):
                    mm = pe.matmul(bank(6)[:, 64 * u:64 * u + 64], bd[:, d, e, 0, :], v_tok[:, 64 * e:64 * e + 64],
                                   start=True, stop=True)
                mm.then_inc(*K.up("bv_ready"))
                for i in range(NL):
                    g = NL * t + i
                    pe.wait_ge(*K.at("corner_ready", g))
                    if i == 0:
                        pe.wait_ge(*K.at("inverse_begun", t))
                    else:
                        pe.wait_ge(*K.at("inverse_grown", (NL - 1) * t + i - 1))
                    for u in range(4):
                        mm = pe.matmul(four(0)[:, u, :], corner[:, i % 2, u, :], T[:, u, :], start=True, stop=True)
                    mm.then_inc(*K.up("corner_product"))
                    pe.wait_ge(*K.at("product_copied", g))
                    for u in range(4):
                        mm = pe.matmul(four(1)[:, u, :], prod[:, u, :], TT[:, u, :], start=True, stop=True)
                    if i + 1 < NL:
                        for u in range(4):
                            mm = pe.matmul(four(2)[:, u, :], TT[:, u, :], prod[:, u, :], start=True, stop=True)
                    mm.then_inc(*K.up("growth_ready"))
                pe.wait_ge(*K.at("transposed_grown", NL * (t + 1) - 1))
                pe.wait_ge(*K.at("x_ready", t))
                for u in range(4):
                    mm = pe.matmul(four(3)[:, u, :], TT[:, u, :], x[:, u, :], start=True, stop=True)
                mm.then_inc(*K.up("ku_ready"))
                pe.wait_ge(*K.at("ku_copied", t))
                for d in range(2):
                    rhs = ab[:, d, :, 1, :]
                    pe.matmul(bank(4)[:, 256 * d:256 * d + 256], kp[:, d, :], rhs, start=True, stop=True)
                    pe.matmul(bank(5)[:, 0:256], v_tok, bd[:, d, :, 1, :], start=d == 0, stop=False)
                    mm = pe.matmul(bank(5)[:, 0:256], nu[:, d, :], rhs, start=False, stop=d == 1)
                mm.then_inc(*K.up("own_ready"))
                for d in range(2):
                    for c in range(2):
                        rows, at = slice(64 * c, 64 * c + 64), slice(d * P, (d + 1) * P)
                        pe.matmul(bank(c)[:, at], kp[rows, d, :], b_tok[rows, d, :], start=True, stop=True)
                        pe.matmul(bank(2 + c)[:, at], k_tok[rows, d, :], v_tok[rows, :], start=True, stop=False)
                        mm = pe.matmul(bank(2 + c)[:, at], b_tok[rows, d, :], nu[rows, d, :], start=False, stop=True)
                mm.then_inc(*K.up("steps_ready"))

        @block.vector
        def _(dve):
            for t in range(TILES):
                tok = slice(t * P, (t + 1) * P)
                dve.wait_ge(*K.at("scores_done", t))
                for e in range(2):
                    for src, dst in ((e, ab), (2 + e, bd)):
                        out = dst[:, :, e].rearrange("p d a t -> p d (a t)")
                        ins = dve.tensor_tensor(out, bank(src).rearrange("p (d n) -> p d n", d=2), K.order_masks,
                                                ALU.mult)
                K.link(dve, ins, "masked")
                for e in range(2):
                    own = lambda m: m.rearrange("p (d e) t -> p d e t", d=2)[:, :, e, :]
                    dve.tensor_tensor(own(T), bank(4 + e)[:, 0:256].rearrange("p (d t) -> p d t", d=2),
                                      K.first_masks[:, 0], ALU.mult)
                    ins = dve.tensor_tensor(own(TT), ab[:, :, e, 0, :], K.first_masks[:, 1], ALU.mult)
                K.link(dve, ins, "dve_step")
                dve.tensor_tensor(T, T, ident4, ALU.add)
                dve.tensor_tensor(TT, TT, ident4, ALU.add).then_inc(*K.up("inverse_begun"))
                dve.wait_ge(*K.at("bv_ready", t))
                dve.tensor_copy(x[:, :, 64:128], bank(6)[:, 0:256].rearrange("p (u n) -> p u n", u=4)
                                ).then_inc(*K.up("x_ready"))
                for i in range(NL):
                    dve.wait_ge(*K.at("growth_ready", NL * t + i))
                    dve.tensor_tensor(TT, TT, four(1), ALU.subtract).then_inc(*K.up("transposed_grown"))
                    if i + 1 < NL:
                        dve.tensor_tensor(T, T, four(2), ALU.subtract).then_inc(*K.up("inverse_grown"))
                dve.wait_ge(*K.at("ku_ready", t))
                ku = bank(3).rearrange("p (d e w n) -> p d e w n", d=2, e=2, w=2)
                parts = lambda m: m.rearrange("p d (e n) -> p d e n", e=2)
                for d in range(2):
                    dve.tensor_copy(parts(kp)[:, d], ku[:, d, :, 0, :])
                    ins = dve.tensor_scalar(parts(nu)[:, d], ku[:, d, :, 1, :], -1.0, None, ALU.mult)
                ins.then_inc(*K.up("ku_copied"))
                dve.wait_ge(*K.at("own_ready", t))
                for e in range(2):
                    rows = slice(64 * e, 64 * e + 64)
                    for d in range(2):
                        out = kr[rows, d, t, 1, :]
                        dve.tensor_tensor(out, out, bank(4)[rows, 256 * d + P * e:256 * d + P * e + P], ALU.subtract)
                    ins = dve.tensor_copy(y[rows, tok], bank(5)[rows, P * e:P * e + P])
                ins.then_inc(*K.up("own_copied"))
                dve.wait_ge(*K.at("steps_ready", t))
                at = [step[:, :, 2 * t + c, :] for c in range(2)]
                two = K.const("head_ones").rearrange("p (a b) -> p a b", a=1).to_broadcast([P, 2, P])
                for c in range(2):
                    for d in range(2):
                        dve.scalar_tensor_tensor(carry[:, d, 2 * t + c, :], bank(2 + c)[:, d * P:(d + 1) * P],
                                                 pc[:, d, 2 * t + c:2 * t + c + 1], K.const("head_ones"),
                                                 ALU.mult, ALU.mult)
                    ins = dve.tensor_tensor(at[c], bank(c)[:, 0:256].rearrange("p (d n) -> p d n", d=2), two, ALU.mult)
                ins.then_inc(*K.up("dve_step"))
                dve.wait_ge(*K.now("dve_step"))
                for c in range(2):
                    ins = dve.tensor_tensor(at[c], ident2, at[c], ALU.subtract)
                ins.then_inc(*K.up("steps_copied"))

        @block.scalar
        def _(act):
            for t in range(TILES):
                act.wait_ge(*K.at("tokens_turned", t))
                if t >= 1:
                    act.wait_ge(*K.at("steps_ready", t - 1))
                act.copy(b_tok[:, 0, :], bank(6)[:, 0:P])
                act.copy(b_tok[:, 1, :], bank(6)[:, P:2 * P])
                act.copy(k_tok[:, 0, :], bank(6)[:, 2 * P:3 * P])
                act.copy(k_tok[:, 1, :], bank(6)[:, 3 * P:4 * P])
                act.copy(x[:, :, 0:64], bank(7)[:, 0:256].rearrange("p (u n) -> p u n", u=4))
                act.copy(v_tok, bank(7)[:, 2 * P:3 * P]).then_inc(*K.up("tokens_copied"))
                for i in range(NL):
                    act.wait_ge(*K.at("corner_product", NL * t + i))
                    act.copy(prod, four(0)).then_inc(*K.up("product_copied"))

        @block.gpsimd
        def _(pool):
            for t in range(TILES):
                pool.wait_ge(*K.at("masked", t))
                for i in range(NL):
                    g = NL * t + i
                    if g >= 2:
                        pool.wait_ge(*K.at("corner_product", g - 2))
                    for d in range(2):
                        ins = pool.tensor_tensor(corner[:, i % 2, 2 * d:2 * d + 2, :], ab[:, d, :, 0, :],
                                                 level_mask(d, i), ALU.mult)
                    ins.then_inc(*K.up("corner_ready"))
    K.top = top


def rwkv_scan(K, kr, pc, step, carry, y, first_out):
    order = [list(range(NCH)), list(range(CTX // CH - 1, -1, -1)) + list(range(NCH - 1, CTX // CH - 1, -1))]
    with K.stage() as block:
        @block.tensor
        def _(pe):
            for j in range(1, NCH - 1):
                if j >= 2:
                    pe.wait_ge(*K.at("state_ready", 2 * (j - 2) + 1))
                for d in range(2):
                    pe.matmul(K.psum[:, 2 * (j % 2) + d, 0:P], step[:, d, order[d][j], :], carry[:, d, order[d][j - 1], :],
                              start=True, stop=True).then_inc(*K.up("state_moved"))
            pe.wait_ge(*K.at("state_ready", 2 * (NCH - 3) + 1))
            for c in range(first_out, NCH):
                at = K.psum[:, 4 + c // 8, (c % 8) * CH:(c % 8 + 1) * CH]
                before = [(d, order[d][order[d].index(c) - 1]) for d in range(2) if order[d].index(c) > 0]
                for n, (d, prior) in enumerate(before):
                    mm = pe.matmul(at, carry[:, d, prior, :], kr[:, d, c // 2, 1, (c % 2) * CH:(c % 2 + 1) * CH],
                                   start=n == 0, stop=n == len(before) - 1)
            mm.then_inc(*K.up("outputs_ready"))

        @block.vector
        def _(dve):
            for j in range(1, NCH - 1):
                for d in range(2):
                    c = order[d][j]
                    dve.wait_ge(*K.at("state_moved", 2 * (j - 1) + d))
                    dve.scalar_tensor_tensor(carry[:, d, c, :], K.psum[:, 2 * (j % 2) + d, 0:P], pc[:, d, c:c + 1],
                                             carry[:, d, c, :], ALU.mult, ALU.add).then_inc(*K.up("state_ready"))
            dve.wait_ge(*K.at("outputs_ready", 0))
            a = first_out * CH
            for lo, hi in ((a, 512), (512, T2)):
                out = y[:, lo:hi]
                dve.tensor_tensor(out, out, K.psum[:, 4:6, :].rearrange("p a b -> p (a b)")[:, lo:hi], ALU.add)


def rwkv_finish(K, layer, pair, y, v, bonus, gate, out, a):
    top = K.top
    n = T2 - a
    tok = slice(a, T2)
    centred, sq, std = K.alloc(n), K.alloc(n), K.alloc(n)
    col = lambda name: K.col(f"{name}{layer}")[:, pair:pair + 1]
    banks = lambda i: K.psum[:, 2 * i:2 * i + 2, :].rearrange("p a b -> p (a b)")[:, 0:n]
    cuts = [(lo, min(lo + 512, n)) for lo in range(0, n, 512)]
    with K.stage() as block:
        @block.tensor
        def _(pe):
            for lo, hi in cuts:
                mm = pe.matmul(banks(0)[:, lo:hi], K.const("head_ones"), y[:, a + lo:a + hi], start=True, stop=True)
            mm.then_inc(*K.up("mean_ready"))
            pe.wait_ge(*K.at("deviation_squared", 0))
            for lo, hi in cuts:
                mm = pe.matmul(banks(1)[:, lo:hi], K.const("head_ones"), sq[:, lo:hi], start=True, stop=True)
            mm.then_inc(*K.up("variance_ready"))

        @block.vector
        def _(dve):
            dve.wait_ge(*K.at("mean_ready", 0))
            dve.scalar_tensor_tensor(centred, banks(0), -1.0 / HD, y[:, tok], ALU.mult, ALU.add
                                     ).then_inc(*K.up("centred"))
            dve.wait_ge(*K.at("std_ready", 0))
            K.link(dve, dve.reciprocal(std, std), "dve_step")
            K.link(dve, dve.scalar_tensor_tensor(centred, centred, col("gn_g"), std, ALU.mult, ALU.mult), "dve_step")
            dve.wait_ge(*K.at("bonus_ready", 0))
            K.link(dve, dve.scalar_tensor_tensor(centred, centred, col("gn_b"), bonus[:, tok], ALU.add, ALU.add),
                   "dve_step")
            dve.tensor_tensor(out[:, tok], centred, gate, ALU.mult)

        @block.scalar
        def _(act):
            act.wait_ge(*K.at("centred", 0))
            act.activation(sq, centred, ACT.Square).then_inc(*K.up("deviation_squared"))
            act.wait_ge(*K.at("variance_ready", 0))
            act.activation(std, banks(1), ACT.Sqrt, scale=1.0 / HD, bias=K.const("eps_gn")).then_inc(*K.up("std_ready"))

        @block.gpsimd
        def _(pool):
            pool.tensor_tensor(bonus[:, tok], bonus[:, tok], v[:, tok], ALU.mult).then_inc(*K.up("bonus_ready"))
    K.top = top


def layer_norm(K, layer, x, n):
    top = K.top
    sq, mean, std = K.alloc(2, n), K.alloc(n), K.alloc(n)
    banks = lambda i: K.psum[:, 2 * i:2 * i + 2, :].rearrange("p a b -> p (a b)")[:, 0:n]
    cuts = [(lo, min(lo + 512, n)) for lo in range(0, n, 512)]
    g, b = K.col(f"ln_g{layer}"), K.col(f"ln_b{layer}")
    with K.stage() as block:
        @block.tensor
        def _(pe):
            for k in range(KT):
                for lo, hi in cuts:
                    mm = pe.matmul(banks(0)[:, lo:hi], K.const("ones"), x[:, k, lo:hi], start=k == 0, stop=k == KT - 1)
            mm.then_inc(*K.up("mean_ready"))
            for k in range(KT):
                pe.wait_ge(*K.at("square_ready", k))
                for lo, hi in cuts:
                    mm = pe.matmul(banks(1)[:, lo:hi], K.const("ones"), sq[:, k % 2, lo:hi], start=k == 0, stop=k == KT - 1)
                mm.then_inc(*K.up("square_summed"))

        @block.vector
        def _(dve):
            dve.wait_ge(*K.at("mean_ready", 0))
            K.link(dve, dve.tensor_scalar(mean, banks(0), -1.0 / D, None, ALU.mult), "dve_step")
            for k in range(KT):
                dve.tensor_tensor(x[:, k, :], x[:, k, :], mean, ALU.add).then_inc(*K.up("centred"))
            dve.wait_ge(*K.at("std_ready", 0))
            K.link(dve, dve.reciprocal(std, std), "dve_step")
            for k in range(KT):
                dve.scalar_tensor_tensor(x[:, k, :], x[:, k, :], g[:, k:k + 1], std, ALU.mult, ALU.mult
                                         ).then_inc(*K.up("scaled"))

        @block.scalar
        def _(act):
            for k in range(KT):
                act.wait_ge(*K.at("centred", k))
                if k >= 2:
                    act.wait_ge(*K.at("square_summed", k - 2))
                act.activation(sq[:, k % 2, :], x[:, k, :], ACT.Square).then_inc(*K.up("square_ready"))
            act.wait_ge(*K.at("square_summed", KT - 1))
            act.activation(std, banks(1), ACT.Sqrt, scale=1.0 / D, bias=K.const("eps_ln")).then_inc(*K.up("std_ready"))
            for k in range(KT):
                act.wait_ge(*K.at("scaled", k))
                act.activation(x[:, k, :], x[:, k, :], ACT.Identity, bias=b[:, k:k + 1])
    K.top = top


def gated_residual(x, mod, tile, a):
    def evacuate(K, eng, ps):
        x_new = x
        K.link(eng, eng.tensor_scalar(x_new, x_new, ALPHA, None, ALU.mult), "dve_step")
        for (lo, hi), which in (((0, CTX), 1), ((CTX, T2), 0)):
            if hi > a:
                ins = eng.scalar_tensor_tensor(x_new[:, lo - a:hi - a], ps[:, lo - a:hi - a],
                                               mod[:, 16 + tile, which:which + 1], x_new[:, lo - a:hi - a],
                                               ALU.mult, ALU.add)
        return ins
    return evacuate


def second_layer(K, layer, x, cond):
    top = K.top
    final = layer == 1
    a = CTX if final else 0
    n = T2 - a
    mod = K.alloc(24, 2)
    modulation(K, layer, cond, mod)
    conv, gates = K.alloc(10, T2), K.alloc(8, T2)
    q, nq = K.alloc(3, T2), K.alloc(2, T2)
    mark = K.top
    kg, nk, v_tok = K.alloc(T2), K.alloc(2, T2), K.alloc(TILES, 384)
    inner = K.top
    h = K.alloc(KT, T2)
    with K.stage() as block:
        @block.vector
        def _(dve):
            for k in range(KT):
                dve.tensor_scalar(h[:, k, LAT], x[:, k, LAT], mod[:, 8 + k, 0:1], mod[:, k, 0:1], ALU.mult, ALU.add)

        @block.gpsimd
        def _(pool):
            for k in range(KT):
                pool.tensor_scalar(h[:, k, 0:CTX], x[:, k, 0:CTX], mod[:, 8 + k, 1:2], mod[:, k, 1:2],
                                   ALU.mult, ALU.add)
    whole = [h[:, k, :] for k in range(KT)]
    asked = [h[:, k, a:T2] for k in range(KT)]
    taps = K.col(f"rwkv_conv{layer}")
    jobs = []

    def feature(src, m, engine, evacuate):
        i = len(jobs)
        jobs.append(Job(i // 2, P * (i % 2), P, 256, src, m, engine, evacuate))
    for i in range(10):
        feature(whole, T2, "dve", centred_evacuation(conv[:, i, :], taps[:, 3 * i:3 * i + 3]))
    for i in range(3):
        feature(asked, n, "act", act_to(gates[:, i, a:T2], ACT.Silu))
    for i in range(3):
        feature(asked, n, "dve", copy_to(q[:, i, a:T2]))
    feature(whole, T2, "dve", copy_to(kg))
    for i in range(3):
        feature(asked, n, "act", act_to(gates[:, 3 + i, a:T2], ACT.Silu))
    for i in range(2):
        feature(asked, n, "dve", copy_to(nq[:, i, a:T2]))
    for i in range(2):
        feature(whole, T2, "dve", copy_to(nk[:, i, :]))
    for i in range(2):
        feature(asked, n, "act", act_to(gates[:, 6 + i, a:T2], ACT.Silu))
    for t in range(TILES):
        jobs.append(Job(13, 0, 256, 256, whole, T2, "act" if t % 2 else "dve", copy_to(v_tok[:, t, 0:256]),
                        tokens=block_of(t)))
    for t in range(TILES):
        jobs.append(Job(14, 0, P, P, whole, T2, "act" if t % 2 else "dve", copy_to(v_tok[:, t, 256:384]),
                        tokens=block_of(t)))
    project(K, jobs, 15)

    K.top = inner
    cos, sin, turn = K.alloc(S), K.alloc(S), K.alloc(P)
    bias, mask = K.alloc(4, 16, 64), K.alloc(64)
    load(K, [(cos, K.dram["rope_cos"]), (sin, K.dram["rope_sin"]), (turn, K.dram["rope_turn"]),
             (bias.rearrange("p a b c -> p (a b c)"), K.dram["window_bias"][layer]), (mask, K.dram["window_mask"])])
    head_norm(K, [q[:, i, a:T2] for i in range(3)], n, K.col(f"gqa_q_norm{layer}"))
    head_norm(K, [kg], T2, K.col(f"gqa_k_norm{layer}"))
    rope(K, [q[:, i, :] for i in range(3)] + [kg], cos, sin, turn)
    with K.stage() as block:
        @block.vector
        def _(dve):
            every = mask.rearrange("p (a b) -> p a b", a=1).to_broadcast([P, 64, 64])
            rows = bias.rearrange("p a b c -> p (a b) c")
            dve.tensor_tensor(rows, rows, every, ALU.add)
    units = []
    for half in range(2):
        rows = slice(64 * half, 64 * half + 64)
        for t in range(TILES):
            tok = slice(t * P, (t + 1) * P)
            if t * P < a:
                continue
            in_ctx = (t + 1) * P <= CTX
            keys, blocks = slice(0, CTX if in_ctx else T2), range(CTX // P if in_ctx else TILES)
            for i in range(3):
                units.append(Unit(half, q[rows, i, tok], kg[rows, keys], [v_tok[:, b, 256:384] for b in blocks],
                                  q[rows, i, tok]))
            for i in range(2):
                window = None
                if not in_ctx:
                    r0 = 2 * (t - CTX // P)
                    window = bias[:, 2 * i + half, 7 - r0:15 - r0, :].rearrange("p a b -> p (a b)")
                units.append(Unit(half, nq[rows, i, tok], nk[rows, i, keys],
                                  [v_tok[:, b, P * i:P * i + P] for b in blocks], nq[rows, i, tok], bias=window))
    attention(K, units)

    with K.stage() as block:
        @block.vector
        def _(dve):
            for i in range(3):
                dve.tensor_tensor(q[:, i, a:T2], q[:, i, a:T2], gates[:, 3 + i, a:T2], ALU.mult)
            for i in range(2):
                dve.tensor_tensor(nq[:, i, a:T2], nq[:, i, a:T2], gates[:, 6 + i, a:T2], ALU.mult)

        @block.scalar
        def _(act):
            act.activation(conv[0:64, 9, :], conv[0:64, 9, :], ACT.Tanh)
    spare = gates[:, 3:8, :].rearrange("p a b -> p (a b)")
    step = spare[:, 0:2 * NCH * P].rearrange("p (d c n) -> p d c n", d=2, c=NCH)
    pc = spare[:, 2 * NCH * P:2 * NCH * P + 2 * NCH].rearrange("p (d c) -> p d c", d=2)
    K.top = mark
    K.reset = K.alloc(T2)
    K.order_masks, K.first_masks = K.alloc(2, 2 * P), K.alloc(2, 2, P)
    K.level_masks, lora = K.alloc(len(LEVELS), 2, P), K.alloc(RH * P)
    load(K, [(K.reset, K.dram["reset"]), (K.order_masks.rearrange("p a b -> p (a b)"), K.dram["order_masks"]),
             (K.first_masks.rearrange("p a b c -> p (a b c)"), K.dram["first_masks"]),
             (K.level_masks.rearrange("p a b c -> p (a b c)"), K.dram["level_masks"]), (lora, K.dram["lora"][layer])])
    kr, bk = K.alloc(2, TILES, 2, P), K.alloc(2, 2, T2)
    carry, bonus = K.alloc(2, NCH, P), K.alloc(T2)
    for pair in range(RH):
        r, k, v = conv[:, pair, :], conv[:, 3 + pair, :], conv[:, 6 + pair, :]
        y = k
        rwkv_prepare(K, layer, pair, r, k, conv[:, 9, :], lora, kr, bk, pc, bonus,
                     carry.rearrange("p a b c -> p (a b c)"))
        rwkv_chunks(K, kr, bk, pc, v, step, carry, y)
        rwkv_scan(K, kr, pc, step, carry, y, a // CH)
        rwkv_finish(K, layer, pair, y, v, bonus, gates[:, pair, a:T2], r, a)
    src = [conv[:, i, a:T2] for i in range(3)] + [q[:, i, a:T2] for i in range(3)] + [nq[:, i, a:T2] for i in range(2)]
    jobs = [Job(d // 2, P * (d % 2), P, 256, src, n, "dve", gated_residual(x[:, d, a:T2], mod, d, a)) for d in range(KT)]
    project(K, jobs, 4)
    K.top = inner
    layer_norm(K, layer, x[:, :, a:T2], n)
    K.top = top


def chunk_plan():
    full = [(k * P, P) for k in range(KT)]
    plan = []

    def add(names, layer, cols, rows=None):
        plan.append((names, layer, cols, rows or full))

    def both(a, b, n=P):
        return [(a, n), (b, n)]

    def ffn_chunks(which, layer):
        for f in range(FT):
            add([f"ffn{which}_w_gate", f"ffn{which}_w_up"], layer, [[(f * P, P)], [(f * P, P)]])
        for d in range(KT):
            for half in range(2):
                add([f"ffn{which}_w_down"], layer, [[(d * P, P)]],
                    [((half * (FT // 2) + f) * P, P) for f in range(FT // 2)])

    def span(name, layer, start, stop, step=256, rows=None):
        for c in range(start, stop, step):
            add([name], layer, [[(c, min(step, stop - c))]], rows)

    w = ML_H * ML_D
    ffn_chunks(1, 0)
    span("a_w_in", 0, 0, 2 * w, 192)
    span("a_w_in", 0, 3 * w, 4 * w, 192)
    span("a_w_in", 0, 2 * w, 3 * w, 192)
    span("a_w_in", 0, 4 * w + 8, 4 * w + 8 + 256)
    span("a_w_in", 0, 4 * w, 4 * w + 8)
    span("w_mem_kv", 0, 0, 512)
    span("a_w_out", 0, 0, D, P, [(96 * i, 96) for i in range(8)] + [(w + P * i, P) for i in range(2)])
    ffn_chunks(2, 0)
    span("w_kv", None, 0, 1536)
    ffn_chunks(1, 1)
    span("b_w_q", 0, 0, D)
    span("w_mem_kv", 1, 0, 512)
    span("b_w_out", 0, 0, D)
    ffn_chunks(2, 1)
    second_plan(add, span)
    return plan


def second_plan(add, span):
    tiles = lambda at, n: [[(at + P * i, P)] for i in range(n)]
    paired = lambda at: [[(at + HD * i, HD), (at + HD * (i + 3), HD)] for i in range(3)]
    mixed = [[(P * i, P)] for i in range(3)] + paired(384) + tiles(768, 2)
    for layer in range(2):
        span("w_mod_2", layer, 0, 3 * D)
        order = (tiles(0, 10) + tiles(1280, 3) + paired(1664) + tiles(2048, 1) + paired(2304)
                 + tiles(2688, 2) + tiles(2944, 2) + tiles(3456, 2))
        for i in range(0, len(order), 2):
            add(["w_in_2"], layer, [order[i] + order[i + 1]])
        add(["w_in_2"], layer, [[(3200, 256)]])
        add(["w_in_2"], layer, [[(2176, P)]])
        span("w_out_2", layer, 0, D, rows=mixed)


def chunk_width(chunk):
    names, layer, cols, rows = chunk
    return len(rows) * sum(n for part in cols for _, n in part)


def build(nc, dram, out, cols, n_cols, consts, n_consts):
    plan = [("weights", i, chunk_width(c)) for i, c in enumerate(chunk_plan())]
    with ExitStack() as ctx:
        K = Core(nc, ctx, dram, cols, consts, plan)
        K.cols_sb, K.consts_sb = K.alloc(n_cols), K.alloc(n_consts)
        x = K.alloc(KT, T2)
        x_T = x[:, :, LAT]
        cond = K.alloc(KT, 2)
        top = K.top
        mem_T = K.alloc(KT, M)
        load(K, [(K.cols_sb, dram["columns"]), (K.consts_sb, dram["constants"]),
                 (x_T, dram["x_T"]), (x[:, :, 0:CTX], dram["ctx_T"]),
                 (cond.rearrange("p a b -> p (a b)"), dram["conditions"]), (mem_T.rearrange("p a b -> p (a b)"), dram["mem_T"])])
        ffn(K, x_T, K.col("ffn1_norm0"))
        mlstm_layer(K, x_T, mem_T)
        k_T, v = K.alloc(6, S), K.alloc(3, S // P, 256)
        ffn(K, x_T, K.col("ffn2_norm0"))
        shared_keys(K, x_T, k_T, v)
        ffn(K, x_T, K.col("ffn1_norm1"))
        dilated_layer(K, x_T, mem_T, k_T, v)
        ffn(K, x_T, K.col("ffn2_norm1"))
        K.top = top
        with K.stage() as block:
            @block.scalar
            def _(act):
                act.activation(cond, cond, ACT.Silu)
        second_layer(K, 0, x, cond)
        second_layer(K, 1, x, cond)
        with K.stage() as block:
            @block.sync
            def _(sp):
                sp.dma_start(out, x_T).then_inc(*K.up("result_stored", 16))
                sp.wait_ge(*K.at("result_stored", 0, 16))


def host_columns(inputs):
    import numpy as np

    blocks = {}

    def per_feature(name, values):
        blocks[name] = values.reshape(-1, P).T

    for i in range(2):
        for name in ("ffn1_norm", "ffn2_norm", "mix_norm", "mem_norm"):
            per_feature(f"{name}{i}", inputs[name][i])
        for name in ("mem_q_norm", "mem_k_norm"):
            per_feature(f"{name}{i}", np.tile(inputs[name][i], 2))
    per_feature("kv_norm", inputs["kv_norm"])
    per_feature("b_q_norm", np.tile(inputs["b_q_norm"][0], 2))
    per_feature("kv_k_norm", np.tile(inputs["kv_k_norm"], 2))

    def rows96(a):
        full = np.zeros((P, a.shape[1]), a.dtype)
        full[0:96] = a
        return full
    for i in range(2):
        per_feature(f"b_mod{i}", inputs["b_mod_2"][i])
        blocks[f"rwkv_conv{i}"] = inputs["rwkv_conv_2"][i].reshape(3, 10, P).transpose(2, 1, 0).reshape(P, 30)
        per_feature(f"decay_w0{i}", inputs["decay_w0_2"][i])
        per_feature(f"iclr_a0{i}", inputs["iclr_a0_2"][i])
        for name in ("k_k", "k_a", "r_k", "gn_g", "gn_b"):
            per_feature(f"{name}{i}", inputs[f"rwkv_{name}_2"][i].reshape(-1))
        for name in ("gqa_q_norm", "gqa_k_norm"):
            per_feature(f"{name}{i}", np.tile(inputs[f"{name}_2"][i], 2))
        for name in ("ln_g", "ln_b"):
            per_feature(f"{name}{i}", inputs[f"{name}_2"][i])
    conv = inputs["a_conv"][0].reshape(4, 16, 96)
    blocks["a_conv"] = rows96(conv.transpose(2, 1, 0).reshape(96, 64))
    blocks["a_h_norm"] = rows96(inputs["a_h_norm"][0].reshape(8, 96).T)
    blocks["a_gate_bias"] = np.tile(inputs["a_gate_bias"], (P, 1))
    return blocks


def shape_constants():
    import numpy as np

    f = np.float32
    s, t = np.arange(P)[:, None], np.arange(P)[None, :]
    core = {
        "eps_rms": np.full((P, 1), RMS_EPS, f), "eps_ln": np.full((P, 1), LN_EPS, f),
        "eps_gn": np.full((P, 1), GN_EPS, f),
        "identity": np.eye(P, dtype=f), "ones": np.ones((P, P), f),
        "head_ones": (s // HD == t // HD).astype(f),
        "upto": (s <= t).astype(f),
        "causal_add": np.where(t <= s, 0, -1e30).astype(f),
    }
    return core


def dilated_tables():
    import math

    import numpy as np

    q = np.arange(P)[:, None]
    k2, k = np.arange(2 * P)[None, :], np.arange(P)[None, :]
    m0 = q + P - k2
    m1 = q - k
    m2 = q // 4 - k // 4
    ok2 = (m2 >= 0) & (q % 4 == k % 4)
    dist = np.concatenate([m0, 4 * m1, 16 * m2], 1)
    ok = np.concatenate([(m0 >= 0) & (m0 <= P), m1 >= 0, ok2], 1)
    dist = np.where(ok, dist, 0)
    d_f = np.maximum(dist, 1).astype(np.float32)
    large = 16 + (np.log(d_f / np.float32(16)) / np.float32(math.log(128)) * np.float32(16)).astype(np.int32)
    bucket = np.where(dist < 16, dist, np.minimum(large, 31))
    return bucket, np.where(ok, 0, -1e30).astype(np.float32)


def second_arrays(inputs):
    import numpy as np

    f = np.float32
    t = np.arange(S)
    inv_freq = f(10000.0) ** (-np.arange(16, dtype=f) / f(16))
    ang_r, ang_c = (t // 64).astype(f)[:, None] * inv_freq, (t % 64).astype(f)[:, None] * inv_freq
    ang = np.tile(np.concatenate([ang_r, ang_r, ang_c, ang_c], -1).T, (2, 1))
    turn = np.zeros((P, P), f)
    for m in range(P):
        turn[m + 16 if m % 32 < 16 else m - 16, m] = -1 if m % 32 < 16 else 1

    parity, c = np.arange(P)[:, None, None] // 64, np.arange(P)[:, None, None] % 64
    slot, kc = np.arange(16)[None, :, None], np.arange(64)[None, None, :]
    start = np.clip(c - 8, 0, 48)
    inside = (kc >= start) & (kc < start + 16)
    dr, dc = np.clip(slot - parity, 0, 14), np.where(inside, kc - c + 15, 0)
    window = inputs["na_rpb_2"][:, :, dr, dc].transpose(0, 2, 1, 3, 4)

    s, u = np.arange(P)[:, None], np.arange(P)[None, :]
    chunk = s // CH == u // CH
    before = [s < u, s > u]
    order = np.stack([np.stack([chunk & before[d], chunk & (before[d] | (s == u))]) for d in range(2)])
    pairs = np.stack([np.stack([(s // 2 == u // 2) & before[1 - d] for d in range(2)]),
                      np.stack([(s // 2 == u // 2) & before[d] for d in range(2)])])
    levels = np.stack([np.stack([(s // n == u // n) & (s // (n // 2) != u // (n // 2)) & before[d] for d in range(2)])
                       for n in LEVELS])
    flat = lambda m: np.ascontiguousarray(np.moveaxis(m, -2, 0).reshape(P, -1).astype(f))
    lora = np.concatenate([inputs["decay_w2_2"].reshape(2, 64, 384), inputs["iclr_a2_2"].reshape(2, 64, 384)], 1)
    return {
        "rope_cos": np.cos(ang).astype(f), "rope_sin": np.sin(ang).astype(f), "rope_turn": turn,
        "window_bias": np.ascontiguousarray(window.reshape(2, P, 4096)),
        "window_mask": np.where(inside[:, 0, :], 0, -1e30).astype(f),
        "reset": np.tile((np.arange(T2) % CH != 0).astype(f), (P, 1)),
        "order_masks": flat(order), "first_masks": -flat(pairs), "level_masks": flat(levels),
        "lora": np.ascontiguousarray(lora),
    }


def kernel(**inputs):
    import numpy as np
    import concourse.bacc as bacc
    from concourse.bass_utils import run_bass_kernel_spmd

    inputs = {name: np.asarray(a) for name, a in inputs.items()}
    plan = chunk_plan()
    weights = np.zeros((len(plan), P, CHUNK), np.float32)
    for i, (names, layer, cols, rows) in enumerate(plan):
        width = sum(n for part in cols for _, n in part)
        for k, row in enumerate(rows):
            to = 0
            for r, nr in row if isinstance(row, list) else [row]:
                at = k * width
                for name, part in zip(names, cols):
                    w = inputs[name] if layer is None else inputs[name][layer]
                    for c, n in part:
                        weights[i, to:to + nr, at:at + n] = w[r:r + nr, c:c + n]
                        at += n
                to += nr

    def joined(blocks):
        where, at = {}, 0
        for name, a in blocks.items():
            where[name] = (at, a.shape[1])
            at += a.shape[1]
        return where, np.ascontiguousarray(np.concatenate(list(blocks.values()), 1))

    def feature_major(a):
        n = a.shape[0]
        return np.ascontiguousarray(a.T.reshape(KT, P, n).transpose(1, 0, 2))

    cols_at, columns = joined(host_columns(inputs))
    consts_at, constants = joined(shape_constants())
    bucket, mask = dilated_tables()
    group_of = np.repeat(np.arange(3), [2 * P, P, P])
    bias = np.stack([inputs["rel_bias"][bucket, group_of[None, :] * 4 + h] for h in range(4)], 1)
    arrays = {
        "weights": weights, "columns": columns, "constants": constants,
        "x_T": feature_major(inputs["x"][0]), "mem_T": feature_major(inputs["mem"][0]).reshape(P, KT * M),
        "ctx_T": feature_major(inputs["ctx_2"][0]),
        "conditions": feature_major(np.stack([inputs["c_2"][0], inputs["c_ctx_2"]])).reshape(P, KT * 2),
        **second_arrays(inputs),
        "dilated_bias": np.ascontiguousarray(bias.reshape(P, 2048)), "dilated_mask": mask,
    }
    nc = bacc.Bacc("TRN2", target_bir_lowering=False, num_devices=1)
    dram = {n: nc.dram_tensor(n, a.shape, mybir.dt.float32, kind="ExternalInput").ap() for n, a in arrays.items()}
    out = nc.dram_tensor("out", (P, KT * S), mybir.dt.float32, kind="ExternalOutput").ap()
    build(nc, dram, out, cols_at, columns.shape[1], consts_at, constants.shape[1])
    r = run_bass_kernel_spmd(nc, [arrays], core_ids=[0])
    got = r.results[0]["out"].reshape(P, KT, S)
    return np.ascontiguousarray(got.transpose(2, 1, 0).reshape(1, S, D))
```

```python
from contextlib import ExitStack

import concourse.bass as bass
from concourse import mybir
from concourse.alu_op_type import AluOpType as ALU

F32 = mybir.dt.float32
F32R = mybir.dt.float32r
ACT = mybir.ActivationFunctionType
AX_X = mybir.AxisListType.X

P = 128
D = 1024
KT = D // P
S = 512
M = 256
CTX = 256
F = 2816
FT = F // P
HD = 64
SCALE = HD ** -0.5
RMS_EPS = 1e-6
LN_EPS = 1e-5
GN_EPS = 64e-5
ALPHA = 4 ** 0.25

ML_H, ML_D = 4, 192
RING = 2
PIECE = 1024
CHUNK = 2048
DOWN = FT // 2 * P
ARENA_AT = 16512
ARENA = 53200


class Core:

    def __init__(self, nc, ctx, dram, cols, consts, plan):
        self.nc, self.ctx, self.dram, self.plan = nc, ctx, dram, plan
        self.tensors = 0
        self.psum = ctx.enter_context(nc.psum_tensor("psum", [P, 8, 512], F32))
        self.top = 0
        self.sems, self.count, self.base = {}, {}, {}
        self.col_at, self.const_at = cols, consts
        self.used = 0
        self.issued = 0
        self.free_at = {}
        self.ring_at = self.top
        self.ring = self.alloc(RING, CHUNK)
        self.w_hi, self.w_lo = self.alloc_rounded(2, PIECE), self.alloc_rounded(2, PIECE)
        self.ring_end = self.top

    def alloc(self, *shape, dtype=F32):
        n = 1
        for size in shape:
            n *= size
        self.tensors += 1
        at = (self.top + 7) // 8 * 8
        self.top = at + n
        assert self.top <= ARENA, self.top
        return self.nc.alloc_sbuf_tensor_at(f"buffer_{self.tensors}", [P, *shape], dtype, offset=ARENA_AT + 4 * at)[:]

    def alloc_rounded(self, *shape):
        return self.alloc(*shape, dtype=F32R)

    def up(self, name, n=1):
        if name not in self.sems:
            self.sems[name] = self.ctx.enter_context(self.nc.semaphore(name))
            self.count[name] = 0
            self.base.setdefault(name, 0)
        self.count[name] += n
        return self.sems[name], n

    def at(self, name, i, step=1):
        if name not in self.sems:
            self.sems[name] = self.ctx.enter_context(self.nc.semaphore(name))
            self.count[name] = 0
            self.base[name] = 0
        assert i >= 0
        return self.sems[name], self.base.get(name, 0) + (i + 1) * step

    def now(self, name):
        return self.sems[name], self.count[name]

    def stage(self):
        self.base = dict(self.count)
        return self.nc.Block()

    def link(self, eng, ins, name):
        sem, n = self.up(name)
        ins.then_inc(sem, n)
        eng.wait_ge(sem, self.count[name])

    def const(self, name):
        a, n = self.const_at[name]
        return self.consts_sb[:, a:a + n]

    def col(self, name):
        a, n = self.col_at[name]
        return self.cols_sb[:, a:a + n]

    def take(self, n):
        first = self.used
        self.used += n
        return first

    def slot(self, c):
        return self.ring[:, c % RING, :]

    def landed(self, c):
        sem, n = self.up(f"chunk_landed_{c % RING}", 0)
        return sem, 16 * (c // RING + 1)

    def frees(self, c, name):
        self.free_at[c] = (self.sems[name], self.count[name])

    def stream(self, sp, ahead=RING):
        while self.issued < min(self.used + ahead, len(self.plan)):
            c = self.issued
            name, row, n = self.plan[c]
            if c - RING in self.free_at:
                sp.wait_ge(*self.free_at[c - RING])
            sp.dma_start(self.slot(c)[:, 0:n], self.dram[name][row, :, 0:n]).then_inc(
                *self.up(f"chunk_landed_{c % RING}", 16))
            self.issued += 1


class Split:

    def __init__(self, K, tiles, n):
        self.hi, self.lo = K.alloc_rounded(tiles, n), K.alloc_rounded(tiles, n)

    def pair(self, k, rows=P):
        return self.hi[0:rows, k, :], self.lo[0:rows, k, :]


def rms_norm(K, src, n, gain, dst):
    top = K.top
    sq, std, rstd, full = K.alloc(2, n), K.alloc(n), K.alloc(n), K.alloc(2, n)
    total = K.psum[:, 0, 0:n]
    with K.stage() as block:
        @block.scalar
        def _(act):
            for k in range(KT):
                if k >= 2:
                    act.wait_ge(*K.at("square_summed", k - 2))
                act.activation(sq[:, k % 2, :], src[:, k, :], ACT.Square).then_inc(*K.up("square_ready"))
            act.wait_ge(*K.at("square_summed", KT - 1))
            act.activation(std, total, ACT.Sqrt, scale=1.0 / D, bias=K.const("eps_rms")).then_inc(*K.up("std_ready"))
            for k in range(KT):
                act.wait_ge(*K.at("normed", k))
                act.copy(dst.hi[:, k, :], full[:, k % 2, :]).then_inc(*K.up("hi_ready"))

        @block.tensor
        def _(pe):
            for k in range(KT):
                pe.wait_ge(*K.at("square_ready", k))
                pe.matmul(total, K.const("ones"), sq[:, k % 2, :], start=k == 0,
                          stop=k == KT - 1).then_inc(*K.up("square_summed"))

        @block.vector
        def _(dve):
            dve.wait_ge(*K.at("std_ready", 0))
            K.link(dve, dve.reciprocal(rstd, std), "dve_step")
            for k in range(KT):
                if k >= 2:
                    dve.wait_ge(*K.at("lo_ready", k - 2))
                dve.scalar_tensor_tensor(full[:, k % 2, :], src[:, k, :], gain[:, k:k + 1], rstd,
                                         ALU.mult, ALU.mult).then_inc(*K.up("normed"))

        @block.gpsimd
        def _(pool):
            for k in range(KT):
                pool.wait_ge(*K.at("hi_ready", k))
                pool.tensor_tensor(dst.lo[:, k, :], full[:, k % 2, :], dst.hi[:, k, :].bitcast(F32),
                                   ALU.subtract).then_inc(*K.up("lo_ready"))
    K.top = top


def split_tiles(K, tiles, dst):
    with K.stage() as block:
        @block.scalar
        def _(act):
            for i, x in enumerate(tiles):
                rows = x.shape[0]
                act.copy(dst.hi[0:rows, i, :], x).then_inc(*K.up("hi_ready"))

        def lows(eng, first):
            for i in range(first, len(tiles), 2):
                rows = tiles[i].shape[0]
                eng.wait_ge(*K.at("hi_ready", i))
                eng.tensor_tensor(dst.lo[0:rows, i, :], tiles[i], dst.hi[0:rows, i, :].bitcast(F32), ALU.subtract)

        @block.vector
        def _(dve):
            lows(dve, 0)

        @block.gpsimd
        def _(pool):
            lows(pool, 1)


def ffn(K, x_T, gain, spare):
    top = K.top
    h = Split(K, KT, S)
    rms_norm(K, x_T, S, gain, h)
    hidden = Split(K, FT, S)
    gate, full = spare[:, 0:4, :], spare[:, 4:8, :]

    def gate_evacuation(f):
        def evacuate(K, eng, ps):
            if f >= 2:
                eng.wait_ge(*K.at("dve_evacuated", f - 2))
            b = 2 * (f % 2)
            return eng.activation(gate[:, b:b + 2, :], ps.rearrange("p (a b) -> p a b", a=2), ACT.Silu)
        return evacuate

    def hidden_evacuation(f):
        def evacuate(K, eng, ps):
            eng.wait_ge(*K.at("act_evacuated", f))
            if f >= 2:
                eng.wait_ge(*K.at("hidden_lo", f - 2))
            b = 2 * (f % 2)
            return eng.tensor_tensor(full[:, b:b + 2, :], gate[:, b:b + 2, :],
                                     ps.rearrange("p (a b) -> p a b", a=2), ALU.mult)
        return evacuate

    def split_hidden(f):
        b = 2 * (f % 2)
        halves = lambda x: x.rearrange("p (a b) -> p a b", a=2)

        def hi(act):
            act.wait_ge(*K.at("dve_evacuated", f))
            act.copy(halves(hidden.hi[:, f, :]), full[:, b:b + 2, :]).then_inc(*K.up("hidden_hi"))

        def lo(pool):
            pool.wait_ge(*K.at("hidden_hi", f))
            pool.tensor_tensor(halves(hidden.lo[:, f, :]), full[:, b:b + 2, :], halves(hidden.hi[:, f, :].bitcast(F32)),
                               ALU.subtract).then_inc(*K.up("hidden_lo"))
        return {"act": hi, "pool": lo}

    src = [h.pair(k) for k in range(KT)]
    jobs = []
    for f in range(FT):
        jobs.append(Job(f, 0, P, 256, src, S, "act", gate_evacuation(f)))
        jobs.append(Job(f, P, P, 256, src, S, "dve", hidden_evacuation(f)))
        jobs[-1].after = split_hidden(f)
    src = [hidden.pair(f) for f in range(FT)]
    for d in range(KT):
        jobs.append(Job(FT + 2 * d, 0, P, P, src, S, "dve", half_residual(x_T[:, d, :]), chunks=2))
        if d == 0:
            jobs[-1].needs = ("hidden_lo", FT - 1)
    project(K, jobs, FT + 2 * KT)
    K.top = top


def half_residual(x):
    def evacuate(K, eng, ps):
        return eng.scalar_tensor_tensor(x, ps, 0.5, x, ALU.mult, ALU.add)
    return evacuate


class Job:

    def __init__(self, chunk, c0, cn, width, src, n, engine, evacuate, tokens=None, chunks=1):
        self.chunk, self.c0, self.cn, self.width, self.chunks = chunk, c0, cn, width, chunks
        self.src, self.n, self.engine, self.evacuate, self.tokens = src, n, engine, evacuate, tokens
        self.after, self.needs = {}, None


def copy_to(out):
    def evacuate(K, eng, ps):
        if eng is K.nc.scalar:
            return eng.copy(out, ps)
        return eng.tensor_copy(out, ps)
    return evacuate


def act_to(out, func):
    def evacuate(K, eng, ps):
        return eng.activation(out, ps, func)
    return evacuate


def cut_pieces(jobs):
    pieces, of_job = [], []
    for j, job in enumerate(jobs):
        prior = jobs[j - 1] if j else None
        if prior and (prior.chunk, prior.c0, prior.cn) == (job.chunk, job.c0, job.cn):
            of_job.append(of_job[-1])
            continue
        mine = []
        per = len(job.src) // job.chunks
        most = min(per, PIECE // job.cn)
        parts = -(-per // most)
        for c in range(job.chunks):
            for i in range(parts):
                a, b = per * i // parts, per * (i + 1) // parts
                mine.append(len(pieces))
                pieces.append((job.chunk + c, a, b - a, c * per + a, job.c0, job.cn, job.width,
                               [x.shape[0] for x, _ in job.src[c * per + a:c * per + b]]))
        of_job.append(mine)
    return pieces, of_job


def project(K, jobs, n_chunks, ahead=RING):
    c0 = K.take(n_chunks)
    pieces, of_job = cut_pieces(jobs)
    order = {"act": [j for j, job in enumerate(jobs) if job.engine == "act"],
             "dve": [j for j, job in enumerate(jobs) if job.engine == "dve"]}
    last_user = {p: j for j, mine in enumerate(of_job) for p in mine}
    released, ended = {}, 0
    for p in range(len(pieces)):
        j = last_user[p]
        if of_job[j][-1] == p or jobs[j].tokens is not None:
            released[p] = ("product_ready", j)
        else:
            released[p] = ("piece_ended", ended)
            ended += 1

    def shape_of(p):
        _, _, tiles, _, _, cn, _, _ = pieces[p]
        return lambda x: x[:, p % 2, 0:tiles * cn].rearrange("p (k n) -> p k n", k=tiles)

    def raw(p):
        chunk, first, tiles, _, at, cn, width, _ = pieces[p]
        return K.slot(c0 + chunk)[:, first * width:(first + tiles) * width].rearrange(
            "p (k n) -> p k n", k=tiles)[:, :, at:at + cn]

    with K.stage() as block:
        @block.tensor
        def _(pe):
            for j, job in enumerate(jobs):
                if j >= 4:
                    e = jobs[j - 4].engine
                    pe.wait_ge(*K.at(f"{e}_evacuated", order[e].index(j - 4)))
                if job.needs:
                    pe.wait_ge(*K.at(*job.needs))
                ps = K.psum[:, 2 * (j % 4):2 * (j % 4) + 2, :].rearrange("p a b -> p (a b)")
                for p in of_job[j]:
                    _, _, tiles, k0, _, cn, _, rows_of = pieces[p]
                    pe.wait_ge(*K.at("piece_ready", p))
                    w_hi, w_lo = shape_of(p)(K.w_hi), shape_of(p)(K.w_lo)
                    for k in range(tiles):
                        rows = rows_of[k]
                        hi, lo = job.src[k0 + k]
                        for i, (w, x) in enumerate(((w_hi, hi), (w_hi, lo), (w_lo, hi))):
                            flags = dict(start=k0 + k == 0 and i == 0, stop=k0 + k == len(job.src) - 1 and i == 2)
                            if job.tokens is not None:
                                mm = pe.matmul(ps[0:P, 0:cn], job.tokens(x), w[0:rows, k, :], **flags)
                            else:
                                for a in range(0, job.n, 512):
                                    b = min(job.n, a + 512)
                                    mm = pe.matmul(ps[0:cn, a:b], w[0:rows, k, :], x[:, a:b], **flags)
                    if last_user[p] == j and released[p][0] == "piece_ended":
                        mm.then_inc(*K.up("piece_ended"))
                mm.then_inc(*K.up("product_ready"))

        def program(eng, name, split):
            done = 0
            for j, job in enumerate(jobs):
                after_it = of_job[min(j + 1, len(jobs) - 1)]
                until = max(of_job[j][-1] + 1, min(after_it[-1] + 1, of_job[j][-1] + 3))
                for p in range(done, until):
                    split(p)
                done = until
                if job.engine == name:
                    rows, n = (P, job.cn) if job.tokens is not None else (job.cn, job.n)
                    ps = K.psum[:, 2 * (j % 4):2 * (j % 4) + 2, :].rearrange("p a b -> p (a b)")[0:rows, 0:n]
                    eng.wait_ge(*K.at("product_ready", j))
                    job.evacuate(K, eng, ps).then_inc(*K.up(f"{name}_evacuated"))
                if name in job.after:
                    job.after[name](eng)

        @block.scalar
        def _(act):
            def round_hi(p):
                rows = max(pieces[p][7])
                act.wait_ge(*K.landed(c0 + pieces[p][0]))
                if p >= 2:
                    act.wait_ge(*K.at(*released[p - 2]))
                act.copy(shape_of(p)(K.w_hi), raw(p)).then_inc(*K.up("hi_ready"))
            program(act, "act", round_hi)

        @block.vector
        def _(dve):
            def subtract_lo(p):
                dve.wait_ge(*K.landed(c0 + pieces[p][0]))
                dve.wait_ge(*K.at("hi_ready", p))
                dve.tensor_tensor(shape_of(p)(K.w_lo), raw(p), shape_of(p)(K.w_hi).bitcast(F32),
                                  ALU.subtract).then_inc(*K.up("piece_ready"))
                K.frees(c0 + pieces[p][0], "piece_ready")
            program(dve, "dve", subtract_lo)

        @block.gpsimd
        def _(pool):
            for job in jobs:
                if "pool" in job.after:
                    job.after["pool"](pool)

        @block.sync
        def _(sp):
            K.stream(sp, ahead)


def project_few(K, jobs, n_chunks):
    c0 = K.take(n_chunks)
    with K.stage() as block:
        @block.tensor
        def _(pe):
            for j, job in enumerate(jobs):
                c = c0 + job.chunk
                if j == 0 or jobs[j - 1].chunk != job.chunk:
                    pe.wait_ge(*K.landed(c))
                if j >= 8:
                    pe.wait_ge(*K.at("dve_evacuated", j - 8))
                w = K.slot(c)[:, 0:len(job.src) * job.width].rearrange("p (k n) -> p k n", k=len(job.src))
                for k, s in enumerate(job.src):
                    mm = pe.matmul(K.psum[0:job.cn, j % 8, 0:job.n], w[:, k, job.c0:job.c0 + job.cn], s,
                                   start=k == 0, stop=k == len(job.src) - 1)
                mm.then_inc(*K.up("product_ready"))
                K.frees(c, "product_ready")

        @block.vector
        def _(dve):
            for j, job in enumerate(jobs):
                dve.wait_ge(*K.at("product_ready", j))
                job.evacuate(K, dve, K.psum[0:job.cn, j % 8, 0:job.n]).then_inc(*K.up("dve_evacuated"))

        @block.sync
        def _(sp):
            K.stream(sp)


def head_norm(K, tiles, n, gain, eps=RMS_EPS):
    top = K.top
    sq, std = K.alloc(2, 1024), K.alloc(2, 1024)
    with K.stage() as block:
        @block.scalar
        def _(act):
            for i, x in enumerate(tiles):
                if i >= 2:
                    act.wait_ge(*K.at("square_summed", i - 2))
                act.activation(sq[:, i % 2, 0:n], x, ACT.Square).then_inc(*K.up("square_ready"))
                act.wait_ge(*K.at("square_summed", i))
                if i >= 2:
                    act.wait_ge(*K.at("head_normed", i - 2))
                ps = K.psum[:, 2 * (i % 2):2 * (i % 2) + 2, :].rearrange("p a b -> p (a b)")
                act.activation(std[:, i % 2, 0:n], ps[:, 0:n], ACT.Sqrt, scale=1.0 / HD,
                               bias=K.const("eps_rms")).then_inc(*K.up("std_ready"))

        @block.tensor
        def _(pe):
            for i in range(len(tiles)):
                pe.wait_ge(*K.at("square_ready", i))
                if i >= 2:
                    pe.wait_ge(*K.at("std_ready", i - 2))
                ps = K.psum[:, 2 * (i % 2):2 * (i % 2) + 2, :].rearrange("p a b -> p (a b)")
                for a in range(0, n, 512):
                    b = min(n, a + 512)
                    mm = pe.matmul(ps[:, a:b], K.const("head_ones"), sq[:, i % 2, a:b], start=True, stop=True)
                mm.then_inc(*K.up("square_summed"))

        @block.vector
        def _(dve):
            for i, x in enumerate(tiles):
                dve.wait_ge(*K.at("std_ready", i))
                r = std[:, i % 2, 0:n]
                K.link(dve, dve.reciprocal(r, r), "dve_step")
                dve.scalar_tensor_tensor(x, x, gain, r, ALU.mult, ALU.mult).then_inc(*K.up("head_normed"))
    K.top = top


def block_of(t):
    return lambda x: x[:, t * P:(t + 1) * P]


def as_shape(x, like):
    if len(like.shape) == 2:
        return x
    return x.rearrange("p (a b) -> p a b", a=like.shape[1])


class Unit:

    def __init__(self, half, q, keys, values, out, bias=None, lse=None):
        self.half, self.q, self.keys, self.values = half, q, keys, values
        self.out, self.bias, self.lse = out, bias, lse
        self.n = P * len(values)


def attention(K, units):
    top = K.top
    width = max(u.n for u in units)
    probs, probs_T = K.alloc(2, width), K.alloc(2, width)
    scored, diagonal = K.alloc(2, width), K.alloc(2, P)
    peak, bound, total, inverse = (K.alloc(len(units)) for _ in range(4))

    def scores_ps(u):
        return K.psum[:, 2 * (u % 2):2 * (u % 2) + 2, :].rearrange("p a b -> p (a b)")
    turned_ps = K.psum[:, 4:6, :].rearrange("p a b -> p (a b)")
    with K.stage() as block:
        @block.tensor
        def _(pe):
            def scores(u):
                unit = units[u]
                n = unit.n
                rows = slice(64 * unit.half, 64 * unit.half + 64)
                if u >= 2:
                    pe.wait_ge(*K.at("probs_ready", u - 2))
                if n <= 512:
                    mm = pe.matmul(scores_ps(u)[:, 0:n], unit.q, unit.keys, start=True, stop=True)
                else:
                    for a in range(0, n, 512):
                        b = min(n, a + 512)
                        mm = pe.matmul(scores_ps(u)[:, a:b], unit.q, unit.keys[:, a:b], start=True, stop=True)
                mm.then_inc(*K.up("scores_ready"))

            def turn(u):
                pe.wait_ge(*K.at("diagonal_ready", u))
                if u >= 1:
                    pe.wait_ge(*K.at("turned_copied", u - 1))
                for b in range(len(units[u].values)):
                    mm = pe.matmul(turned_ps[:, b * P:(b + 1) * P], probs[:, u % 2, b * P:(b + 1) * P],
                                   diagonal[:, u % 2, :], start=True, stop=True)
                mm.then_inc(*K.up("turned_ready"))

            def output(u):
                unit = units[u]
                blocks = len(unit.values)
                pe.wait_ge(*K.at("turned_copied", u))
                if u >= 2:
                    pe.wait_ge(*K.at("output_copied", u - 2))
                for b in range(blocks):
                    mm = pe.matmul(K.psum[:, 6 + u % 2, 0:P], unit.values[b], probs_T[:, u % 2, b * P:(b + 1) * P],
                                   start=b == 0, stop=b == blocks - 1)
                mm.then_inc(*K.up("output_ready"))

            for u in range(-2, len(units) + 1):
                if u + 2 < len(units):
                    scores(u + 2)
                if 0 <= u < len(units):
                    turn(u)
                if u >= 1:
                    output(u - 1)

        @block.vector
        def _(dve):
            def find_peak(u):
                unit = units[u]
                n = unit.n
                dve.wait_ge(*K.at("scores_ready", u))
                source = scores_ps(u)[:, 0:n]
                factor = -SCALE
                if unit.bias is not None:
                    dve_in = source
                    source = scored[:, u % 2, 0:n]
                    if u >= 2:
                        dve.wait_ge(*K.at("probs_ready", u - 2))
                    free = n - unit.bias.shape[1]
                    if free:
                        dve.tensor_scalar(source[:, 0:free], dve_in[:, 0:free], SCALE, None, ALU.mult)
                    K.link(dve, dve.scalar_tensor_tensor(source[:, free:n], dve_in[:, free:n], SCALE, unit.bias,
                                                         ALU.mult, ALU.add), "dve_step")
                    factor = -1.0
                K.link(dve, dve.tensor_reduce(peak[:, u:u + 1], source, AX_X, ALU.max), "dve_step")
                dve.tensor_scalar(bound[:, u:u + 1], peak[:, u:u + 1], factor, None,
                                  ALU.mult).then_inc(*K.up("bound_ready"))

            def invert(u):
                dve.wait_ge(*K.at("probs_ready", u))
                if u >= 2:
                    dve.wait_ge(*K.at("turned_ready", u - 2))
                K.link(dve, dve.reciprocal(inverse[:, u:u + 1], total[:, u:u + 1]), "dve_step")
                dve.tensor_scalar(diagonal[:, u % 2, :], K.const("identity"), inverse[:, u:u + 1], None,
                                  ALU.mult).then_inc(*K.up("diagonal_ready"))

            def copy_out(u):
                unit = units[u]
                rows = slice(64 * unit.half, 64 * unit.half + 64)
                dve.wait_ge(*K.at("output_ready", u))
                dve.tensor_copy(unit.out, as_shape(K.psum[rows, 6 + u % 2, 0:P], unit.out)).then_inc(*K.up("output_copied"))

            for u in range(-2, len(units) + 2):
                if 0 <= u + 1 < len(units):
                    invert(u + 1)
                if u + 2 < len(units):
                    find_peak(u + 2)
                if u >= 2:
                    copy_out(u - 2)

        @block.scalar
        def _(act):
            def exponentials(u):
                unit = units[u]
                n = unit.n
                act.wait_ge(*K.at("bound_ready", u))
                if u >= 2:
                    act.wait_ge(*K.at("turned_ready", u - 2))
                source, scale = (scores_ps(u)[:, 0:n], SCALE) if unit.bias is None else (scored[:, u % 2, 0:n], 1.0)
                act.activation(probs[:, u % 2, 0:n], source, ACT.Exp, scale=scale, bias=bound[:, u:u + 1],
                               accum_out=total[:, u:u + 1]).then_inc(*K.up("probs_ready"))

            def turn(u):
                n = units[u].n
                act.wait_ge(*K.at("turned_ready", u))
                if u >= 2:
                    act.wait_ge(*K.at("output_ready", u - 2))
                act.copy(probs_T[:, u % 2, 0:n], turned_ps[:, 0:n]).then_inc(*K.up("turned_copied"))

            for u in range(-1, len(units)):
                if u + 1 < len(units):
                    exponentials(u + 1)
                if u >= 0:
                    turn(u)
    if units[0].lse is not None:
        logs = K.alloc(len(units))
        with K.stage() as block:
            @block.scalar
            def _(act):
                act.activation(logs[:, :], total[:, :], ACT.Ln).then_inc(*K.up("log_ready"))

            @block.vector
            def _(dve):
                dve.wait_ge(*K.at("log_ready", 0))
                dve.tensor_tensor(units[0].lse, logs[:, :], bound[:, :], ALU.subtract)
    K.top = top


def memory_attention(K, layer, q_mem):
    top = K.top
    mem_T = K.alloc(KT, M)
    load(K, [(mem_T.rearrange("p a b -> p (a b)"), K.dram["mem_T"])])
    mem_n = Split(K, KT, M)
    rms_norm(K, mem_T, M, K.col(f"mem_norm{layer}"), mem_n)
    k_T, v = K.alloc(2, M), K.alloc(2, 256)
    src = [mem_n.pair(k) for k in range(KT)]
    jobs = [Job(0, P * i, P, 256, src, M, "act" if i else "dve", copy_to(k_T[:, i, :])) for i in range(2)]
    jobs += [Job(1, 0, 256, 256, src, M, "act" if t else "dve", copy_to(v[:, t, :]), tokens=block_of(t))
             for t in range(2)]
    project(K, jobs, 2)
    head_norm(K, [k_T[:, i, :] for i in range(2)], M, K.col(f"mem_k_norm{layer}"))
    head_norm(K, q_mem, S, K.col(f"mem_q_norm{layer}"))
    units = []
    for t in range(S // P):
        for pair in range(2):
            for half in range(2):
                rows = slice(64 * half, 64 * half + 64)
                q = q_mem[pair][rows, t * P:(t + 1) * P]
                units.append(Unit(half, q, k_T[rows, pair, :],
                                  [v[:, b, pair * P:(pair + 1) * P] for b in range(2)], q))
    attention(K, units)
    K.top = top


def conv_evacuation(out, taps):
    def evacuate(K, eng, ps):
        n = ps.shape[1]
        K.link(eng, eng.tensor_scalar(out, ps, taps[:, 3:4], None, ALU.mult), "dve_step")
        for shift in (1, 2, 3):
            ins = eng.scalar_tensor_tensor(out[:, shift:n], ps[:, 0:n - shift], taps[:, 3 - shift:4 - shift],
                                           out[:, shift:n], ALU.mult, ALU.add)
            if shift < 3:
                K.link(eng, ins, "dve_step")
        return ins
    return evacuate


def add_to(out, row):
    def evacuate(K, eng, ps):
        return eng.tensor_tensor(out, ps, row, ALU.add)
    return evacuate


def residual(x, factor=None):
    def evacuate(K, eng, ps):
        return eng.tensor_tensor(x, ps, x, ALU.add)
    return evacuate


def values_evacuation(v1, t, at):
    def evacuate(K, eng, ps):
        copy = eng.copy if eng is K.nc.scalar else eng.tensor_copy
        while_at = at
        while while_at < at + 256:
            hd, c = while_at // ML_D, while_at % ML_D
            n = min(ML_D - c, at + 256 - while_at)
            ins = copy(v1[:, t, hd, c:c + n], ps[:, while_at - at:while_at - at + n])
            while_at += n
        return ins
    return evacuate


def mlstm_gates(K, gates):
    H, N = ML_H, (S // P) * ML_H
    tiny = lambda: K.alloc(S // P, H)
    b, c, tot, cmax, upto, m0, m1, u, neg_u, inter, wgt, decay, floor, tmp = (tiny() for _ in range(14))
    flat = lambda x: x.rearrange("p a b -> p (a b)")
    masked = K.alloc(N, P)
    top = K.top
    size, soft, logf = tiny(), tiny(), tiny()
    f = gates[:, :, H:2 * H]
    with K.stage() as block:
        @block.vector
        def _(dve):
            dve.scalar_tensor_tensor(size, f, -1.0, f, ALU.mult, ALU.max).then_inc(*K.up("size_ready"))
            dve.wait_ge(*K.at("softplus_ready", 1))
            K.link(dve, dve.tensor_scalar(logf, f, 0.0, None, ALU.min), "dve_step")
            dve.tensor_tensor(logf, logf, soft, ALU.subtract).then_inc(*K.up("logf_ready"))
            dve.wait_ge(*K.at("sums_ready", 0))
            dve.tensor_copy(flat(b), K.psum[:, 0, 0:N])
            K.link(dve, dve.tensor_copy(flat(tot), K.psum[:, 1, 0:N]), "dve_step")
            dve.tensor_tensor(c, gates[:, :, 0:H], b, ALU.subtract).then_inc(*K.up("c_ready"))
            for q in range(4):
                dve.wait_ge(*K.at("c_spread", q))
                rows = K.psum[:, 2 + q, :].rearrange("p (a b) -> p a b", a=4)
                mask = K.const("causal_add").rearrange("p (a b) -> p a b", a=1).to_broadcast([P, 4, P])
                dve.tensor_reduce(cmax[:, q, :], rows, AX_X, ALU.max)
                K.link(dve, dve.tensor_tensor(masked[:, 4 * q:4 * q + 4, :], rows, mask, ALU.add), "dve_step")
                dve.tensor_reduce(upto[:, q, :], masked[:, 4 * q:4 * q + 4, :], AX_X, ALU.max)
            K.link(dve, dve.memset(m0[:, 0, :], 0.0), "dve_step")
            for q in range(S // P):
                K.link(dve, dve.tensor_tensor(m1[:, q, :], m0[:, q, :], cmax[:, q, :], ALU.max), "dve_step")
                if q + 1 < S // P:
                    K.link(dve, dve.tensor_tensor(m0[:, q + 1, :], m1[:, q, :], tot[:, q, :], ALU.add), "dve_step")
            K.link(dve, dve.tensor_tensor(u, m0, upto, ALU.max), "dve_step")
            dve.tensor_scalar(neg_u, u, -1.0, None, ALU.mult)
            dve.tensor_tensor(inter, m0, u, ALU.subtract)
            dve.tensor_tensor(wgt, c, m1, ALU.subtract)
            dve.tensor_tensor(decay, m0, m1, ALU.subtract)
            dve.tensor_tensor(floor, b, u, ALU.add).then_inc(*K.up("exponents_ready"))

        @block.scalar
        def _(act):
            act.wait_ge(*K.at("size_ready", 0))
            act.activation(soft, size, ACT.Exp, scale=-1.0).then_inc(*K.up("softplus_ready"))
            act.wait_ge(*K.at("softplus_ready", 0))
            act.activation(soft, soft, ACT.Ln, bias=1.0).then_inc(*K.up("softplus_ready"))
            act.wait_ge(*K.at("exponents_ready", 0))
            for x in (inter, wgt, decay):
                act.activation(x, x, ACT.Exp)
            act.activation(floor, floor, ACT.Exp, scale=-1.0)
            for j in range(N):
                act.activation(masked[:, j, :], masked[:, j, :], ACT.Exp, bias=flat(neg_u)[:, j:j + 1])

        @block.tensor
        def _(pe):
            pe.wait_ge(*K.at("logf_ready", 0))
            pe.matmul(K.psum[:, 0, 0:N], K.const("upto"), flat(logf), start=True, stop=True)
            pe.matmul(K.psum[:, 1, 0:N], K.const("ones"), flat(logf), start=True, stop=True
                      ).then_inc(*K.up("sums_ready"))
            pe.wait_ge(*K.at("c_ready", 0))
            for j in range(N):
                mm = pe.matmul(K.psum[:, 2 + j // 4, (j % 4) * P:(j % 4 + 1) * P],
                               flat(c)[:, j:j + 1].to_broadcast([P, P]), K.const("identity"), start=True, stop=True)
                if j % 4 == 3:
                    mm.then_inc(*K.up("c_spread"))
    K.top = top
    return masked, inter, wgt, decay, floor


def mlstm_cell(K, q_T, k_T, v1, o_T, gates, h_gain, h_aT):
    top = K.top
    H, C = ML_H, S // P
    weight, inter, wgt, decay, floor = mlstm_gates(K, gates)
    k_tok = K.alloc(2, H, 2, 96)
    memory = K.alloc(H, 2, 193)
    w, w_T = K.alloc(2, H, P), K.alloc(2, H, P)
    num = K.alloc(H, 193)
    square = K.alloc(192)
    den, ss = K.alloc(H), K.alloc(2, H)
    h = K.alloc(2, H, 192)
    bank = lambda i: K.psum[:, i, :]
    s_ps = bank(0).rearrange("p (h t) -> p h t", h=H)
    wt_ps = bank(1).rearrange("p (h t) -> p h t", h=H)
    local_ps = lambda hd: K.psum[:, 2 + hd // 2, (hd % 2) * 193:(hd % 2) * 193 + 193]
    carried_ps = lambda hd: K.psum[:, 4 + hd // 2, (hd % 2) * 193:(hd % 2) * 193 + 193]
    update_ps = lambda hd: K.psum[0:96, 6 + hd % 2, 0:386].rearrange("p (a b) -> p a b", a=2)
    pair_ps = lambda base, g: K.psum[:, base + g, 0:386].rearrange("p (a b) -> p a b", a=2)
    with K.stage() as block:
        @block.tensor
        def _(pe):
            for c in range(C):
                tok = slice(c * P, (c + 1) * P)
                if c >= 1:
                    pe.wait_ge(*K.at("h_gated", c - 1))
                for hd in range(H):
                    for part in range(2):
                        mm = pe.matmul(s_ps[:, hd, :], q_T[0:96, 2 * hd + part, tok], k_T[0:96, 2 * hd + part, tok],
                                       start=part == 0, stop=part == 1)
                mm.then_inc(*K.up("qk_ready"))
                for hd in range(H):
                    if c >= 1:
                        pe.wait_ge(*K.at("memory_updated", 4 * c - 1))
                    for part in range(2):
                        mm = pe.transpose(K.psum[:, 6 + hd // 2, (2 * (hd % 2) + part) * 96:(2 * (hd % 2) + part) * 96 + 96],
                                          k_T[0:96, 2 * hd + part, tok], K.const("identity")[0:96, 0:96])
                mm.then_inc(*K.up("k_turned"))
                pe.wait_ge(*K.at("w_ready", c))
                for hd in range(H):
                    mm = pe.transpose(wt_ps[:, hd, :], w[:, c % 2, hd, :], K.const("identity"))
                mm.then_inc(*K.up("w_turned"))
                if c >= 1:
                    pe.wait_ge(*K.at("memory_updated", 4 * c - 1))
                else:
                    pe.wait_ge(*K.at("memory_cleared", 0))
                for hd in range(H):
                    for part in range(2):
                        mm = pe.matmul(carried_ps(hd), q_T[0:96, 2 * hd + part, tok], memory[0:96, hd, part, :],
                                       start=part == 0, stop=part == 1)
                mm.then_inc(*K.up("carried_ready"))
                pe.wait_ge(*K.at("w_T_ready", c))
                for hd in range(H):
                    mm = pe.matmul(local_ps(hd), w_T[:, c % 2, hd, :], v1[:, c, hd, :], start=True, stop=True)
                mm.then_inc(*K.up("local_ready"))
                pe.wait_ge(*K.at("k_copied", c))
                for hd in range(H):
                    if hd >= 2:
                        pe.wait_ge(*K.at("memory_updated", 4 * c + hd - 2))
                    for part in range(2):
                        mm = pe.matmul(update_ps(hd)[:, part, :], k_tok[:, c % 2, hd, part, :], v1[:, c, hd, :],
                                       start=True, stop=True)
                    mm.then_inc(*K.up("update_ready"))
                pe.wait_ge(*K.at("h_ready", c))
                for hd in range(H):
                    for part in range(2):
                        mm = pe.transpose(K.psum[0:96, hd // 2, (2 * (hd % 2) + part) * P:(2 * (hd % 2) + part) * P + P],
                                          h[:, c % 2, hd, part * 96:(part + 1) * 96], K.const("identity"))
                mm.then_inc(*K.up("h_turned"))

        @block.vector
        def _(dve):
            dve.memset(memory[:, :, :, :], 0.0).then_inc(*K.up("memory_cleared"))
            dve.wait_ge(*K.at("memory_cleared", 0))
            for c in range(C):
                tok = slice(c * P, (c + 1) * P)
                dve.wait_ge(*K.at("qk_ready", c))
                dve.scalar_tensor_tensor(w[:, c % 2, :, :], s_ps, ML_D ** -0.5, weight[:, 4 * c:4 * c + 4, :],
                                         ALU.mult, ALU.mult).then_inc(*K.up("w_ready"))
                dve.wait_ge(*K.at("k_turned", c))
                for hd in range(H):
                    out = k_tok[:, c % 2, hd, :, :].rearrange("p a b -> p (a b)")
                    ins = dve.tensor_scalar(out, K.psum[:, 6 + hd // 2, (hd % 2) * 192:(hd % 2) * 192 + 192],
                                            wgt[:, c, hd:hd + 1], ML_D ** -0.5, ALU.mult, ALU.mult)
                ins.then_inc(*K.up("k_copied"))
                dve.wait_ge(*K.at("local_ready", c))
                dve.wait_ge(*K.at("carried_scaled", c))
                for g in range(2):
                    ins = dve.tensor_tensor(num[:, 2 * g:2 * g + 2, :], num[:, 2 * g:2 * g + 2, :], pair_ps(2, g), ALU.add)
                K.link(dve, ins, "dve_step")
                last = num[:, :, 192]
                K.link(dve, dve.scalar_tensor_tensor(den, last, -1.0, last, ALU.mult, ALU.max), "dve_step")
                K.link(dve, dve.tensor_tensor(den, den, floor[:, c, :], ALU.max), "dve_step")
                K.link(dve, dve.reciprocal(den, den), "dve_step")
                for hd in range(H):
                    ins = dve.tensor_scalar(h[:, c % 2, hd, :], num[:, hd, 0:192], den[:, hd:hd + 1], None, ALU.mult)
                ins.then_inc(*K.up("h_raw"))
                for hd in range(H):
                    dve.wait_ge(*K.at("update_ready", 4 * c + hd))
                    dve.scalar_tensor_tensor(memory[0:96, hd, :, :], memory[0:96, hd, :, :], decay[0:96, c, hd:hd + 1],
                                             update_ps(hd), ALU.mult, ALU.add).then_inc(*K.up("memory_updated"))
                dve.wait_ge(*K.at("h_deviation", c))
                K.link(dve, dve.reciprocal(ss[:, 1, :], ss[:, 1, :]), "dve_step")
                for hd in range(H):
                    ins = dve.tensor_scalar(h[:, c % 2, hd, :], h[:, c % 2, hd, :], ss[:, 1, hd:hd + 1], None, ALU.mult)
                ins.then_inc(*K.up("h_ready"))
                dve.wait_ge(*K.at("h_turned", c))
                for j in range(8):
                    ins = dve.scalar_tensor_tensor(h_aT[0:96, j, tok], K.psum[0:96, j // 4, (j % 4) * P:(j % 4 + 1) * P],
                                                   h_gain[0:96, j:j + 1], o_T[0:96, j, tok], ALU.mult, ALU.mult)
                ins.then_inc(*K.up("h_gated"))

        @block.scalar
        def _(act):
            for c in range(C):
                act.wait_ge(*K.at("w_turned", c))
                act.copy(w_T[:, c % 2, :, :], wt_ps).then_inc(*K.up("w_T_ready"))
                act.wait_ge(*K.at("carried_ready", c))
                if c >= 1:
                    act.wait_ge(*K.at("h_raw", c - 1))
                for hd in range(H):
                    ins = act.mul(num[:, hd, :], carried_ps(hd), inter[:, c, hd:hd + 1])
                ins.then_inc(*K.up("carried_scaled"))
                act.wait_ge(*K.at("h_raw", c))
                if c >= 1:
                    act.wait_ge(*K.at("h_ready", c - 1))
                for hd in range(H):
                    ins = act.activation(square, h[:, c % 2, hd, :], ACT.Square, accum_out=ss[:, 0, hd:hd + 1])
                    ins.then_inc(*K.up("h_squares"))
                    act.wait_ge(*K.at("h_squares", 4 * c + hd))
                act.activation(ss[:, 1, :], ss[:, 0, :], ACT.Sqrt, scale=1.0 / ML_D,
                               bias=K.const("eps_rms")).then_inc(*K.up("h_deviation"))
    K.top = top


def mlstm_layer(K, x_T):
    top = K.top
    qk_T, o_T = K.alloc(16, S), K.alloc(8, S)
    v1 = K.alloc(S // P, ML_H, 193)
    q_mem = K.alloc(2, S)
    gates = K.alloc(S // P, 2 * ML_H)
    h_aT = K.alloc(8, S)
    inner = K.top
    h = Split(K, KT, S)
    rms_norm(K, x_T, S, K.col("mix_norm0"), h)
    src = [h.pair(k) for k in range(KT)]
    taps = K.col("a_conv")
    jobs = []
    for j in range(16):
        jobs.append(Job(j // 2, 96 * (j % 2), 96, 192, src, S, "dve",
                        conv_evacuation(qk_T[0:96, j, :], taps[0:96, 4 * j:4 * j + 4])))
    for j in range(8):
        jobs.append(Job(8 + j // 2, 96 * (j % 2), 96, 192, src, S, "act", act_to(o_T[0:96, j, :], ACT.Sigmoid)))
    for i in range(3):
        for t in range(S // P):
            jobs.append(Job(12 + i, 0, 256, 256, src, S, "act" if t % 2 else "dve",
                            values_evacuation(v1, t, 256 * i), tokens=block_of(t)))
    for i in range(2):
        jobs.append(Job(15, P * i, P, 256, src, S, "act", copy_to(q_mem[:, i, :])))
    for t in range(S // P):
        jobs.append(Job(16, 0, 8, 8, src, S, "dve", add_to(gates[:, t, :], K.col("a_gate_bias")),
                        tokens=block_of(t)))
    project(K, jobs, 17)
    K.top = inner
    with K.stage() as block:
        @block.scalar
        def _(act):
            for half in range(2):
                x = qk_T[0:96, 8 * half:8 * half + 8, :]
                act.activation(x, x, ACT.Silu)

        @block.vector
        def _(dve):
            dve.memset(v1[:, :, :, 192:193], 1.0)
    mlstm_cell(K, qk_T[:, 0:8, :], qk_T[:, 8:16, :], v1, o_T, gates, K.col("a_h_norm"), h_aT)
    memory_attention(K, 0, [q_mem[:, i, :] for i in range(2)])
    mixed = Split(K, 10, S)
    split_tiles(K, [h_aT[0:96, j, :] for j in range(8)] + [q_mem[:, i, :] for i in range(2)], mixed)
    src = [mixed.pair(j, 96 if j < 8 else P) for j in range(10)]
    jobs = [Job(d, 0, P, P, src, S, "dve", residual(x_T[:, d, :])) for d in range(KT)]
    project(K, jobs, 8)
    K.top = top


def strided_tokens(group, t):
    if group == 0:
        return block_of(t)
    return lambda x: x[:, t:S:4]


def shared_keys(K, x_T, k_T, v):
    top = K.top
    h = Split(K, KT, S)
    rms_norm(K, x_T, S, K.col("kv_norm"), h)
    src = [h.pair(k) for k in range(KT)]
    jobs = [Job(i // 2, P * (i % 2), P, 256, src, S, "act" if i % 2 else "dve", copy_to(k_T[:, i, :])) for i in range(6)]
    for g in range(3):
        for t in range(S // P):
            jobs.append(Job(3 + g, 0, 256, 256, src, S, "act" if t % 2 else "dve", copy_to(v[:, g, t, :]),
                            tokens=strided_tokens(g, t)))
    project(K, jobs, 6)
    head_norm(K, [k_T[:, i, :] for i in range(6)], S, K.col("kv_k_norm"))
    K.top = top


def load(K, pairs):
    with K.stage() as block:
        @block.sync
        def _(sp):
            for dst, src in pairs:
                sp.dma_start(dst, src).then_inc(*K.up("array_landed", 16))
            sp.wait_ge(*K.at("array_landed", len(pairs) - 1, 16))


def merge_groups(K, lse, out_T):
    top = K.top
    spread = K.alloc(3, 2, S)
    peak, total = K.alloc(2, S), K.alloc(2, S)
    wide = K.alloc(48, 64)
    with K.stage() as block:
        @block.tensor
        def _(pe):
            pe.wait_ge(*K.at("lse_widened", 0))
            for i in range(24):
                g, pair, t = i // 8, i // 4 % 2, i % 4
                c = (g * 4 + t) * 4 + 2 * pair
                two = wide[:, c:c + 2, :].rearrange("p a b -> p (a b)")
                mm = pe.matmul(K.psum[:, i // 4, t * P:(t + 1) * P], two, K.const("identity"), start=True, stop=True)
                if t == 3:
                    mm.then_inc(*K.up("lse_spread"))

        @block.vector
        def _(dve):
            dve.tensor_copy(wide, lse.rearrange("p (a b) -> p a b", b=1).to_broadcast([P, 48, 64])
                            ).then_inc(*K.up("lse_widened"))
            for i in range(24):
                g, pair, t = i // 8, i // 4 % 2, i % 4
                if t == 0:
                    dve.wait_ge(*K.at("lse_spread", i // 4))
                out = strided_tokens(g, t)(spread[:, g, pair, :])
                ins = dve.tensor_copy(out, as_shape(K.psum[:, i // 4, t * P:(t + 1) * P], out))
            K.link(dve, ins, "dve_step")
            K.link(dve, dve.tensor_tensor(peak, spread[:, 0], spread[:, 1], ALU.max), "dve_step")
            K.link(dve, dve.tensor_tensor(peak, peak, spread[:, 2], ALU.max), "dve_step")
            for g in range(3):
                dve.tensor_tensor(spread[:, g], spread[:, g], peak, ALU.subtract).then_inc(*K.up("lse_shifted"))
            for g in range(3):
                dve.wait_ge(*K.at("weight_ready", g))
            K.link(dve, dve.tensor_tensor(total, spread[:, 0], spread[:, 1], ALU.add), "dve_step")
            K.link(dve, dve.tensor_tensor(total, total, spread[:, 2], ALU.add), "dve_step")
            K.link(dve, dve.reciprocal(total, total), "dve_step")
            for g in range(3):
                K.link(dve, dve.tensor_tensor(spread[:, g], spread[:, g], total, ALU.mult), "dve_step")
                out = out_T[:, 2 * g:2 * g + 2, :]
                dve.tensor_tensor(out, out, spread[:, g], ALU.mult)

        @block.scalar
        def _(act):
            for g in range(3):
                act.wait_ge(*K.at("lse_shifted", g))
                act.activation(spread[:, g], spread[:, g], ACT.Exp).then_inc(*K.up("weight_ready"))
    K.top = top


def dilated_layer(K, x_T, k_T, v):
    top = K.top
    bias = K.alloc(4, 512)
    mask = K.alloc(512)
    load(K, [(bias.rearrange("p a b -> p (a b)"), K.dram["dilated_bias"]), (mask, K.dram["dilated_mask"])])
    q_T = K.alloc(KT, S)
    inner = K.top
    h = Split(K, KT, S)
    rms_norm(K, x_T, S, K.col("mix_norm1"), h)
    src = [h.pair(k) for k in range(KT)]
    jobs = [Job(i // 2, P * (i % 2), P, 256, src, S, "act" if i % 2 else "dve", copy_to(q_T[:, i, :]))
            for i in range(KT)]
    project(K, jobs, 4)
    K.top = inner
    head_norm(K, [q_T[:, i, :] for i in range(6)], S, K.col("b_q_norm"))
    with K.stage() as block:
        @block.vector
        def _(dve):
            every = mask.rearrange("p (a b) -> p a b", a=1).to_broadcast([P, 4, 512])
            dve.tensor_tensor(bias, bias, every, ALU.add)
    lse = K.alloc(48)
    units = []
    for g in range(3):
        for t in range(S // P):
            for head in range(4):
                pair, half = 2 * g + head // 2, head % 2
                rows = slice(64 * half, 64 * half + 64)
                own = strided_tokens(g, t)
                q = own(q_T[rows, pair, :])
                features = slice(P * (head // 2), P * (head // 2) + P)
                if g == 0 and t > 0:
                    keys, blocks, where = k_T[rows, pair, (t - 1) * P:(t + 1) * P], (t - 1, t), slice(0, 256)
                else:
                    keys, blocks = own(k_T[rows, pair, :]), (t,)
                    where = slice((1, 2, 3)[g] * P, (2, 3, 4)[g] * P)
                units.append(Unit(half, q, keys, [v[:, g, b, features] for b in blocks], q,
                                  bias=bias[:, head, where], lse=lse))
    attention(K, units)
    merge_groups(K, lse, q_T[:, 0:6, :])
    memory_attention(K, 1, [q_T[:, 6 + i, :] for i in range(2)])
    mixed = Split(K, KT, S)
    split_tiles(K, [q_T[:, i, :] for i in range(KT)], mixed)
    src = [mixed.pair(i) for i in range(KT)]
    jobs = [Job(d // 2, P * (d % 2), P, 256, src, S, "dve", residual(x_T[:, d, :])) for d in range(KT)]
    project(K, jobs, 4)
    K.top = top



T2 = CTX + S
LAT = slice(CTX, T2)
RH, CH = 3, 64
NCH, TILES = T2 // CH, T2 // P
LEVELS = (4, 8, 16, 32, 64)
DECAY_SCALE = 0.6065306597126334


def modulation(K, layer, cond, mod):
    bias = K.col(f"b_mod{layer}")

    def shifted(tile):
        def evacuate(K, eng, ps):
            if 8 <= tile < 16:
                return eng.tensor_scalar(mod[:, tile, :], ps, bias[:, tile:tile + 1], 1.0, ALU.add, ALU.add)
            return eng.tensor_scalar(mod[:, tile, :], ps, bias[:, tile:tile + 1], None, ALU.add)
        return evacuate
    src = [cond[:, k, :] for k in range(KT)]
    project_few(K, [Job(i // 2, P * (i % 2), P, 256, src, 2, "dve", shifted(i)) for i in range(24)], 12)


def centred_evacuation(out, taps):
    def evacuate(K, eng, ps):
        K.link(eng, eng.tensor_scalar(out, ps, taps[:, 1:2], None, ALU.mult), "dve_step")
        for a, b in ((0, CTX), (CTX, T2)):
            ins = eng.scalar_tensor_tensor(out[:, a + 1:b], ps[:, a:b - 1], taps[:, 0:1], out[:, a + 1:b],
                                           ALU.mult, ALU.add)
        K.link(eng, ins, "dve_step")
        for a, b in ((0, CTX), (CTX, T2)):
            ins = eng.scalar_tensor_tensor(out[:, a:b - 1], ps[:, a + 1:b], taps[:, 2:3], out[:, a:b - 1],
                                           ALU.mult, ALU.add)
        return ins
    return evacuate


def rope(K, tiles, cos, sin, turn):
    top = K.top
    straight = K.alloc(2, S)
    with K.stage() as block:
        @block.tensor
        def _(pe):
            for i, x in enumerate(tiles):
                if i >= 2:
                    pe.wait_ge(*K.at("rotated", i - 2))
                pe.matmul(K.psum[:, i % 2, :], turn, x[:, LAT], start=True, stop=True).then_inc(*K.up("turned"))

        @block.vector
        def _(dve):
            for i, x in enumerate(tiles):
                if i >= 2:
                    dve.wait_ge(*K.at("rotated", i - 2))
                K.link(dve, dve.tensor_tensor(straight[:, i % 2, :], x[:, LAT], cos, ALU.mult), "dve_step")
                dve.wait_ge(*K.at("turned", i))
                K.link(dve, dve.tensor_tensor(x[:, LAT], K.psum[:, i % 2, :], sin, ALU.mult), "dve_step")
                dve.tensor_tensor(x[:, LAT], x[:, LAT], straight[:, i % 2, :], ALU.add).then_inc(*K.up("rotated"))
    K.top = top


def rwkv_prepare(K, layer, pair, r, k, ddad, lora, kr, bk, pc, bonus, scratch):
    top = K.top
    ld, L = K.alloc(2, T2), K.alloc(2, T2)
    iclr, decay_before = (scratch[:, i * 2 * T2:(i + 1) * 2 * T2].rearrange("p (d n) -> p d n", d=2) for i in range(2))
    kk, norm = K.alloc(T2), K.alloc(T2)
    less = K.alloc(1)
    col = lambda name, i=pair: K.col(f"{name}{layer}")[:, i:i + 1]
    banks = lambda i: K.psum[:, 2 * i:2 * i + 2, :].rearrange("p a b -> p (a b)")[:, 0:T2]
    parts = ((0, 512), (512, T2))
    tiled = lambda x: x.rearrange("p (t n) -> p t n", n=P)
    with K.stage() as block:
        @block.tensor
        def _(pe):
            for i in range(4):
                rows = slice(32 * i, 32 * i + 32)
                for a, b in parts:
                    mm = pe.matmul(banks(i)[:, a:b], lora[rows, pair * P:(pair + 1) * P], ddad[rows, a:b],
                                   start=True, stop=True)
                mm.then_inc(*K.up("logits_ready"))
            pe.wait_ge(*K.at("kk_squared", 0))
            pe.wait_ge(*K.at("sigmoid_ready", 0))
            for a, b in parts:
                mm = pe.matmul(banks(0)[:, a:b], K.const("head_ones"), norm[:, a:b], start=True, stop=True)
            mm.then_inc(*K.up("kk_summed"))
            pe.wait_ge(*K.at("bonus_terms", 0))
            pe.wait_ge(*K.at("sigmoid_ready", 1))
            for a, b in parts:
                mm = pe.matmul(banks(1)[:, a:b], K.const("head_ones"), bonus[:, a:b], start=True, stop=True)
            mm.then_inc(*K.up("bonus_summed"))

        @block.scalar
        def _(act):
            for i in range(4):
                d, out, bias = i % 2, (ld, iclr)[i // 2], ("decay_w0", "iclr_a0")[i // 2]
                act.wait_ge(*K.at("logits_ready", i))
                act.activation(out[:, d, :], banks(i), ACT.Sigmoid, bias=col(bias, 3 * d + pair)
                               ).then_inc(*K.up("sigmoid_ready"))
            act.wait_ge(*K.at("kk_raw", 0))
            act.activation(norm, kk, ACT.Square).then_inc(*K.up("kk_squared"))
            act.wait_ge(*K.at("norm_bounded", 0))
            act.activation(norm, norm, ACT.Sqrt).then_inc(*K.up("norm_ready"))
            for d in range(2):
                act.wait_ge(*K.at("sum_before", d))
                act.activation(decay_before[:, d, :], decay_before[:, d, :], ACT.Exp).then_inc(*K.up("before_ready"))
                act.activation(ld[:, d, :], L[:, d, :], ACT.Exp, scale=-1.0).then_inc(*K.up("inverse_ready"))
            for d in range(2):
                act.wait_ge(*K.at("inverse_ready", d))
                act.activation(L[:, d, :], L[:, d, :], ACT.Exp).then_inc(*K.up("decay_ready"))

        @block.vector
        def _(dve):
            dve.tensor_scalar(kk, k, col("k_k"), None, ALU.mult).then_inc(*K.up("kk_raw"))
            for d in range(2):
                dve.wait_ge(*K.at("sigmoid_ready", d))
                K.link(dve, dve.tensor_scalar(ld[:, d, :], ld[:, d, :], -DECAY_SCALE, None, ALU.mult), "dve_step")
                turn = slice(None) if d == 0 else slice(None, None, -1)
                K.link(dve, dve.tensor_tensor_scan(L[:, d, turn], K.reset[:, :], ld[:, d, turn], 0.0,
                                                   ALU.mult, ALU.add), "dve_step")
                dve.tensor_tensor(decay_before[:, d, :], L[:, d, :], ld[:, d, :], ALU.subtract
                                  ).then_inc(*K.up("sum_before"))
            dve.wait_ge(*K.at("kk_summed", 0))
            dve.wait_ge(*K.at("kk_squared", 0))
            dve.tensor_scalar(norm, banks(0), 1e-12, None, ALU.max).then_inc(*K.up("norm_bounded"))
            dve.wait_ge(*K.at("norm_ready", 0))
            K.link(dve, dve.reciprocal(norm, norm), "dve_step")
            K.link(dve, dve.tensor_tensor(kk, kk, norm, ALU.mult), "dve_step")
            for d in range(2):
                dve.wait_ge(*K.at("before_ready", d))
                dve.tensor_tensor(kr[:, d, :, 0, :], tiled(kk), tiled(decay_before[:, d, :]), ALU.mult)
            for d in range(2):
                dve.wait_ge(*K.at("sigmoid_ready", 2 + d))
                K.link(dve, dve.tensor_tensor(bk[:, d, 0, :], kk, iclr[:, d, :], ALU.mult), "iclr_used")
                dve.wait_ge(*K.at("inverse_ready", d))
                dve.tensor_tensor(bk[:, d, 0, :], bk[:, d, 0, :], ld[:, d, :], ALU.mult)
            for d in range(2):
                dve.wait_ge(*K.at("keys_ready", d))
                dve.tensor_tensor(bk[:, d, 1, :], iclr[:, d, :], ld[:, d, :], ALU.mult)
                dve.wait_ge(*K.at("decay_ready", d))
                dve.tensor_tensor(kr[:, d, :, 1, :], tiled(r), tiled(L[:, d, :]), ALU.mult)
                first = CH - 1 if d == 0 else 0
                dve.tensor_copy(pc[:, d, :], L[:, d, first:T2:CH])
            dve.wait_ge(*K.at("bonus_summed", 0))
            dve.tensor_copy(bonus, banks(1))

        @block.gpsimd
        def _(pool):
            pool.tensor_scalar(less, col("k_a"), -1.0, 1.0, ALU.mult, ALU.add).then_inc(*K.up("less_ready"))
            pool.wait_ge(*K.at("less_ready", 0))
            for d in range(2):
                pool.wait_ge(*K.at("sigmoid_ready", 2 + d))
                pool.wait_ge(*K.at("iclr_used", d))
                K.link(pool, pool.tensor_scalar(iclr[:, d, :], iclr[:, d, :], col("k_a"), less, ALU.mult, ALU.add),
                       "pool_step")
                pool.tensor_tensor(iclr[:, d, :], iclr[:, d, :], k, ALU.mult).then_inc(*K.up("keys_ready"))
            for d in range(2):
                pool.wait_ge(*K.at("keys_ready", d))
            K.link(pool, pool.tensor_tensor(bonus, iclr[:, 0, :], iclr[:, 1, :], ALU.add), "pool_step")
            K.link(pool, pool.tensor_tensor(bonus, bonus, r, ALU.mult), "pool_step")
            pool.tensor_scalar(bonus, bonus, col("r_k"), None, ALU.mult).then_inc(*K.up("bonus_terms"))
    K.top = top


def rwkv_chunks(K, kr, bk, pc, v, step, carry, y):
    top = K.top
    K.top = K.ring_at
    ab, bd = (K.alloc(2, 2, 4 * P) for _ in range(2))
    ab = ab.rearrange("p s d (e a t) -> p s d e a t", e=2, a=2)
    bd = bd.rearrange("p s d (e a t) -> p s d e a t", e=2, a=2)
    corner = K.alloc(2, 2, 4, P)
    both = K.alloc(2, 2, 4 * P)
    assert K.top <= K.ring_end
    K.top = top
    prod = K.alloc(2, 4, P)
    x = K.alloc(2, 4, P)
    b_tok, k_tok, v_tok = K.alloc(2, 2, P), K.alloc(2, 2, P), K.alloc(2, P)
    kp, nu = K.alloc(2, 2, P), K.alloc(2, 2, P)
    TT = both[:, :, 0].rearrange("p s (u t) -> p s u t", u=4)
    T = both[:, :, 1].rearrange("p s (u t) -> p s u t", u=4)
    bank = lambda i: K.psum[:, i, :]
    four = lambda i: bank(i).rearrange("p (u t) -> p u t", u=4)
    ident4 = K.const("identity").rearrange("p (a b) -> p a b", a=1).to_broadcast([P, 4, P])
    ident2 = K.const("identity").rearrange("p (a b) -> p a b", a=1).to_broadcast([P, 2, P])
    heads2 = K.const("head_ones").rearrange("p (a b) -> p a b", a=1).to_broadcast([P, 2, P])
    units = [(d, e) for d in range(2) for e in range(2)]

    def level_mask(d, i):
        return K.level_masks[:, i, d, :].rearrange("p (a b) -> p a b", a=1).to_broadcast([P, 2, P])

    NL = len(LEVELS)

    def event(t, i):
        return (t // 2 * NL + i) * 2 + t % 2

    with K.stage() as block:
        @block.tensor
        def _(pe):
            def scores(t):
                s, tok = t % 2, slice(t * P, (t + 1) * P)
                if t >= 1 and s == 1:
                    pe.wait_ge(*K.at("x_ready", t - 1))
                if t >= 2 and s == 0:
                    pe.wait_ge(*K.at("steps_copied", t - 1))
                    pe.wait_ge(*K.at("own_copied", t - 1))
                for d in range(2):
                    pe.transpose(bank(6)[:, d * P:(d + 1) * P], bk[:, d, 0, tok], K.const("identity"))
                    pe.transpose(bank(6)[:, (2 + d) * P:(3 + d) * P], bk[:, d, 1, tok], K.const("identity"))
                    pe.transpose(bank(7)[:, d * P:(d + 1) * P], kr[:, d, t, 0, :], K.const("identity"))
                pe.transpose(bank(7)[:, 2 * P:3 * P], v[:, tok], K.const("identity")).then_inc(*K.up("tokens_turned"))
                if s == 1:
                    pe.wait_ge(*K.at("inverse_begun", t - 1))
                for d, e in units:
                    rows = slice(64 * e, 64 * e + 64)
                    rhs = kr[rows, d, t, :, :].rearrange("p a b -> p (a b)")
                    pe.matmul(bank(e)[:, 256 * d:256 * d + 256], bk[rows, d, 0, tok], rhs, start=True, stop=True)
                    pe.matmul(bank(2 + e)[:, 256 * d:256 * d + 256], bk[rows, d, 1, tok], rhs, start=True, stop=True)
                    mm = pe.matmul(bank(4 + e)[:, P * d:P * d + P], kr[rows, d, t, 0, :], bk[rows, d, 0, tok],
                                   start=True, stop=True)
                mm.then_inc(*K.up("scores_done"))
                pe.wait_ge(*K.at("masked", t))
                pe.wait_ge(*K.at("tokens_copied", t))
                for u, (d, e) in enumerate(units):
                    mm = pe.matmul(four(6)[:, u, :], bd[:, s, d, e, 0, :], v_tok[:, s, :], start=True, stop=True)
                mm.then_inc(*K.up("bv_ready"))

            def corners(t, i):
                s = t % 2
                pe.wait_ge(*K.at("corner_ready", event(t, i)))
                if i == 0:
                    pe.wait_ge(*K.at("inverse_begun", t))
                    if s == 0:
                        pe.wait_ge(*K.at("inverse_begun", t + 1))
                else:
                    pe.wait_ge(*K.at("inverse_grown", event(t, i - 1)))
                for u in range(4):
                    mm = pe.matmul(four(3 * s)[:, u, :], corner[:, s, i % 2, u, :], T[:, s, u, :], start=True, stop=True)
                mm.then_inc(*K.up("corner_product"))

            def growth(t, i):
                s = t % 2
                pe.wait_ge(*K.at("product_copied", event(t, i)))
                for u in range(4):
                    mm = pe.matmul(four(3 * s + 1)[:, u, :], prod[:, s, u, :], TT[:, s, u, :], start=True, stop=True)
                if i + 1 < NL:
                    for u in range(4):
                        mm = pe.matmul(four(3 * s + 2)[:, u, :], TT[:, s, u, :], prod[:, s, u, :],
                                       start=True, stop=True)
                mm.then_inc(*K.up("growth_ready"))

            def solve(t):
                s = t % 2
                pe.wait_ge(*K.at("inverse_grown", event(t, NL - 1)))
                pe.wait_ge(*K.at("x_ready", t))
                if s == 0:
                    pe.wait_ge(*K.at("x_ready", t + 1))
                for u in range(4):
                    mm = pe.matmul(four(6 + s)[:, u, :], TT[:, s, u, :], x[:, s, u, :], start=True, stop=True)
                mm.then_inc(*K.up("ku_ready"))

            def own(t):
                s = t % 2
                pe.wait_ge(*K.at("ku_copied", t))
                for d in range(2):
                    rhs = ab[:, s, d, :, 1, :]
                    pe.matmul(bank(2 * s)[:, 256 * d:256 * d + 256], kp[:, s, d, :], rhs, start=True, stop=True)
                    pe.matmul(bank(2 * s + 1)[:, 0:256], v_tok[:, s, :], bd[:, s, d, :, 1, :], start=d == 0, stop=False)
                    mm = pe.matmul(bank(2 * s + 1)[:, 0:256], nu[:, s, d, :], rhs, start=False, stop=d == 1)
                mm.then_inc(*K.up("own_ready"))

            def steps(t):
                s = t % 2
                if s == 0:
                    pe.wait_ge(*K.at("inverse_grown", event(t + 1, NL - 1)))
                for d in range(2):
                    for c in range(2):
                        rows, at, at2 = slice(64 * c, 64 * c + 64), slice(d * P, (d + 1) * P), slice((2 + d) * P, (3 + d) * P)
                        ps = bank(4 + 2 * s + c)
                        pe.matmul(ps[:, at], kp[rows, s, d, :], b_tok[rows, s, d, :], start=True, stop=True)
                        pe.matmul(ps[:, at2], k_tok[rows, s, d, :], v_tok[rows, s, :], start=True, stop=False)
                        mm = pe.matmul(ps[:, at2], b_tok[rows, s, d, :], nu[rows, s, d, :], start=False, stop=True)
                mm.then_inc(*K.up("steps_ready"))

            for t in range(0, TILES, 2):
                scores(t)
                scores(t + 1)
                for i in range(NL):
                    corners(t, i)
                    corners(t + 1, i)
                    growth(t, i)
                    growth(t + 1, i)
                solve(t)
                solve(t + 1)
                own(t)
                steps(t)
                pe.wait_ge(*K.at("ku_copied", t + 1))
                own(t + 1)
                steps(t + 1)

        @block.vector
        def _(dve):
            def begin(t):
                s = t % 2
                dve.wait_ge(*K.at("scores_done", t))
                if t >= 2:
                    dve.wait_ge(*K.at("steps_ready", t - s - 1))
                for e in range(2):
                    for src, dst in ((e, ab), (2 + e, bd)):
                        out = dst[:, s, :, e].rearrange("p d a t -> p d (a t)")
                        ins = dve.tensor_tensor(out, bank(src).rearrange("p (d n) -> p d n", d=2), K.order_masks,
                                                ALU.mult)
                K.link(dve, ins, "masked")
                for e in range(2):
                    mine = lambda m: m[:, s].rearrange("p (d e) t -> p d e t", d=2)[:, :, e, :]
                    dve.tensor_tensor(mine(T), bank(4 + e)[:, 0:256].rearrange("p (d t) -> p d t", d=2),
                                      K.first_masks[:, 0], ALU.mult)
                    ins = dve.tensor_tensor(mine(TT), ab[:, s, :, e, 0, :], K.first_masks[:, 1], ALU.mult)
                K.link(dve, ins, "dve_step")
                dve.tensor_tensor(T[:, s], T[:, s], ident4, ALU.add)
                dve.tensor_tensor(TT[:, s], TT[:, s], ident4, ALU.add).then_inc(*K.up("inverse_begun"))
                dve.wait_ge(*K.at("bv_ready", t))
                by_head = lambda m: m.rearrange("p (d e) n -> p d e n", d=2)
                for e in range(2):
                    ins = dve.tensor_copy(by_head(x[:, s])[:, :, e, 64:128],
                                          by_head(four(6))[:, :, e, 64 * e:64 * e + 64])
                ins.then_inc(*K.up("x_ready"))

            def grow(t, i):
                s = t % 2
                dve.wait_ge(*K.at("growth_ready", event(t, i)))
                if i + 1 < NL:
                    two = K.psum[:, 3 * s + 1:3 * s + 3, :]
                    dve.tensor_tensor(both[:, s], both[:, s], two, ALU.subtract).then_inc(*K.up("inverse_grown"))
                else:
                    dve.tensor_tensor(TT[:, s], TT[:, s], four(3 * s + 1), ALU.subtract).then_inc(*K.up("inverse_grown"))

            def copy_own(t):
                s = t % 2
                dve.wait_ge(*K.at("own_ready", t))
                for e in range(2):
                    rows = slice(64 * e, 64 * e + 64)
                    out = kr[rows, :, t, 1, :]
                    dve.tensor_tensor(out, out, bank(2 * s)[rows].rearrange("p (d n) -> p d n", d=2)[:, :, P * e:P * e + P],
                                      ALU.subtract)
                    ins = dve.tensor_copy(y[rows, t * P:(t + 1) * P], bank(2 * s + 1)[rows, P * e:P * e + P])
                ins.then_inc(*K.up("own_copied"))

            def copy_steps(t):
                s = t % 2
                dve.wait_ge(*K.at("steps_ready", t))
                at = [step[:, :, 2 * t + c, :] for c in range(2)]
                for c in range(2):
                    ps = bank(4 + 2 * s + c)
                    for d in range(2):
                        dve.scalar_tensor_tensor(carry[:, d, 2 * t + c, :], ps[:, (2 + d) * P:(3 + d) * P],
                                                 pc[:, d, 2 * t + c:2 * t + c + 1], K.const("head_ones"),
                                                 ALU.mult, ALU.mult)
                    ins = dve.tensor_tensor(at[c], ps[:, 0:256].rearrange("p (d n) -> p d n", d=2), heads2, ALU.mult)
                ins.then_inc(*K.up("dve_step"))
                dve.wait_ge(*K.now("dve_step"))
                for c in range(2):
                    ins = dve.tensor_tensor(at[c], ident2, at[c], ALU.subtract)
                ins.then_inc(*K.up("steps_copied"))

            for t in range(0, TILES, 2):
                begin(t)
                begin(t + 1)
                for i in range(NL):
                    grow(t, i)
                    grow(t + 1, i)
                copy_own(t)
                copy_steps(t)
                copy_own(t + 1)
                copy_steps(t + 1)

        @block.scalar
        def _(act):
            def copy_tokens(t):
                s = t % 2
                act.wait_ge(*K.at("tokens_turned", t))
                if t >= 2:
                    act.wait_ge(*K.at("steps_ready", t - s - 1))
                act.copy(b_tok[:, s], bank(6)[:, 0:2 * P].rearrange("p (d n) -> p d n", d=2))
                act.copy(k_tok[:, s], bank(6)[:, 2 * P:4 * P].rearrange("p (d n) -> p d n", d=2))
                act.copy(x[:, s, :, 0:64], bank(7)[:, 0:256].rearrange("p (u n) -> p u n", u=4))
                act.copy(v_tok[:, s], bank(7)[:, 2 * P:3 * P]).then_inc(*K.up("tokens_copied"))

            for t in range(0, TILES, 2):
                copy_tokens(t)
                copy_tokens(t + 1)
                for i in range(NL):
                    for tile in (t, t + 1):
                        act.wait_ge(*K.at("corner_product", event(tile, i)))
                        act.copy(prod[:, tile % 2], four(3 * (tile % 2))).then_inc(*K.up("product_copied"))
                for s in range(2):
                    act.wait_ge(*K.at("ku_ready", t + s))
                    ku = bank(6 + s).rearrange("p (u w n) -> p u w n", u=4, w=2)
                    parts = lambda m: m[:, s].rearrange("p d (e n) -> p (d e) n", e=2)
                    act.copy(parts(kp), ku[:, :, 0, :])
                    act.mul(parts(nu), ku[:, :, 1, :], -1.0).then_inc(*K.up("ku_copied"))

        @block.gpsimd
        def _(pool):
            for t in range(0, TILES, 2):
                for i in range(NL):
                    for tile in (t, t + 1):
                        s = tile % 2
                        if i == 0:
                            pool.wait_ge(*K.at("masked", tile))
                        if i >= 2:
                            pool.wait_ge(*K.at("corner_product", event(tile, i - 2)))
                        for d in range(2):
                            ins = pool.tensor_tensor(corner[:, s, i % 2, 2 * d:2 * d + 2, :], ab[:, s, d, :, 0, :],
                                                     level_mask(d, i), ALU.mult)
                        ins.then_inc(*K.up("corner_ready"))
    K.top = top


def rwkv_scan(K, kr, pc, step, carry, y, first_out):
    order = [list(range(NCH)), list(range(CTX // CH - 1, -1, -1)) + list(range(NCH - 1, CTX // CH - 1, -1))]
    with K.stage() as block:
        @block.tensor
        def _(pe):
            for j in range(1, NCH - 1):
                if j >= 2:
                    pe.wait_ge(*K.at("state_ready", 2 * (j - 2) + 1))
                for d in range(2):
                    pe.matmul(K.psum[:, 2 * (j % 2) + d, 0:P], step[:, d, order[d][j], :], carry[:, d, order[d][j - 1], :],
                              start=True, stop=True).then_inc(*K.up("state_moved"))
            pe.wait_ge(*K.at("state_ready", 2 * (NCH - 3) + 1))
            for c in range(first_out, NCH):
                at = K.psum[:, 4 + c // 8, (c % 8) * CH:(c % 8 + 1) * CH]
                before = [(d, order[d][order[d].index(c) - 1]) for d in range(2) if order[d].index(c) > 0]
                for n, (d, prior) in enumerate(before):
                    mm = pe.matmul(at, carry[:, d, prior, :], kr[:, d, c // 2, 1, (c % 2) * CH:(c % 2 + 1) * CH],
                                   start=n == 0, stop=n == len(before) - 1)
            mm.then_inc(*K.up("outputs_ready"))

        @block.vector
        def _(dve):
            for j in range(1, NCH - 1):
                for d in range(2):
                    c = order[d][j]
                    dve.wait_ge(*K.at("state_moved", 2 * (j - 1) + d))
                    dve.scalar_tensor_tensor(carry[:, d, c, :], K.psum[:, 2 * (j % 2) + d, 0:P], pc[:, d, c:c + 1],
                                             carry[:, d, c, :], ALU.mult, ALU.add).then_inc(*K.up("state_ready"))
            dve.wait_ge(*K.at("outputs_ready", 0))
            a = first_out * CH
            for lo, hi in ((a, 512), (512, T2)):
                out = y[:, lo:hi]
                dve.tensor_tensor(out, out, K.psum[:, 4:6, :].rearrange("p a b -> p (a b)")[:, lo:hi], ALU.add)


def rwkv_finish(K, layer, pair, y, v, bonus, gate, out, a):
    top = K.top
    n = T2 - a
    tok = slice(a, T2)
    centred, sq, std = K.alloc(n), K.alloc(n), K.alloc(n)
    col = lambda name: K.col(f"{name}{layer}")[:, pair:pair + 1]
    banks = lambda i: K.psum[:, 2 * i:2 * i + 2, :].rearrange("p a b -> p (a b)")[:, 0:n]
    cuts = [(lo, min(lo + 512, n)) for lo in range(0, n, 512)]
    with K.stage() as block:
        @block.tensor
        def _(pe):
            for lo, hi in cuts:
                mm = pe.matmul(banks(0)[:, lo:hi], K.const("head_ones"), y[:, a + lo:a + hi], start=True, stop=True)
            mm.then_inc(*K.up("mean_ready"))
            pe.wait_ge(*K.at("deviation_squared", 0))
            for lo, hi in cuts:
                mm = pe.matmul(banks(1)[:, lo:hi], K.const("head_ones"), sq[:, lo:hi], start=True, stop=True)
            mm.then_inc(*K.up("variance_ready"))

        @block.vector
        def _(dve):
            dve.wait_ge(*K.at("mean_ready", 0))
            dve.scalar_tensor_tensor(centred, banks(0), -1.0 / HD, y[:, tok], ALU.mult, ALU.add
                                     ).then_inc(*K.up("centred"))
            dve.wait_ge(*K.at("std_ready", 0))
            K.link(dve, dve.reciprocal(std, std), "dve_step")
            K.link(dve, dve.scalar_tensor_tensor(centred, centred, col("gn_g"), std, ALU.mult, ALU.mult), "dve_step")
            dve.wait_ge(*K.at("bonus_ready", 0))
            K.link(dve, dve.scalar_tensor_tensor(centred, centred, col("gn_b"), bonus[:, tok], ALU.add, ALU.add),
                   "dve_step")
            dve.tensor_tensor(out[:, tok], centred, gate, ALU.mult)

        @block.scalar
        def _(act):
            act.wait_ge(*K.at("centred", 0))
            act.activation(sq, centred, ACT.Square).then_inc(*K.up("deviation_squared"))
            act.wait_ge(*K.at("variance_ready", 0))
            act.activation(std, banks(1), ACT.Sqrt, scale=1.0 / HD, bias=K.const("eps_gn")).then_inc(*K.up("std_ready"))

        @block.gpsimd
        def _(pool):
            pool.tensor_tensor(bonus[:, tok], bonus[:, tok], v[:, tok], ALU.mult).then_inc(*K.up("bonus_ready"))
    K.top = top


def layer_norm(K, layer, x, n):
    top = K.top
    sq, mean, std = K.alloc(2, n), K.alloc(n), K.alloc(n)
    banks = lambda i: K.psum[:, 2 * i:2 * i + 2, :].rearrange("p a b -> p (a b)")[:, 0:n]
    cuts = [(lo, min(lo + 512, n)) for lo in range(0, n, 512)]
    g, b = K.col(f"ln_g{layer}"), K.col(f"ln_b{layer}")
    with K.stage() as block:
        @block.tensor
        def _(pe):
            for k in range(KT):
                for lo, hi in cuts:
                    mm = pe.matmul(banks(0)[:, lo:hi], K.const("ones"), x[:, k, lo:hi], start=k == 0, stop=k == KT - 1)
            mm.then_inc(*K.up("mean_ready"))
            for k in range(KT):
                pe.wait_ge(*K.at("square_ready", k))
                for lo, hi in cuts:
                    mm = pe.matmul(banks(1)[:, lo:hi], K.const("ones"), sq[:, k % 2, lo:hi], start=k == 0, stop=k == KT - 1)
                mm.then_inc(*K.up("square_summed"))

        @block.vector
        def _(dve):
            dve.wait_ge(*K.at("mean_ready", 0))
            K.link(dve, dve.tensor_scalar(mean, banks(0), -1.0 / D, None, ALU.mult), "dve_step")
            for k in range(KT):
                dve.tensor_tensor(x[:, k, :], x[:, k, :], mean, ALU.add).then_inc(*K.up("centred"))
            dve.wait_ge(*K.at("std_ready", 0))
            K.link(dve, dve.reciprocal(std, std), "dve_step")
            for k in range(KT):
                dve.scalar_tensor_tensor(x[:, k, :], x[:, k, :], g[:, k:k + 1], std, ALU.mult, ALU.mult
                                         ).then_inc(*K.up("scaled"))

        @block.scalar
        def _(act):
            for k in range(KT):
                act.wait_ge(*K.at("centred", k))
                if k >= 2:
                    act.wait_ge(*K.at("square_summed", k - 2))
                act.activation(sq[:, k % 2, :], x[:, k, :], ACT.Square).then_inc(*K.up("square_ready"))
            act.wait_ge(*K.at("square_summed", KT - 1))
            act.activation(std, banks(1), ACT.Sqrt, scale=1.0 / D, bias=K.const("eps_ln")).then_inc(*K.up("std_ready"))
            for k in range(KT):
                act.wait_ge(*K.at("scaled", k))
                act.activation(x[:, k, :], x[:, k, :], ACT.Identity, bias=b[:, k:k + 1])
    K.top = top


def gated_residual(x, mod, tile, a):
    def evacuate(K, eng, ps):
        x_new = x
        K.link(eng, eng.tensor_scalar(x_new, x_new, ALPHA, None, ALU.mult), "dve_step")
        for (lo, hi), which in (((0, CTX), 1), ((CTX, T2), 0)):
            if hi > a:
                ins = eng.scalar_tensor_tensor(x_new[:, lo - a:hi - a], ps[:, lo - a:hi - a],
                                               mod[:, 16 + tile, which:which + 1], x_new[:, lo - a:hi - a],
                                               ALU.mult, ALU.add)
        return ins
    return evacuate


def second_layer(K, layer, x, cond):
    top = K.top
    final = layer == 1
    a = CTX if final else 0
    n = T2 - a
    mod = K.alloc(24, 2)
    modulation(K, layer, cond, mod)
    conv, gates = K.alloc(10, T2), K.alloc(8, T2)
    q, nq = K.alloc(3, T2), K.alloc(2, T2)
    mark = K.top
    kg, nk, v_tok = K.alloc(T2), K.alloc(2, T2), K.alloc(TILES, 384)
    inner = K.top
    h = Split(K, KT, T2)
    full = q[:, 0:2, :]
    with K.stage() as block:
        @block.vector
        def _(dve):
            for k in range(KT):
                if k >= 2:
                    dve.wait_ge(*K.at("lo_ready", k - 2))
                dve.tensor_scalar(full[:, k % 2, LAT], x[:, k, LAT], mod[:, 8 + k, 0:1], mod[:, k, 0:1],
                                  ALU.mult, ALU.add)
                dve.tensor_scalar(full[:, k % 2, 0:CTX], x[:, k, 0:CTX], mod[:, 8 + k, 1:2], mod[:, k, 1:2],
                                  ALU.mult, ALU.add).then_inc(*K.up("modulated"))

        @block.scalar
        def _(act):
            for k in range(KT):
                act.wait_ge(*K.at("modulated", k))
                act.copy(h.hi[:, k, :], full[:, k % 2, :]).then_inc(*K.up("hi_ready"))

        @block.gpsimd
        def _(pool):
            for k in range(KT):
                pool.wait_ge(*K.at("hi_ready", k))
                pool.tensor_tensor(h.lo[:, k, :], full[:, k % 2, :], h.hi[:, k, :].bitcast(F32),
                                   ALU.subtract).then_inc(*K.up("lo_ready"))
    whole = [h.pair(k) for k in range(KT)]
    asked = [tuple(x[:, a:T2] for x in h.pair(k)) for k in range(KT)]
    taps = K.col(f"rwkv_conv{layer}")
    jobs = []

    def feature(src, m, engine, evacuate):
        i = len(jobs)
        jobs.append(Job(i // 2, P * (i % 2), P, 256, src, m, engine, evacuate))
    for i in range(10):
        feature(whole, T2, "dve", centred_evacuation(conv[:, i, :], taps[:, 3 * i:3 * i + 3]))
    for i in range(3):
        feature(asked, n, "act", act_to(gates[:, i, a:T2], ACT.Silu))
    for i in range(3):
        feature(asked, n, "dve", copy_to(q[:, i, a:T2]))
    feature(whole, T2, "dve", copy_to(kg))
    for i in range(3):
        feature(asked, n, "act", act_to(gates[:, 3 + i, a:T2], ACT.Silu))
    for i in range(2):
        feature(asked, n, "dve", copy_to(nq[:, i, a:T2]))
    for i in range(2):
        feature(whole, T2, "dve", copy_to(nk[:, i, :]))
    for i in range(2):
        feature(asked, n, "act", act_to(gates[:, 6 + i, a:T2], ACT.Silu))
    for t in range(TILES):
        jobs.append(Job(13, 0, 256, 256, whole, T2, "act" if t % 2 else "dve", copy_to(v_tok[:, t, 0:256]),
                        tokens=block_of(t)))
    for t in range(TILES):
        jobs.append(Job(14, 0, P, P, whole, T2, "act" if t % 2 else "dve", copy_to(v_tok[:, t, 256:384]),
                        tokens=block_of(t)))
    project(K, jobs, 15, ahead=0)

    K.top = inner
    cos, sin, turn = K.alloc(S), K.alloc(S), K.alloc(P)
    bias, mask = K.alloc(4, 16, 64), K.alloc(64)
    load(K, [(cos, K.dram["rope_cos"]), (sin, K.dram["rope_sin"]), (turn, K.dram["rope_turn"]),
             (bias.rearrange("p a b c -> p (a b c)"), K.dram["window_bias"][layer]), (mask, K.dram["window_mask"])])
    head_norm(K, [q[:, i, a:T2] for i in range(3)], n, K.col(f"gqa_q_norm{layer}"))
    head_norm(K, [kg], T2, K.col(f"gqa_k_norm{layer}"))
    rope(K, [q[:, i, :] for i in range(3)] + [kg], cos, sin, turn)
    with K.stage() as block:
        @block.vector
        def _(dve):
            every = mask.rearrange("p (a b) -> p a b", a=1).to_broadcast([P, 64, 64])
            rows = bias.rearrange("p a b c -> p (a b) c")
            dve.tensor_tensor(rows, rows, every, ALU.add)
    units = []
    for half in range(2):
        rows = slice(64 * half, 64 * half + 64)
        for t in range(TILES):
            tok = slice(t * P, (t + 1) * P)
            if t * P < a:
                continue
            in_ctx = (t + 1) * P <= CTX
            keys, blocks = slice(0, CTX if in_ctx else T2), range(CTX // P if in_ctx else TILES)
            for i in range(3):
                units.append(Unit(half, q[rows, i, tok], kg[rows, keys], [v_tok[:, b, 256:384] for b in blocks],
                                  q[rows, i, tok]))
            for i in range(2):
                window = None
                if not in_ctx:
                    r0 = 2 * (t - CTX // P)
                    window = bias[:, 2 * i + half, 7 - r0:15 - r0, :].rearrange("p a b -> p (a b)")
                units.append(Unit(half, nq[rows, i, tok], nk[rows, i, keys],
                                  [v_tok[:, b, P * i:P * i + P] for b in blocks], nq[rows, i, tok], bias=window))
    attention(K, units)

    with K.stage() as block:
        @block.vector
        def _(dve):
            for i in range(3):
                dve.tensor_tensor(q[:, i, a:T2], q[:, i, a:T2], gates[:, 3 + i, a:T2], ALU.mult)
            for i in range(2):
                dve.tensor_tensor(nq[:, i, a:T2], nq[:, i, a:T2], gates[:, 6 + i, a:T2], ALU.mult)

        @block.scalar
        def _(act):
            act.activation(conv[0:64, 9, :], conv[0:64, 9, :], ACT.Tanh)
    spare = gates[:, 3:8, :].rearrange("p a b -> p (a b)")
    step = spare[:, 0:2 * NCH * P].rearrange("p (d c n) -> p d c n", d=2, c=NCH)
    pc = spare[:, 2 * NCH * P:2 * NCH * P + 2 * NCH].rearrange("p (d c) -> p d c", d=2)
    K.top = mark
    K.reset = K.alloc(T2)
    K.order_masks, K.first_masks = K.alloc(2, 2 * P), K.alloc(2, 2, P)
    K.level_masks, lora = K.alloc(len(LEVELS), 2, P), K.alloc(RH * P)
    load(K, [(K.reset, K.dram["reset"]), (K.order_masks.rearrange("p a b -> p (a b)"), K.dram["order_masks"]),
             (K.first_masks.rearrange("p a b c -> p (a b c)"), K.dram["first_masks"]),
             (K.level_masks.rearrange("p a b c -> p (a b c)"), K.dram["level_masks"]), (lora, K.dram["lora"][layer])])
    kr, bk = K.alloc(2, TILES, 2, P), K.alloc(2, 2, T2)
    carry, bonus = K.alloc(2, NCH, P), K.alloc(T2)
    for pair in range(RH):
        r, k, v = conv[:, pair, :], conv[:, 3 + pair, :], conv[:, 6 + pair, :]
        y = k
        rwkv_prepare(K, layer, pair, r, k, conv[:, 9, :], lora, kr, bk, pc, bonus,
                     carry.rearrange("p a b c -> p (a b c)"))
        rwkv_chunks(K, kr, bk, pc, v, step, carry, y)
        rwkv_scan(K, kr, pc, step, carry, y, a // CH)
        rwkv_finish(K, layer, pair, y, v, bonus, gates[:, pair, a:T2], r, a)
    K.top = mark
    mixed = Split(K, KT, n)
    split_tiles(K, [conv[:, i, a:T2] for i in range(3)] + [q[:, i, a:T2] for i in range(3)]
                + [nq[:, i, a:T2] for i in range(2)], mixed)
    src = [mixed.pair(i) for i in range(KT)]
    jobs = [Job(d // 2, P * (d % 2), P, 256, src, n, "dve", gated_residual(x[:, d, a:T2], mod, d, a)) for d in range(KT)]
    project(K, jobs, 4)
    K.top = inner
    layer_norm(K, layer, x[:, :, a:T2], n)
    K.top = top


def chunk_plan():
    full = [(k * P, P) for k in range(KT)]
    plan = []

    def add(names, layer, cols, rows=None):
        plan.append((names, layer, cols, rows or full))

    def both(a, b, n=P):
        return [(a, n), (b, n)]

    def ffn_chunks(which, layer):
        for f in range(FT):
            add([f"ffn{which}_w_gate", f"ffn{which}_w_up"], layer, [[(f * P, P)], [(f * P, P)]])
        for d in range(KT):
            for half in range(2):
                add([f"ffn{which}_w_down"], layer, [[(d * P, P)]],
                    [((half * (FT // 2) + f) * P, P) for f in range(FT // 2)])

    def span(name, layer, start, stop, step=256, rows=None):
        for c in range(start, stop, step):
            add([name], layer, [[(c, min(step, stop - c))]], rows)

    w = ML_H * ML_D
    ffn_chunks(1, 0)
    span("a_w_in", 0, 0, 2 * w, 192)
    span("a_w_in", 0, 3 * w, 4 * w, 192)
    span("a_w_in", 0, 2 * w, 3 * w)
    span("a_w_in", 0, 4 * w + 8, 4 * w + 8 + 256)
    span("a_w_in", 0, 4 * w, 4 * w + 8)
    span("w_mem_kv", 0, 0, 512)
    span("a_w_out", 0, 0, D, P, [(96 * i, 96) for i in range(8)] + [(w + P * i, P) for i in range(2)])
    ffn_chunks(2, 0)
    span("w_kv", None, 0, 1536)
    ffn_chunks(1, 1)
    span("b_w_q", 0, 0, D)
    span("w_mem_kv", 1, 0, 512)
    span("b_w_out", 0, 0, D)
    ffn_chunks(2, 1)
    second_plan(add, span)
    return plan


def second_plan(add, span):
    tiles = lambda at, n: [[(at + P * i, P)] for i in range(n)]
    paired = lambda at: [[(at + HD * i, HD), (at + HD * (i + 3), HD)] for i in range(3)]
    mixed = [[(P * i, P)] for i in range(3)] + paired(384) + tiles(768, 2)
    for layer in range(2):
        span("w_mod_2", layer, 0, 3 * D)
        order = (tiles(0, 10) + tiles(1280, 3) + paired(1664) + tiles(2048, 1) + paired(2304)
                 + tiles(2688, 2) + tiles(2944, 2) + tiles(3456, 2))
        for i in range(0, len(order), 2):
            add(["w_in_2"], layer, [order[i] + order[i + 1]])
        add(["w_in_2"], layer, [[(3200, 256)]])
        add(["w_in_2"], layer, [[(2176, P)]])
        span("w_out_2", layer, 0, D, rows=mixed)


def chunk_width(chunk):
    names, layer, cols, rows = chunk
    return len(rows) * sum(n for part in cols for _, n in part)


def build(nc, dram, out, cols, n_cols, consts, n_consts):
    plan = [("weights", i, chunk_width(c)) for i, c in enumerate(chunk_plan())]
    with ExitStack() as ctx:
        K = Core(nc, ctx, dram, cols, consts, plan)
        K.cols_sb, K.consts_sb = K.alloc(n_cols), K.alloc(n_consts)
        x = K.alloc(KT, T2)
        x_T = x[:, :, LAT]
        cond = K.alloc(KT, 2)
        top = K.top
        load(K, [(K.cols_sb, dram["columns"]), (K.consts_sb, dram["constants"]),
                 (x_T, dram["x_T"]),
                 (cond.rearrange("p a b -> p (a b)"), dram["conditions"])])
        spare = x[:, :, 0:CTX]
        ffn(K, x_T, K.col("ffn1_norm0"), spare)
        mlstm_layer(K, x_T)
        k_T, v = K.alloc(6, S), K.alloc(3, S // P, 256)
        ffn(K, x_T, K.col("ffn2_norm0"), spare)
        shared_keys(K, x_T, k_T, v)
        ffn(K, x_T, K.col("ffn1_norm1"), spare)
        dilated_layer(K, x_T, k_T, v)
        ffn(K, x_T, K.col("ffn2_norm1"), spare)
        K.top = top
        load(K, [(x[:, :, 0:CTX], dram["ctx_T"])])
        with K.stage() as block:
            @block.scalar
            def _(act):
                act.activation(cond, cond, ACT.Silu)
        second_layer(K, 0, x, cond)
        second_layer(K, 1, x, cond)
        with K.stage() as block:
            @block.sync
            def _(sp):
                sp.dma_start(out, x_T).then_inc(*K.up("result_stored", 16))
                sp.wait_ge(*K.at("result_stored", 0, 16))


def host_columns(inputs):
    import numpy as np

    blocks = {}

    def per_feature(name, values):
        blocks[name] = values.reshape(-1, P).T

    for i in range(2):
        for name in ("ffn1_norm", "ffn2_norm", "mix_norm", "mem_norm"):
            per_feature(f"{name}{i}", inputs[name][i])
        for name in ("mem_q_norm", "mem_k_norm"):
            per_feature(f"{name}{i}", np.tile(inputs[name][i], 2))
    per_feature("kv_norm", inputs["kv_norm"])
    per_feature("b_q_norm", np.tile(inputs["b_q_norm"][0], 2))
    per_feature("kv_k_norm", np.tile(inputs["kv_k_norm"], 2))

    def rows96(a):
        full = np.zeros((P, a.shape[1]), a.dtype)
        full[0:96] = a
        return full
    for i in range(2):
        per_feature(f"b_mod{i}", inputs["b_mod_2"][i])
        blocks[f"rwkv_conv{i}"] = inputs["rwkv_conv_2"][i].reshape(3, 10, P).transpose(2, 1, 0).reshape(P, 30)
        per_feature(f"decay_w0{i}", inputs["decay_w0_2"][i])
        per_feature(f"iclr_a0{i}", inputs["iclr_a0_2"][i])
        for name in ("k_k", "k_a", "r_k", "gn_g", "gn_b"):
            per_feature(f"{name}{i}", inputs[f"rwkv_{name}_2"][i].reshape(-1))
        for name in ("gqa_q_norm", "gqa_k_norm"):
            per_feature(f"{name}{i}", np.tile(inputs[f"{name}_2"][i], 2))
        for name in ("ln_g", "ln_b"):
            per_feature(f"{name}{i}", inputs[f"{name}_2"][i])
    conv = inputs["a_conv"][0].reshape(4, 16, 96)
    blocks["a_conv"] = rows96(conv.transpose(2, 1, 0).reshape(96, 64))
    blocks["a_h_norm"] = rows96(inputs["a_h_norm"][0].reshape(8, 96).T)
    blocks["a_gate_bias"] = np.tile(inputs["a_gate_bias"], (P, 1))
    return blocks


def shape_constants():
    import numpy as np

    f = np.float32
    s, t = np.arange(P)[:, None], np.arange(P)[None, :]
    core = {
        "eps_rms": np.full((P, 1), RMS_EPS, f), "eps_ln": np.full((P, 1), LN_EPS, f),
        "eps_gn": np.full((P, 1), GN_EPS, f),
        "identity": np.eye(P, dtype=f), "ones": np.ones((P, P), f),
        "head_ones": (s // HD == t // HD).astype(f),
        "upto": (s <= t).astype(f),
        "causal_add": np.where(t <= s, 0, -1e30).astype(f),
    }
    return core


def dilated_tables():
    import math

    import numpy as np

    q = np.arange(P)[:, None]
    k2, k = np.arange(2 * P)[None, :], np.arange(P)[None, :]
    m0 = q + P - k2
    m1 = q - k
    m2 = q // 4 - k // 4
    ok2 = (m2 >= 0) & (q % 4 == k % 4)
    dist = np.concatenate([m0, 4 * m1, 16 * m2], 1)
    ok = np.concatenate([(m0 >= 0) & (m0 <= P), m1 >= 0, ok2], 1)
    dist = np.where(ok, dist, 0)
    d_f = np.maximum(dist, 1).astype(np.float32)
    large = 16 + (np.log(d_f / np.float32(16)) / np.float32(math.log(128)) * np.float32(16)).astype(np.int32)
    bucket = np.where(dist < 16, dist, np.minimum(large, 31))
    return bucket, np.where(ok, 0, -1e30).astype(np.float32)


def second_arrays(inputs):
    import numpy as np

    f = np.float32
    t = np.arange(S)
    inv_freq = f(10000.0) ** (-np.arange(16, dtype=f) / f(16))
    ang_r, ang_c = (t // 64).astype(f)[:, None] * inv_freq, (t % 64).astype(f)[:, None] * inv_freq
    ang = np.tile(np.concatenate([ang_r, ang_r, ang_c, ang_c], -1).T, (2, 1))
    turn = np.zeros((P, P), f)
    for m in range(P):
        turn[m + 16 if m % 32 < 16 else m - 16, m] = -1 if m % 32 < 16 else 1

    parity, c = np.arange(P)[:, None, None] // 64, np.arange(P)[:, None, None] % 64
    slot, kc = np.arange(16)[None, :, None], np.arange(64)[None, None, :]
    start = np.clip(c - 8, 0, 48)
    inside = (kc >= start) & (kc < start + 16)
    dr, dc = np.clip(slot - parity, 0, 14), np.where(inside, kc - c + 15, 0)
    window = inputs["na_rpb_2"][:, :, dr, dc].transpose(0, 2, 1, 3, 4)

    s, u = np.arange(P)[:, None], np.arange(P)[None, :]
    chunk = s // CH == u // CH
    before = [s < u, s > u]
    order = np.stack([np.stack([chunk & before[d], chunk & (before[d] | (s == u))]) for d in range(2)])
    pairs = np.stack([np.stack([(s // 2 == u // 2) & before[1 - d] for d in range(2)]),
                      np.stack([(s // 2 == u // 2) & before[d] for d in range(2)])])
    levels = np.stack([np.stack([(s // n == u // n) & (s // (n // 2) != u // (n // 2)) & before[d] for d in range(2)])
                       for n in LEVELS])
    flat = lambda m: np.ascontiguousarray(np.moveaxis(m, -2, 0).reshape(P, -1).astype(f))
    lora = np.concatenate([inputs["decay_w2_2"].reshape(2, 64, 384), inputs["iclr_a2_2"].reshape(2, 64, 384)], 1)
    return {
        "rope_cos": np.cos(ang).astype(f), "rope_sin": np.sin(ang).astype(f), "rope_turn": turn,
        "window_bias": np.ascontiguousarray(window.reshape(2, P, 4096)),
        "window_mask": np.where(inside[:, 0, :], 0, -1e30).astype(f),
        "reset": np.tile((np.arange(T2) % CH != 0).astype(f), (P, 1)),
        "order_masks": flat(order), "first_masks": -flat(pairs), "level_masks": flat(levels),
        "lora": np.ascontiguousarray(lora),
    }


def kernel(**inputs):
    import numpy as np
    import concourse.bacc as bacc
    from concourse.bass_utils import run_bass_kernel_spmd

    inputs = {name: np.asarray(a) for name, a in inputs.items()}
    plan = chunk_plan()
    weights = np.zeros((len(plan), P, CHUNK), np.float32)
    for i, (names, layer, cols, rows) in enumerate(plan):
        width = sum(n for part in cols for _, n in part)
        for k, row in enumerate(rows):
            to = 0
            for r, nr in row if isinstance(row, list) else [row]:
                at = k * width
                for name, part in zip(names, cols):
                    w = inputs[name] if layer is None else inputs[name][layer]
                    for c, n in part:
                        weights[i, to:to + nr, at:at + n] = w[r:r + nr, c:c + n]
                        at += n
                to += nr

    def joined(blocks):
        where, at = {}, 0
        for name, a in blocks.items():
            where[name] = (at, a.shape[1])
            at += a.shape[1]
        return where, np.ascontiguousarray(np.concatenate(list(blocks.values()), 1))

    def feature_major(a):
        n = a.shape[0]
        return np.ascontiguousarray(a.T.reshape(KT, P, n).transpose(1, 0, 2))

    cols_at, columns = joined(host_columns(inputs))
    consts_at, constants = joined(shape_constants())
    bucket, mask = dilated_tables()
    group_of = np.repeat(np.arange(3), [2 * P, P, P])
    bias = np.stack([inputs["rel_bias"][bucket, group_of[None, :] * 4 + h] for h in range(4)], 1)
    arrays = {
        "weights": weights, "columns": columns, "constants": constants,
        "x_T": feature_major(inputs["x"][0]), "mem_T": feature_major(inputs["mem"][0]).reshape(P, KT * M),
        "ctx_T": feature_major(inputs["ctx_2"][0]),
        "conditions": feature_major(np.stack([inputs["c_2"][0], inputs["c_ctx_2"]])).reshape(P, KT * 2),
        **second_arrays(inputs),
        "dilated_bias": np.ascontiguousarray(bias.reshape(P, 2048)), "dilated_mask": mask,
    }
    nc = bacc.Bacc("TRN2", target_bir_lowering=False, num_devices=1)
    dram = {n: nc.dram_tensor(n, a.shape, mybir.dt.float32, kind="ExternalInput").ap() for n, a in arrays.items()}
    out = nc.dram_tensor("out", (P, KT * S), mybir.dt.float32, kind="ExternalOutput").ap()
    build(nc, dram, out, cols_at, columns.shape[1], consts_at, constants.shape[1])
    r = run_bass_kernel_spmd(nc, [arrays], core_ids=[0])
    got = r.results[0]["out"].reshape(P, KT, S)
    return np.ascontiguousarray(got.transpose(2, 1, 0).reshape(1, S, D))
```

```python
from contextlib import ExitStack

import concourse.bass as bass
from concourse import mybir
from concourse.alu_op_type import AluOpType as ALU

F32 = mybir.dt.float32
F32R = mybir.dt.float32r
ACT = mybir.ActivationFunctionType
AX_X = mybir.AxisListType.X

P = 128
D = 1024
KT = D // P
S = 512
M = 256
CTX = 256
F = 2816
FT = F // P
HD = 64
SCALE = HD ** -0.5
RMS_EPS = 1e-6
LN_EPS = 1e-5
GN_EPS = 64e-5
ALPHA = 4 ** 0.25

ML_H, ML_D = 4, 192
RING = 2
PIECE = 1024
CHUNK = 2048
DOWN = FT // 2 * P
ARENA_AT = 16512
ARENA = 53200


class Core:

    def __init__(self, nc, ctx, dram, cols, consts, plan):
        self.nc, self.ctx, self.dram, self.plan = nc, ctx, dram, plan
        self.tensors = 0
        self.psum = ctx.enter_context(nc.psum_tensor("psum", [P, 8, 512], F32))
        self.top = 0
        self.sems, self.count, self.base = {}, {}, {}
        self.col_at, self.const_at = cols, consts
        self.used = 0
        self.issued = 0
        self.free_at = {}
        self.ring_at = self.top
        self.ring = self.alloc(RING, CHUNK)
        self.w_hi, self.w_lo = self.alloc_rounded(2, PIECE), self.alloc_rounded(2, PIECE)
        self.ring_end = self.top

    def alloc(self, *shape, dtype=F32):
        n = 1
        for size in shape:
            n *= size
        self.tensors += 1
        at = (self.top + 7) // 8 * 8
        self.top = at + n
        assert self.top <= ARENA, self.top
        return self.nc.alloc_sbuf_tensor_at(f"buffer_{self.tensors}", [P, *shape], dtype, offset=ARENA_AT + 4 * at)[:]

    def alloc_rounded(self, *shape):
        return self.alloc(*shape, dtype=F32R)

    def up(self, name, n=1):
        if name not in self.sems:
            self.sems[name] = self.ctx.enter_context(self.nc.semaphore(name))
            self.count[name] = 0
            self.base.setdefault(name, 0)
        self.count[name] += n
        return self.sems[name], n

    def at(self, name, i, step=1):
        if name not in self.sems:
            self.sems[name] = self.ctx.enter_context(self.nc.semaphore(name))
            self.count[name] = 0
            self.base[name] = 0
        assert i >= 0
        return self.sems[name], self.base.get(name, 0) + (i + 1) * step

    def now(self, name):
        return self.sems[name], self.count[name]

    def stage(self):
        self.base = dict(self.count)
        return self.nc.Block()

    def link(self, eng, ins, name):
        sem, n = self.up(name)
        ins.then_inc(sem, n)
        eng.wait_ge(sem, self.count[name])

    def const(self, name):
        a, n = self.const_at[name]
        return self.consts_sb[:, a:a + n]

    def col(self, name):
        a, n = self.col_at[name]
        return self.cols_sb[:, a:a + n]

    def take(self, n):
        first = self.used
        self.used += n
        return first

    def slot(self, c):
        return self.ring[:, c % RING, :]

    def landed(self, c):
        sem, n = self.up(f"chunk_landed_{c % RING}", 0)
        return sem, 16 * (c // RING + 1)

    def frees(self, c, name):
        self.free_at[c] = (self.sems[name], self.count[name])

    def stream(self, sp, ahead=RING):
        while self.issued < min(self.used + ahead, len(self.plan)):
            c = self.issued
            name, row, n = self.plan[c]
            if c - RING in self.free_at:
                sp.wait_ge(*self.free_at[c - RING])
            sp.dma_start(self.slot(c)[:, 0:n], self.dram[name][row, :, 0:n]).then_inc(
                *self.up(f"chunk_landed_{c % RING}", 16))
            self.issued += 1


class Split:

    def __init__(self, K, tiles, n):
        self.hi, self.lo = K.alloc_rounded(tiles, n), K.alloc_rounded(tiles, n)

    def pair(self, k, rows=P):
        return self.hi[0:rows, k, :], self.lo[0:rows, k, :]


class Feed:

    def __init__(self, K, tiles, **by_engine):
        self.K, self.tiles, self.by_engine = K, tiles, by_engine

    def run(self, name, eng):
        if name in self.by_engine:
            self.by_engine[name](eng)

    def ready(self, k):
        return self.K.at("lo_odd" if k % 2 else "lo_even", k // 2)


def feed_low(K, eng, k, lo, full, hi):
    eng.wait_ge(*K.at("tile_hi", k))
    eng.tensor_tensor(lo, full, hi.bitcast(F32), ALU.subtract).then_inc(*K.up("lo_odd" if k % 2 else "lo_even"))


def rms_norm(K, src, n, gain, dst):
    top = K.top
    sq, rstd, full = K.alloc(2, n), K.alloc(n), K.alloc(2, n)
    K.top = top
    total = K.psum[:, 0, 0:n]

    def act_part(act):
        for k in range(KT):
            if k >= 2:
                act.wait_ge(*K.at("square_summed", k - 2))
            act.activation(sq[:, k % 2, :], src[:, k, :], ACT.Square).then_inc(*K.up("square_ready"))
        act.wait_ge(*K.at("square_summed", KT - 1))
        act.activation(rstd, total, ACT.Sqrt, scale=1.0 / D, bias=K.const("eps_rms")).then_inc(*K.up("std_ready"))
        for k in range(KT):
            act.wait_ge(*K.at("normed", k))
            act.copy(dst.hi[:, k, :], full[:, k % 2, :]).then_inc(*K.up("tile_hi"))

    def pe_part(pe):
        for k in range(KT):
            pe.wait_ge(*K.at("square_ready", k))
            pe.matmul(total, K.const("ones"), sq[:, k % 2, :], start=k == 0,
                      stop=k == KT - 1).then_inc(*K.up("square_summed"))

    def low(eng, k):
        feed_low(K, eng, k, dst.lo[:, k, :], full[:, k % 2, :], dst.hi[:, k, :])

    def dve_part(dve):
        dve.wait_ge(*K.at("std_ready", 0))
        K.link(dve, dve.reciprocal(rstd, rstd), "dve_step")
        for k in range(KT):
            if k >= 2:
                dve.wait_ge(*K.at("lo_odd" if k % 2 else "lo_even", k // 2 - 1))
            dve.scalar_tensor_tensor(full[:, k % 2, :], src[:, k, :], gain[:, k:k + 1], rstd,
                                     ALU.mult, ALU.mult).then_inc(*K.up("normed"))
            if k % 2:
                low(dve, k - 1)

    def pool_part(pool):
        for k in range(1, KT, 2):
            low(pool, k)
    return Feed(K, KT, act=act_part, pe=pe_part, dve=dve_part, pool=pool_part)


def split_tiles(K, tiles, dst):
    def act_part(act):
        for k, x in enumerate(tiles):
            act.copy(dst.hi[0:x.shape[0], k, :], x).then_inc(*K.up("tile_hi"))

    def lows(first):
        def part(eng):
            for k in range(first, len(tiles), 2):
                rows = tiles[k].shape[0]
                feed_low(K, eng, k, dst.lo[0:rows, k, :], tiles[k], dst.hi[0:rows, k, :])
        return part
    return Feed(K, len(tiles), act=act_part, dve=lows(0), pool=lows(1))


def ffn(K, x_T, gain, spare):
    top = K.top
    h = Split(K, KT, S)
    feed = rms_norm(K, x_T, S, gain, h)
    hidden = Split(K, FT, S)
    gate, full = spare[:, 0:4, :], spare[:, 4:8, :]

    def gate_evacuation(f):
        def evacuate(K, eng, ps):
            if f >= 2:
                eng.wait_ge(*K.at("dve_evacuated", f - 2))
            b = 2 * (f % 2)
            return eng.activation(gate[:, b:b + 2, :], ps.rearrange("p (a b) -> p a b", a=2), ACT.Silu)
        return evacuate

    def hidden_evacuation(f):
        def evacuate(K, eng, ps):
            eng.wait_ge(*K.at("act_evacuated", f))
            if f >= 2:
                eng.wait_ge(*K.at("hidden_lo", f - 2))
            b = 2 * (f % 2)
            return eng.tensor_tensor(full[:, b:b + 2, :], gate[:, b:b + 2, :],
                                     ps.rearrange("p (a b) -> p a b", a=2), ALU.mult)
        return evacuate

    def split_hidden(f):
        b = 2 * (f % 2)
        halves = lambda x: x.rearrange("p (a b) -> p a b", a=2)

        def hi(act):
            act.wait_ge(*K.at("dve_evacuated", f))
            act.copy(halves(hidden.hi[:, f, :]), full[:, b:b + 2, :]).then_inc(*K.up("hidden_hi"))

        def lo(pool):
            pool.wait_ge(*K.at("hidden_hi", f))
            pool.tensor_tensor(halves(hidden.lo[:, f, :]), full[:, b:b + 2, :], halves(hidden.hi[:, f, :].bitcast(F32)),
                               ALU.subtract).then_inc(*K.up("hidden_lo"))
        return {"act": hi, "pool": lo}

    src = [h.pair(k) for k in range(KT)]
    jobs = []
    for f in range(FT):
        jobs.append(Job(f, 0, P, 256, src, S, "act", gate_evacuation(f)))
        jobs.append(Job(f, P, P, 256, src, S, "dve", hidden_evacuation(f)))
        jobs[-1].after = split_hidden(f)
    src = [hidden.pair(f) for f in range(FT)]
    for d in range(KT):
        jobs.append(Job(FT + 2 * d, 0, P, P, src, S, "dve", half_residual(x_T[:, d, :]), chunks=2))
        if d == 0:
            jobs[-1].needs = ("hidden_lo", FT - 1)
    project(K, jobs, FT + 2 * KT, feed)
    K.top = top


def half_residual(x):
    def evacuate(K, eng, ps):
        return eng.scalar_tensor_tensor(x, ps, 0.5, x, ALU.mult, ALU.add)
    return evacuate


class Job:

    def __init__(self, chunk, c0, cn, width, src, n, engine, evacuate, tokens=None, chunks=1):
        self.chunk, self.c0, self.cn, self.width, self.chunks = chunk, c0, cn, width, chunks
        self.src, self.n, self.engine, self.evacuate, self.tokens = src, n, engine, evacuate, tokens
        self.after, self.needs = {}, None


def copy_to(out):
    def evacuate(K, eng, ps):
        if eng is K.nc.scalar:
            return eng.copy(out, ps)
        return eng.tensor_copy(out, ps)
    return evacuate


def act_to(out, func):
    def evacuate(K, eng, ps):
        return eng.activation(out, ps, func)
    return evacuate


def cut_pieces(jobs):
    pieces, of_job = [], []
    for j, job in enumerate(jobs):
        prior = jobs[j - 1] if j else None
        if prior and (prior.chunk, prior.c0, prior.cn) == (job.chunk, job.c0, job.cn):
            of_job.append(of_job[-1])
            continue
        mine = []
        per = len(job.src) // job.chunks
        most = min(per, PIECE // job.cn)
        parts = -(-per // most)
        for c in range(job.chunks):
            for i in range(parts):
                a, b = per * i // parts, per * (i + 1) // parts
                mine.append(len(pieces))
                pieces.append((job.chunk + c, a, b - a, c * per + a, job.c0, job.cn, job.width,
                               [x.shape[0] for x, _ in job.src[c * per + a:c * per + b]]))
        of_job.append(mine)
    return pieces, of_job


def project(K, jobs, n_chunks, feed, ahead=RING):
    c0 = K.take(n_chunks)
    pieces, of_job = cut_pieces(jobs)
    order = {"act": [j for j, job in enumerate(jobs) if job.engine == "act"],
             "dve": [j for j, job in enumerate(jobs) if job.engine == "dve"]}
    last_user = {p: j for j, mine in enumerate(of_job) for p in mine}
    released, ended = {}, 0
    for p in range(len(pieces)):
        j = last_user[p]
        if of_job[j][-1] == p or jobs[j].tokens is not None:
            released[p] = ("product_ready", j)
        else:
            released[p] = ("piece_ended", ended)
            ended += 1

    def shape_of(p):
        _, _, tiles, _, _, cn, _, _ = pieces[p]
        return lambda x: x[:, p % 2, 0:tiles * cn].rearrange("p (k n) -> p k n", k=tiles)

    def raw(p):
        chunk, first, tiles, _, at, cn, width, _ = pieces[p]
        return K.slot(c0 + chunk)[:, first * width:(first + tiles) * width].rearrange(
            "p (k n) -> p k n", k=tiles)[:, :, at:at + cn]

    with K.stage() as block:
        @block.tensor
        def _(pe):
            feed.run("pe", pe)
            for j, job in enumerate(jobs):
                if j >= 4:
                    e = jobs[j - 4].engine
                    pe.wait_ge(*K.at(f"{e}_evacuated", order[e].index(j - 4)))
                if job.needs:
                    pe.wait_ge(*K.at(*job.needs))
                ps = K.psum[:, 2 * (j % 4):2 * (j % 4) + 2, :].rearrange("p a b -> p (a b)")
                for p in of_job[j]:
                    _, _, tiles, k0, _, cn, _, rows_of = pieces[p]
                    pe.wait_ge(*K.at("piece_ready", p))
                    w_hi, w_lo = shape_of(p)(K.w_hi), shape_of(p)(K.w_lo)
                    for k in range(tiles):
                        rows = rows_of[k]
                        if j == 0:
                            pe.wait_ge(*feed.ready(k0 + k))
                        hi, lo = job.src[k0 + k]
                        for i, (w, x) in enumerate(((w_hi, hi), (w_hi, lo), (w_lo, hi))):
                            flags = dict(start=k0 + k == 0 and i == 0, stop=k0 + k == len(job.src) - 1 and i == 2)
                            if job.tokens is not None:
                                mm = pe.matmul(ps[0:P, 0:cn], job.tokens(x), w[0:rows, k, :], **flags)
                            else:
                                for a in range(0, job.n, 512):
                                    b = min(job.n, a + 512)
                                    mm = pe.matmul(ps[0:cn, a:b], w[0:rows, k, :], x[:, a:b], **flags)
                    if last_user[p] == j and released[p][0] == "piece_ended":
                        mm.then_inc(*K.up("piece_ended"))
                mm.then_inc(*K.up("product_ready"))

        def program(eng, name, split):
            done = min(2, len(pieces))
            for p in range(done):
                split(p)
            feed.run(name, eng)
            for j, job in enumerate(jobs):
                after_it = of_job[min(j + 1, len(jobs) - 1)]
                until = max(of_job[j][-1] + 1, min(after_it[-1] + 1, of_job[j][-1] + 3))
                for p in range(done, until):
                    split(p)
                done = max(done, until)
                if job.engine == name:
                    rows, n = (P, job.cn) if job.tokens is not None else (job.cn, job.n)
                    ps = K.psum[:, 2 * (j % 4):2 * (j % 4) + 2, :].rearrange("p a b -> p (a b)")[0:rows, 0:n]
                    eng.wait_ge(*K.at("product_ready", j))
                    job.evacuate(K, eng, ps).then_inc(*K.up(f"{name}_evacuated"))
                if name in job.after:
                    job.after[name](eng)

        @block.scalar
        def _(act):
            def round_hi(p):
                rows = max(pieces[p][7])
                act.wait_ge(*K.landed(c0 + pieces[p][0]))
                if p >= 2:
                    act.wait_ge(*K.at(*released[p - 2]))
                act.copy(shape_of(p)(K.w_hi), raw(p)).then_inc(*K.up("hi_ready"))
            program(act, "act", round_hi)

        @block.vector
        def _(dve):
            def subtract_lo(p):
                dve.wait_ge(*K.landed(c0 + pieces[p][0]))
                dve.wait_ge(*K.at("hi_ready", p))
                dve.tensor_tensor(shape_of(p)(K.w_lo), raw(p), shape_of(p)(K.w_hi).bitcast(F32),
                                  ALU.subtract).then_inc(*K.up("piece_ready"))
                K.frees(c0 + pieces[p][0], "piece_ready")
            program(dve, "dve", subtract_lo)

        @block.gpsimd
        def _(pool):
            feed.run("pool", pool)
            for job in jobs:
                if "pool" in job.after:
                    job.after["pool"](pool)

        @block.sync
        def _(sp):
            K.stream(sp, ahead)


class Modulation:

    def __init__(self, K, layer, cond, mod, first, count, slots):
        self.K, self.cond, self.mod, self.first = K, cond, mod, first
        self.bias = K.col(f"b_mod{layer}")
        self.c0 = K.take(count)
        self.sums = K.alloc(2, 2, 256)
        work = []
        for i in range(count):
            work += [("step", i, k) for k in range(KT)] + [("end", i, 0)]
        self.slots = [work[len(work) * u // slots:len(work) * (u + 1) // slots] for u in range(slots)]

    def ends(self, u):
        return [i for what, i, _ in self.slots[u] if what == "end"] if 0 <= u < len(self.slots) else []

    def sum_up(self, dve, u):
        K = self.K
        for what, i, k in self.slots[u] if 0 <= u < len(self.slots) else []:
            if what == "end":
                continue
            w = K.slot(self.c0 + i).rearrange("p (k n) -> p k n", k=KT)[:, k, :]
            if k == 0:
                dve.wait_ge(*K.landed(self.c0 + i))
                if i >= 2:
                    dve.wait_ge(*K.at("mod_product", i - 2))
            for which in range(2):
                total, c = self.sums[:, i % 2, which, :], self.cond[:, k, which:which + 1]
                if k == 0:
                    ins = dve.tensor_scalar(total, w, c, None, ALU.mult)
                else:
                    dve.wait_ge(*K.at("mod_step", 2 * (KT * i + k - 1) + which))
                    ins = dve.scalar_tensor_tensor(total, w, c, total, ALU.mult, ALU.add)
                ins.then_inc(*K.up("mod_step"))
            if k == KT - 1:
                K.frees(self.c0 + i, "mod_step")

    def product(self, pe, i):
        K = self.K
        pe.wait_ge(*K.at("mod_step", 2 * KT * (i + 1) - 1))
        for half in range(2):
            for which in range(2):
                mm = pe.matmul(K.psum[:, 5, 2 * half + which:2 * half + which + 1],
                               self.sums[:, i % 2, which, half * P:(half + 1) * P], K.const("ones")[:, 0:1],
                               start=True, stop=True)
        mm.then_inc(*K.up("mod_product"))

    def add_bias(self, dve, i):
        K = self.K
        dve.wait_ge(*K.at("mod_product", i))
        for half in range(2):
            tile = 2 * (self.first + i) + half
            one = 1.0 if KT <= tile < 2 * KT else 0.0
            ins = dve.tensor_scalar(self.mod[:, tile, :], K.psum[:, 5, 2 * half:2 * half + 2],
                                    self.bias[:, tile:tile + 1], one, ALU.add, ALU.add)
        ins.then_inc(*K.up("mod_biased"))


def head_norm(K, tiles):
    top = K.top
    sq, rstd = K.alloc(2, 1024), K.alloc(2, 1024)
    with K.stage() as block:
        @block.scalar
        def _(act):
            for i in range(len(tiles) + 1):
                if i < len(tiles):
                    if i >= 2:
                        act.wait_ge(*K.at("square_summed", i - 2))
                    x, _ = tiles[i]
                    act.activation(sq[:, i % 2, 0:x.shape[1]], x, ACT.Square).then_inc(*K.up("square_ready"))
                if i >= 1:
                    u, n = i - 1, tiles[i - 1][0].shape[1]
                    act.wait_ge(*K.at("square_summed", u))
                    if u >= 2:
                        act.wait_ge(*K.at("head_normed", u - 2))
                    ps = K.psum[:, 2 * (u % 2):2 * (u % 2) + 2, :].rearrange("p a b -> p (a b)")
                    act.activation(rstd[:, u % 2, 0:n], ps[:, 0:n], ACT.Sqrt, scale=1.0 / HD,
                                   bias=K.const("eps_rms")).then_inc(*K.up("std_ready"))

        @block.tensor
        def _(pe):
            for i, (x, _) in enumerate(tiles):
                n = x.shape[1]
                pe.wait_ge(*K.at("square_ready", i))
                if i >= 2:
                    pe.wait_ge(*K.at("std_ready", i - 2))
                ps = K.psum[:, 2 * (i % 2):2 * (i % 2) + 2, :].rearrange("p a b -> p (a b)")
                for a in range(0, n, 512):
                    b = min(n, a + 512)
                    mm = pe.matmul(ps[:, a:b], K.const("head_ones"), sq[:, i % 2, a:b], start=True, stop=True)
                mm.then_inc(*K.up("square_summed"))

        @block.vector
        def _(dve):
            for i, (x, gain) in enumerate(tiles):
                n = x.shape[1]
                dve.wait_ge(*K.at("std_ready", i))
                K.link(dve, dve.reciprocal(rstd[:, i % 2, 0:n], rstd[:, i % 2, 0:n]), "dve_step")
                dve.scalar_tensor_tensor(x, x, gain, rstd[:, i % 2, 0:n], ALU.mult, ALU.mult).then_inc(*K.up("head_normed"))
    K.top = top


def block_of(t):
    return lambda x: x[:, t * P:(t + 1) * P]


def as_shape(x, like):
    if len(like.shape) == 2:
        return x
    return x.rearrange("p (a b) -> p a b", a=like.shape[1])


class Unit:

    def __init__(self, half, q, keys, values, out, bias=None, lse=None):
        self.half, self.q, self.keys, self.values = half, q, keys, values
        self.out, self.bias, self.lse = out, bias, lse
        self.n = P * len(values)


def attention(K, units, beside=None, ahead=RING):
    top = K.top
    width = max(u.n for u in units)
    probs, probs_T = K.alloc(2, width), K.alloc(2, width)
    scored, diagonal = K.alloc(2, width), K.alloc(2, P)
    peak, bound, total, inverse = (K.alloc(len(units)) for _ in range(4))

    def scores_ps(u):
        return K.psum[:, 2 * (u % 2):2 * (u % 2) + 2, :].rearrange("p a b -> p (a b)")
    turned_ps = K.psum[:, 4:6, :].rearrange("p a b -> p (a b)")

    def due(u):
        return beside.ends(u) if beside else []

    with K.stage() as block:
        @block.tensor
        def _(pe):
            def scores(u):
                unit = units[u]
                n = unit.n
                rows = slice(64 * unit.half, 64 * unit.half + 64)
                if u >= 2:
                    pe.wait_ge(*K.at("probs_ready", u - 2))
                if n <= 512:
                    mm = pe.matmul(scores_ps(u)[:, 0:n], unit.q, unit.keys, start=True, stop=True)
                else:
                    for a in range(0, n, 512):
                        b = min(n, a + 512)
                        mm = pe.matmul(scores_ps(u)[:, a:b], unit.q, unit.keys[:, a:b], start=True, stop=True)
                mm.then_inc(*K.up("scores_ready"))

            def turn(u):
                pe.wait_ge(*K.at("diagonal_ready", u))
                if due(u - 1):
                    pe.wait_ge(*K.at("mod_biased", due(u - 1)[-1]))
                if u >= 1:
                    pe.wait_ge(*K.at("turned_copied", u - 1))
                for b in range(len(units[u].values)):
                    mm = pe.matmul(turned_ps[:, b * P:(b + 1) * P], probs[:, u % 2, b * P:(b + 1) * P],
                                   diagonal[:, u % 2, :], start=True, stop=True)
                mm.then_inc(*K.up("turned_ready"))

            def output(u):
                unit = units[u]
                blocks = len(unit.values)
                pe.wait_ge(*K.at("turned_copied", u))
                if u >= 2:
                    pe.wait_ge(*K.at("output_copied", u - 2))
                for b in range(blocks):
                    mm = pe.matmul(K.psum[:, 6 + u % 2, 0:P], unit.values[b], probs_T[:, u % 2, b * P:(b + 1) * P],
                                   start=b == 0, stop=b == blocks - 1)
                mm.then_inc(*K.up("output_ready"))

            for u in range(-2, len(units) + 1):
                if u + 2 < len(units):
                    scores(u + 2)
                if 0 <= u < len(units):
                    turn(u)
                if u >= 1:
                    output(u - 1)
                if due(u):
                    pe.wait_ge(*K.at("turned_copied", u))
                    for i in due(u):
                        beside.product(pe, i)

        @block.vector
        def _(dve):
            def find_peak(u):
                unit = units[u]
                n = unit.n
                dve.wait_ge(*K.at("scores_ready", u))
                source = scores_ps(u)[:, 0:n]
                factor = -SCALE
                if unit.bias is not None:
                    dve_in = source
                    source = scored[:, u % 2, 0:n]
                    if u >= 2:
                        dve.wait_ge(*K.at("probs_ready", u - 2))
                    free = n - unit.bias.shape[1]
                    if free:
                        dve.tensor_scalar(source[:, 0:free], dve_in[:, 0:free], SCALE, None, ALU.mult)
                    K.link(dve, dve.scalar_tensor_tensor(source[:, free:n], dve_in[:, free:n], SCALE, unit.bias,
                                                         ALU.mult, ALU.add), "dve_step")
                    factor = -1.0
                K.link(dve, dve.tensor_reduce(peak[:, u:u + 1], source, AX_X, ALU.max), "dve_step")
                dve.tensor_scalar(bound[:, u:u + 1], peak[:, u:u + 1], factor, None,
                                  ALU.mult).then_inc(*K.up("bound_ready"))

            def invert(u):
                dve.wait_ge(*K.at("probs_ready", u))
                dve.reciprocal(inverse[:, u:u + 1], total[:, u:u + 1]).then_inc(*K.up("inverse_ready"))

            def copy_out(u):
                unit = units[u]
                rows = slice(64 * unit.half, 64 * unit.half + 64)
                dve.wait_ge(*K.at("output_ready", u))
                dve.tensor_copy(unit.out, as_shape(K.psum[rows, 6 + u % 2, 0:P], unit.out)).then_inc(*K.up("output_copied"))

            for u in range(-2, len(units) + 2):
                if 0 <= u + 1 < len(units):
                    invert(u + 1)
                for i in due(u - 1):
                    beside.add_bias(dve, i)
                if u + 2 < len(units):
                    find_peak(u + 2)
                if u >= 2:
                    copy_out(u - 2)
                if beside:
                    beside.sum_up(dve, u)

        @block.scalar
        def _(act):
            def exponentials(u):
                unit = units[u]
                n = unit.n
                act.wait_ge(*K.at("bound_ready", u))
                if u >= 2:
                    act.wait_ge(*K.at("turned_ready", u - 2))
                source, scale = (scores_ps(u)[:, 0:n], SCALE) if unit.bias is None else (scored[:, u % 2, 0:n], 1.0)
                act.activation(probs[:, u % 2, 0:n], source, ACT.Exp, scale=scale, bias=bound[:, u:u + 1],
                               accum_out=total[:, u:u + 1]).then_inc(*K.up("probs_ready"))

            def turn(u):
                n = units[u].n
                act.wait_ge(*K.at("turned_ready", u))
                if u >= 2:
                    act.wait_ge(*K.at("output_ready", u - 2))
                act.copy(probs_T[:, u % 2, 0:n], turned_ps[:, 0:n]).then_inc(*K.up("turned_copied"))

            for u in range(-1, len(units)):
                if u + 1 < len(units):
                    exponentials(u + 1)
                if u >= 0:
                    turn(u)

        @block.gpsimd
        def _(pool):
            for u in range(len(units)):
                pool.wait_ge(*K.at("inverse_ready", u))
                if u >= 2:
                    pool.wait_ge(*K.at("turned_ready", u - 2))
                pool.tensor_scalar(diagonal[:, u % 2, :], K.const("identity"), inverse[:, u:u + 1], None,
                                   ALU.mult).then_inc(*K.up("diagonal_ready"))

        @block.sync
        def _(sp):
            if beside:
                K.stream(sp, ahead)
    if units[0].lse is not None:
        logs = K.alloc(len(units))
        with K.stage() as block:
            @block.scalar
            def _(act):
                act.activation(logs[:, :], total[:, :], ACT.Ln).then_inc(*K.up("log_ready"))

            @block.vector
            def _(dve):
                dve.wait_ge(*K.at("log_ready", 0))
                dve.tensor_tensor(units[0].lse, logs[:, :], bound[:, :], ALU.subtract)
    K.top = top


def memory_attention(K, layer, q_mem, cond, mod, first):
    top = K.top
    mem_T = K.alloc(KT, M)
    load(K, [(mem_T.rearrange("p a b -> p (a b)"), K.dram["mem_T"])])
    mem_n = Split(K, KT, M)
    feed = rms_norm(K, mem_T, M, K.col(f"mem_norm{layer}"), mem_n)
    k_T, v = K.alloc(2, M), K.alloc(2, 256)
    src = [mem_n.pair(k) for k in range(KT)]
    jobs = [Job(0, P * i, P, 256, src, M, "act" if i else "dve", copy_to(k_T[:, i, :])) for i in range(2)]
    jobs += [Job(1, 0, 256, 256, src, M, "act" if t else "dve", copy_to(v[:, t, :]), tokens=block_of(t))
             for t in range(2)]
    project(K, jobs, 2, feed)
    head_norm(K, [(k_T[:, i, :], K.col(f"mem_k_norm{layer}")) for i in range(2)]
              + [(q, K.col(f"mem_q_norm{layer}")) for q in q_mem])
    units = []
    for t in range(S // P):
        for pair in range(2):
            for half in range(2):
                rows = slice(64 * half, 64 * half + 64)
                q = q_mem[pair][rows, t * P:(t + 1) * P]
                units.append(Unit(half, q, k_T[rows, pair, :],
                                  [v[:, b, pair * P:(pair + 1) * P] for b in range(2)], q))
    attention(K, units, Modulation(K, 0, cond, mod, first, 2, len(units) - 1))
    K.top = top


def conv_evacuation(out, taps):
    def evacuate(K, eng, ps):
        n = ps.shape[1]
        K.link(eng, eng.tensor_scalar(out, ps, taps[:, 3:4], None, ALU.mult), "dve_step")
        for shift in (1, 2, 3):
            ins = eng.scalar_tensor_tensor(out[:, shift:n], ps[:, 0:n - shift], taps[:, 3 - shift:4 - shift],
                                           out[:, shift:n], ALU.mult, ALU.add)
            if shift < 3:
                K.link(eng, ins, "dve_step")
        return ins
    return evacuate


def add_to(out, row):
    def evacuate(K, eng, ps):
        return eng.tensor_tensor(out, ps, row, ALU.add)
    return evacuate


def residual(x, factor=None):
    def evacuate(K, eng, ps):
        return eng.tensor_tensor(x, ps, x, ALU.add)
    return evacuate


def values_evacuation(v1, t, at):
    def evacuate(K, eng, ps):
        copy = eng.copy if eng is K.nc.scalar else eng.tensor_copy
        while_at = at
        while while_at < at + 256:
            hd, c = while_at // ML_D, while_at % ML_D
            n = min(ML_D - c, at + 256 - while_at)
            ins = copy(v1[:, t, hd, c:c + n], ps[:, while_at - at:while_at - at + n])
            while_at += n
        return ins
    return evacuate


def mlstm_gates(K, gates):
    H, N = ML_H, (S // P) * ML_H
    tiny = lambda: K.alloc(S // P, H)
    b, c, tot, cmax, upto, m0, m1, u, neg_u, inter, wgt, decay, floor, tmp = (tiny() for _ in range(14))
    flat = lambda x: x.rearrange("p a b -> p (a b)")
    masked = K.alloc(N, P)
    top = K.top
    size, soft, logf = tiny(), tiny(), tiny()
    f = gates[:, :, H:2 * H]
    with K.stage() as block:
        @block.vector
        def _(dve):
            dve.scalar_tensor_tensor(size, f, -1.0, f, ALU.mult, ALU.max).then_inc(*K.up("size_ready"))
            dve.wait_ge(*K.at("softplus_ready", 1))
            K.link(dve, dve.tensor_scalar(logf, f, 0.0, None, ALU.min), "dve_step")
            dve.tensor_tensor(logf, logf, soft, ALU.subtract).then_inc(*K.up("logf_ready"))
            dve.wait_ge(*K.at("sums_ready", 0))
            dve.tensor_copy(flat(b), K.psum[:, 0, 0:N])
            K.link(dve, dve.tensor_copy(flat(tot), K.psum[:, 1, 0:N]), "dve_step")
            dve.tensor_tensor(c, gates[:, :, 0:H], b, ALU.subtract).then_inc(*K.up("c_ready"))
            for q in range(4):
                dve.wait_ge(*K.at("c_spread", q))
                rows = K.psum[:, 2 + q, :].rearrange("p (a b) -> p a b", a=4)
                mask = K.const("causal_add").rearrange("p (a b) -> p a b", a=1).to_broadcast([P, 4, P])
                dve.tensor_reduce(cmax[:, q, :], rows, AX_X, ALU.max)
                K.link(dve, dve.tensor_tensor(masked[:, 4 * q:4 * q + 4, :], rows, mask, ALU.add), "dve_step")
                dve.tensor_reduce(upto[:, q, :], masked[:, 4 * q:4 * q + 4, :], AX_X, ALU.max)
            K.link(dve, dve.memset(m0[:, 0, :], 0.0), "dve_step")
            for q in range(S // P):
                K.link(dve, dve.tensor_tensor(m1[:, q, :], m0[:, q, :], cmax[:, q, :], ALU.max), "dve_step")
                if q + 1 < S // P:
                    K.link(dve, dve.tensor_tensor(m0[:, q + 1, :], m1[:, q, :], tot[:, q, :], ALU.add), "dve_step")
            K.link(dve, dve.tensor_tensor(u, m0, upto, ALU.max), "dve_step")
            dve.tensor_scalar(neg_u, u, -1.0, None, ALU.mult)
            dve.tensor_tensor(inter, m0, u, ALU.subtract)
            dve.tensor_tensor(wgt, c, m1, ALU.subtract)
            dve.tensor_tensor(decay, m0, m1, ALU.subtract)
            dve.tensor_tensor(floor, b, u, ALU.add).then_inc(*K.up("exponents_ready"))

        @block.scalar
        def _(act):
            act.wait_ge(*K.at("size_ready", 0))
            act.activation(soft, size, ACT.Exp, scale=-1.0).then_inc(*K.up("softplus_ready"))
            act.wait_ge(*K.at("softplus_ready", 0))
            act.activation(soft, soft, ACT.Ln, bias=1.0).then_inc(*K.up("softplus_ready"))
            act.wait_ge(*K.at("exponents_ready", 0))
            for x in (inter, wgt, decay):
                act.activation(x, x, ACT.Exp)
            act.activation(floor, floor, ACT.Exp, scale=-1.0)
            for j in range(N):
                act.activation(masked[:, j, :], masked[:, j, :], ACT.Exp, bias=flat(neg_u)[:, j:j + 1])

        @block.tensor
        def _(pe):
            pe.wait_ge(*K.at("logf_ready", 0))
            pe.matmul(K.psum[:, 0, 0:N], K.const("upto"), flat(logf), start=True, stop=True)
            pe.matmul(K.psum[:, 1, 0:N], K.const("ones"), flat(logf), start=True, stop=True
                      ).then_inc(*K.up("sums_ready"))
            pe.wait_ge(*K.at("c_ready", 0))
            for j in range(N):
                mm = pe.matmul(K.psum[:, 2 + j // 4, (j % 4) * P:(j % 4 + 1) * P],
                               flat(c)[:, j:j + 1].to_broadcast([P, P]), K.const("identity"), start=True, stop=True)
                if j % 4 == 3:
                    mm.then_inc(*K.up("c_spread"))
    K.top = top
    return masked, inter, wgt, decay, floor


def mlstm_cell(K, q_T, k_T, v1, o_T, gates, h_gain, h_aT):
    top = K.top
    H, C = ML_H, S // P
    weight, inter, wgt, decay, floor = mlstm_gates(K, gates)
    k_tok = K.alloc(2, H, 2, 96)
    memory = K.alloc(H, 2, 193)
    w, w_T = K.alloc(2, H, P), K.alloc(2, H, P)
    num = K.alloc(H, 193)
    square = K.alloc(192)
    den, ss = K.alloc(H), K.alloc(2, H)
    h = K.alloc(2, H, 192)
    bank = lambda i: K.psum[:, i, :]
    s_ps = bank(0).rearrange("p (h t) -> p h t", h=H)
    wt_ps = bank(1).rearrange("p (h t) -> p h t", h=H)
    local_ps = lambda hd: K.psum[:, 2 + hd // 2, (hd % 2) * 193:(hd % 2) * 193 + 193]
    carried_ps = lambda hd: K.psum[:, 4 + hd // 2, (hd % 2) * 193:(hd % 2) * 193 + 193]
    update_ps = lambda hd: K.psum[0:96, 6 + hd % 2, 0:386].rearrange("p (a b) -> p a b", a=2)
    pair_ps = lambda base, g: K.psum[:, base + g, 0:386].rearrange("p (a b) -> p a b", a=2)
    with K.stage() as block:
        @block.tensor
        def _(pe):
            for c in range(C):
                tok = slice(c * P, (c + 1) * P)
                if c >= 1:
                    pe.wait_ge(*K.at("h_gated", c - 1))
                for hd in range(H):
                    for part in range(2):
                        mm = pe.matmul(s_ps[:, hd, :], q_T[0:96, 2 * hd + part, tok], k_T[0:96, 2 * hd + part, tok],
                                       start=part == 0, stop=part == 1)
                mm.then_inc(*K.up("qk_ready"))
                for hd in range(H):
                    if c >= 1:
                        pe.wait_ge(*K.at("memory_updated", 4 * c - 1))
                    for part in range(2):
                        mm = pe.transpose(K.psum[:, 6 + hd // 2, (2 * (hd % 2) + part) * 96:(2 * (hd % 2) + part) * 96 + 96],
                                          k_T[0:96, 2 * hd + part, tok], K.const("identity")[0:96, 0:96])
                mm.then_inc(*K.up("k_turned"))
                pe.wait_ge(*K.at("w_ready", c))
                for hd in range(H):
                    mm = pe.transpose(wt_ps[:, hd, :], w[:, c % 2, hd, :], K.const("identity"))
                mm.then_inc(*K.up("w_turned"))
                if c >= 1:
                    pe.wait_ge(*K.at("memory_updated", 4 * c - 1))
                else:
                    pe.wait_ge(*K.at("memory_cleared", 0))
                for hd in range(H):
                    for part in range(2):
                        mm = pe.matmul(carried_ps(hd), q_T[0:96, 2 * hd + part, tok], memory[0:96, hd, part, :],
                                       start=part == 0, stop=part == 1)
                mm.then_inc(*K.up("carried_ready"))
                pe.wait_ge(*K.at("w_T_ready", c))
                for hd in range(H):
                    mm = pe.matmul(local_ps(hd), w_T[:, c % 2, hd, :], v1[:, c, hd, :], start=True, stop=True)
                mm.then_inc(*K.up("local_ready"))
                pe.wait_ge(*K.at("k_copied", c))
                for hd in range(H):
                    if hd >= 2:
                        pe.wait_ge(*K.at("memory_updated", 4 * c + hd - 2))
                    for part in range(2):
                        mm = pe.matmul(update_ps(hd)[:, part, :], k_tok[:, c % 2, hd, part, :], v1[:, c, hd, :],
                                       start=True, stop=True)
                    mm.then_inc(*K.up("update_ready"))
                pe.wait_ge(*K.at("h_ready", c))
                for hd in range(H):
                    for part in range(2):
                        mm = pe.transpose(K.psum[0:96, hd // 2, (2 * (hd % 2) + part) * P:(2 * (hd % 2) + part) * P + P],
                                          h[:, c % 2, hd, part * 96:(part + 1) * 96], K.const("identity"))
                mm.then_inc(*K.up("h_turned"))

        @block.vector
        def _(dve):
            dve.memset(memory[:, :, :, :], 0.0).then_inc(*K.up("memory_cleared"))
            dve.wait_ge(*K.at("memory_cleared", 0))
            for c in range(C):
                tok = slice(c * P, (c + 1) * P)
                dve.wait_ge(*K.at("qk_ready", c))
                dve.scalar_tensor_tensor(w[:, c % 2, :, :], s_ps, ML_D ** -0.5, weight[:, 4 * c:4 * c + 4, :],
                                         ALU.mult, ALU.mult).then_inc(*K.up("w_ready"))
                dve.wait_ge(*K.at("k_turned", c))
                for hd in range(H):
                    out = k_tok[:, c % 2, hd, :, :].rearrange("p a b -> p (a b)")
                    ins = dve.tensor_scalar(out, K.psum[:, 6 + hd // 2, (hd % 2) * 192:(hd % 2) * 192 + 192],
                                            wgt[:, c, hd:hd + 1], ML_D ** -0.5, ALU.mult, ALU.mult)
                ins.then_inc(*K.up("k_copied"))
                dve.wait_ge(*K.at("local_ready", c))
                dve.wait_ge(*K.at("carried_scaled", c))
                for g in range(2):
                    ins = dve.tensor_tensor(num[:, 2 * g:2 * g + 2, :], num[:, 2 * g:2 * g + 2, :], pair_ps(2, g), ALU.add)
                K.link(dve, ins, "dve_step")
                last = num[:, :, 192]
                K.link(dve, dve.scalar_tensor_tensor(den, last, -1.0, last, ALU.mult, ALU.max), "dve_step")
                K.link(dve, dve.tensor_tensor(den, den, floor[:, c, :], ALU.max), "dve_step")
                K.link(dve, dve.reciprocal(den, den), "dve_step")
                for hd in range(H):
                    ins = dve.tensor_scalar(h[:, c % 2, hd, :], num[:, hd, 0:192], den[:, hd:hd + 1], None, ALU.mult)
                ins.then_inc(*K.up("h_raw"))
                for hd in range(H):
                    dve.wait_ge(*K.at("update_ready", 4 * c + hd))
                    dve.scalar_tensor_tensor(memory[0:96, hd, :, :], memory[0:96, hd, :, :], decay[0:96, c, hd:hd + 1],
                                             update_ps(hd), ALU.mult, ALU.add).then_inc(*K.up("memory_updated"))
                dve.wait_ge(*K.at("h_deviation", c))
                K.link(dve, dve.reciprocal(ss[:, 1, :], ss[:, 1, :]), "dve_step")
                for hd in range(H):
                    ins = dve.tensor_scalar(h[:, c % 2, hd, :], h[:, c % 2, hd, :], ss[:, 1, hd:hd + 1], None, ALU.mult)
                ins.then_inc(*K.up("h_ready"))
                dve.wait_ge(*K.at("h_turned", c))
                for j in range(8):
                    ins = dve.scalar_tensor_tensor(h_aT[0:96, j, tok], K.psum[0:96, j // 4, (j % 4) * P:(j % 4 + 1) * P],
                                                   h_gain[0:96, j:j + 1], o_T[0:96, j, tok], ALU.mult, ALU.mult)
                ins.then_inc(*K.up("h_gated"))

        @block.scalar
        def _(act):
            for c in range(C):
                act.wait_ge(*K.at("w_turned", c))
                act.copy(w_T[:, c % 2, :, :], wt_ps).then_inc(*K.up("w_T_ready"))
                act.wait_ge(*K.at("carried_ready", c))
                if c >= 1:
                    act.wait_ge(*K.at("h_raw", c - 1))
                for hd in range(H):
                    ins = act.mul(num[:, hd, :], carried_ps(hd), inter[:, c, hd:hd + 1])
                ins.then_inc(*K.up("carried_scaled"))
                act.wait_ge(*K.at("h_raw", c))
                if c >= 1:
                    act.wait_ge(*K.at("h_ready", c - 1))
                for hd in range(H):
                    ins = act.activation(square, h[:, c % 2, hd, :], ACT.Square, accum_out=ss[:, 0, hd:hd + 1])
                    ins.then_inc(*K.up("h_squares"))
                    act.wait_ge(*K.at("h_squares", 4 * c + hd))
                act.activation(ss[:, 1, :], ss[:, 0, :], ACT.Sqrt, scale=1.0 / ML_D,
                               bias=K.const("eps_rms")).then_inc(*K.up("h_deviation"))
    K.top = top


def mlstm_layer(K, x_T, cond, mod):
    top = K.top
    qk_T, o_T = K.alloc(16, S), K.alloc(8, S)
    v1 = K.alloc(S // P, ML_H, 193)
    q_mem = K.alloc(2, S)
    gates = K.alloc(S // P, 2 * ML_H)
    h_aT = K.alloc(8, S)
    inner = K.top
    h = Split(K, KT, S)
    feed = rms_norm(K, x_T, S, K.col("mix_norm0"), h)
    src = [h.pair(k) for k in range(KT)]
    taps = K.col("a_conv")
    jobs = []
    for j in range(16):
        jobs.append(Job(j // 2, 96 * (j % 2), 96, 192, src, S, "dve",
                        conv_evacuation(qk_T[0:96, j, :], taps[0:96, 4 * j:4 * j + 4])))
    for j in range(8):
        jobs.append(Job(8 + j // 2, 96 * (j % 2), 96, 192, src, S, "act", act_to(o_T[0:96, j, :], ACT.Sigmoid)))
    for i in range(3):
        for t in range(S // P):
            jobs.append(Job(12 + i, 0, 256, 256, src, S, "act" if t % 2 else "dve",
                            values_evacuation(v1, t, 256 * i), tokens=block_of(t)))
    for i in range(2):
        jobs.append(Job(15, P * i, P, 256, src, S, "act", copy_to(q_mem[:, i, :])))
    for t in range(S // P):
        jobs.append(Job(16, 0, 8, 8, src, S, "dve", add_to(gates[:, t, :], K.col("a_gate_bias")),
                        tokens=block_of(t)))
    project(K, jobs, 17, feed)
    K.top = inner
    with K.stage() as block:
        @block.scalar
        def _(act):
            for half in range(2):
                x = qk_T[0:96, 8 * half:8 * half + 8, :]
                act.activation(x, x, ACT.Silu)

        @block.vector
        def _(dve):
            dve.memset(v1[:, :, :, 192:193], 1.0)
    mlstm_cell(K, qk_T[:, 0:8, :], qk_T[:, 8:16, :], v1, o_T, gates, K.col("a_h_norm"), h_aT)
    memory_attention(K, 0, [q_mem[:, i, :] for i in range(2)], cond, mod, 0)
    mixed = Split(K, 10, S)
    feed = split_tiles(K, [h_aT[0:96, j, :] for j in range(8)] + [q_mem[:, i, :] for i in range(2)], mixed)
    src = [mixed.pair(j, 96 if j < 8 else P) for j in range(10)]
    jobs = [Job(d, 0, P, P, src, S, "dve", residual(x_T[:, d, :])) for d in range(KT)]
    project(K, jobs, 8, feed)
    K.top = top


def strided_tokens(group, t):
    if group == 0:
        return block_of(t)
    return lambda x: x[:, t:S:4]


def shared_keys(K, x_T, k_T, v):
    top = K.top
    h = Split(K, KT, S)
    feed = rms_norm(K, x_T, S, K.col("kv_norm"), h)
    src = [h.pair(k) for k in range(KT)]
    jobs = [Job(i // 2, P * (i % 2), P, 256, src, S, "act" if i % 2 else "dve", copy_to(k_T[:, i, :])) for i in range(6)]
    for g in range(3):
        for t in range(S // P):
            jobs.append(Job(3 + g, 0, 256, 256, src, S, "act" if t % 2 else "dve", copy_to(v[:, g, t, :]),
                            tokens=strided_tokens(g, t)))
    project(K, jobs, 6, feed)
    head_norm(K, [(k_T[:, i, :], K.col("kv_k_norm")) for i in range(6)])
    K.top = top


def load(K, pairs):
    with K.stage() as block:
        @block.sync
        def _(sp):
            for dst, src in pairs:
                sp.dma_start(dst, src).then_inc(*K.up("array_landed", 16))
            sp.wait_ge(*K.at("array_landed", len(pairs) - 1, 16))


def merge_groups(K, lse, out_T):
    top = K.top
    spread = K.alloc(3, 2, S)
    peak, total = K.alloc(2, S), K.alloc(2, S)
    wide = K.alloc(48, 64)
    with K.stage() as block:
        @block.tensor
        def _(pe):
            pe.wait_ge(*K.at("lse_widened", 0))
            for i in range(24):
                g, pair, t = i // 8, i // 4 % 2, i % 4
                c = (g * 4 + t) * 4 + 2 * pair
                two = wide[:, c:c + 2, :].rearrange("p a b -> p (a b)")
                mm = pe.matmul(K.psum[:, i // 4, t * P:(t + 1) * P], two, K.const("identity"), start=True, stop=True)
                if t == 3:
                    mm.then_inc(*K.up("lse_spread"))

        @block.vector
        def _(dve):
            dve.tensor_copy(wide, lse.rearrange("p (a b) -> p a b", b=1).to_broadcast([P, 48, 64])
                            ).then_inc(*K.up("lse_widened"))
            for i in range(24):
                g, pair, t = i // 8, i // 4 % 2, i % 4
                if t == 0:
                    dve.wait_ge(*K.at("lse_spread", i // 4))
                out = strided_tokens(g, t)(spread[:, g, pair, :])
                ins = dve.tensor_copy(out, as_shape(K.psum[:, i // 4, t * P:(t + 1) * P], out))
            K.link(dve, ins, "dve_step")
            K.link(dve, dve.tensor_tensor(peak, spread[:, 0], spread[:, 1], ALU.max), "dve_step")
            K.link(dve, dve.tensor_tensor(peak, peak, spread[:, 2], ALU.max), "dve_step")
            for g in range(3):
                dve.tensor_tensor(spread[:, g], spread[:, g], peak, ALU.subtract).then_inc(*K.up("lse_shifted"))
            for g in range(3):
                dve.wait_ge(*K.at("weight_ready", g))
            K.link(dve, dve.tensor_tensor(total, spread[:, 0], spread[:, 1], ALU.add), "dve_step")
            K.link(dve, dve.tensor_tensor(total, total, spread[:, 2], ALU.add), "dve_step")
            K.link(dve, dve.reciprocal(total, total), "dve_step")
            for g in range(3):
                K.link(dve, dve.tensor_tensor(spread[:, g], spread[:, g], total, ALU.mult), "dve_step")
                out = out_T[:, 2 * g:2 * g + 2, :]
                dve.tensor_tensor(out, out, spread[:, g], ALU.mult)

        @block.scalar
        def _(act):
            for g in range(3):
                act.wait_ge(*K.at("lse_shifted", g))
                act.activation(spread[:, g], spread[:, g], ACT.Exp).then_inc(*K.up("weight_ready"))
    K.top = top


def dilated_layer(K, x_T, k_T, v, cond, mod):
    top = K.top
    bias = K.alloc(4, 512)
    mask = K.alloc(512)
    load(K, [(bias.rearrange("p a b -> p (a b)"), K.dram["dilated_bias"]), (mask, K.dram["dilated_mask"])])
    q_T = K.alloc(KT, S)
    inner = K.top
    h = Split(K, KT, S)
    feed = rms_norm(K, x_T, S, K.col("mix_norm1"), h)
    src = [h.pair(k) for k in range(KT)]
    jobs = [Job(i // 2, P * (i % 2), P, 256, src, S, "act" if i % 2 else "dve", copy_to(q_T[:, i, :]))
            for i in range(KT)]
    project(K, jobs, 4, feed)
    K.top = inner
    head_norm(K, [(q_T[:, i, :], K.col("b_q_norm")) for i in range(6)])
    with K.stage() as block:
        @block.vector
        def _(dve):
            every = mask.rearrange("p (a b) -> p a b", a=1).to_broadcast([P, 4, 512])
            dve.tensor_tensor(bias, bias, every, ALU.add)
    lse = K.alloc(48)
    units = []
    for g in range(3):
        for t in range(S // P):
            for head in range(4):
                pair, half = 2 * g + head // 2, head % 2
                rows = slice(64 * half, 64 * half + 64)
                own = strided_tokens(g, t)
                q = own(q_T[rows, pair, :])
                features = slice(P * (head // 2), P * (head // 2) + P)
                if g == 0 and t > 0:
                    keys, blocks, where = k_T[rows, pair, (t - 1) * P:(t + 1) * P], (t - 1, t), slice(0, 256)
                else:
                    keys, blocks = own(k_T[rows, pair, :]), (t,)
                    where = slice((1, 2, 3)[g] * P, (2, 3, 4)[g] * P)
                units.append(Unit(half, q, keys, [v[:, g, b, features] for b in blocks], q,
                                  bias=bias[:, head, where], lse=lse))
    attention(K, units, Modulation(K, 0, cond, mod, 2, 8, len(units) - 1))
    merge_groups(K, lse, q_T[:, 0:6, :])
    memory_attention(K, 1, [q_T[:, 6 + i, :] for i in range(2)], cond, mod, 10)
    mixed = Split(K, KT, S)
    feed = split_tiles(K, [q_T[:, i, :] for i in range(KT)], mixed)
    src = [mixed.pair(i) for i in range(KT)]
    jobs = [Job(d // 2, P * (d % 2), P, 256, src, S, "dve", residual(x_T[:, d, :])) for d in range(KT)]
    project(K, jobs, 4, feed)
    K.top = top



T2 = CTX + S
LAT = slice(CTX, T2)
RH, CH = 3, 64
NCH, TILES = T2 // CH, T2 // P
LEVELS = (4, 8, 16, 32, 64)
DECAY_SCALE = 0.6065306597126334


def centred_evacuation(out, taps):
    def evacuate(K, eng, ps):
        K.link(eng, eng.tensor_scalar(out, ps, taps[:, 1:2], None, ALU.mult), "dve_step")
        for a, b in ((0, CTX), (CTX, T2)):
            ins = eng.scalar_tensor_tensor(out[:, a + 1:b], ps[:, a:b - 1], taps[:, 0:1], out[:, a + 1:b],
                                           ALU.mult, ALU.add)
        K.link(eng, ins, "dve_step")
        for a, b in ((0, CTX), (CTX, T2)):
            ins = eng.scalar_tensor_tensor(out[:, a:b - 1], ps[:, a + 1:b], taps[:, 2:3], out[:, a:b - 1],
                                           ALU.mult, ALU.add)
        return ins
    return evacuate


def rope(K, tiles, cos, sin, turn):
    top = K.top
    straight = K.alloc(2, S)
    with K.stage() as block:
        @block.tensor
        def _(pe):
            for i, x in enumerate(tiles):
                if i >= 2:
                    pe.wait_ge(*K.at("rotated", i - 2))
                pe.matmul(K.psum[:, i % 2, :], turn, x[:, LAT], start=True, stop=True).then_inc(*K.up("turned"))

        @block.vector
        def _(dve):
            for i, x in enumerate(tiles):
                if i >= 2:
                    dve.wait_ge(*K.at("rotated", i - 2))
                K.link(dve, dve.tensor_tensor(straight[:, i % 2, :], x[:, LAT], cos, ALU.mult), "dve_step")
                dve.wait_ge(*K.at("turned", i))
                K.link(dve, dve.tensor_tensor(x[:, LAT], K.psum[:, i % 2, :], sin, ALU.mult), "dve_step")
                dve.tensor_tensor(x[:, LAT], x[:, LAT], straight[:, i % 2, :], ALU.add).then_inc(*K.up("rotated"))
    K.top = top


def rwkv_prepare(K, layer, pair, r, k, ddad, lora, kr, bk, pc, bonus, scratch):
    top = K.top
    ld, L = K.alloc(2, T2), K.alloc(2, T2)
    iclr, decay_before = (scratch[:, i * 2 * T2:(i + 1) * 2 * T2].rearrange("p (d n) -> p d n", d=2) for i in range(2))
    kk, norm = K.alloc(T2), K.alloc(T2)
    less = K.alloc(1)
    col = lambda name, i=pair: K.col(f"{name}{layer}")[:, i:i + 1]
    banks = lambda i: K.psum[:, 2 * i:2 * i + 2, :].rearrange("p a b -> p (a b)")[:, 0:T2]
    parts = ((0, 512), (512, T2))
    tiled = lambda x: x.rearrange("p (t n) -> p t n", n=P)
    with K.stage() as block:
        @block.tensor
        def _(pe):
            for i in range(4):
                rows = slice(32 * i, 32 * i + 32)
                for a, b in parts:
                    mm = pe.matmul(banks(i)[:, a:b], lora[rows, pair * P:(pair + 1) * P], ddad[rows, a:b],
                                   start=True, stop=True)
                mm.then_inc(*K.up("logits_ready"))
            pe.wait_ge(*K.at("kk_squared", 0))
            pe.wait_ge(*K.at("sigmoid_ready", 0))
            for a, b in parts:
                mm = pe.matmul(banks(0)[:, a:b], K.const("head_ones"), norm[:, a:b], start=True, stop=True)
            mm.then_inc(*K.up("kk_summed"))
            pe.wait_ge(*K.at("bonus_terms", 0))
            pe.wait_ge(*K.at("sigmoid_ready", 1))
            for a, b in parts:
                mm = pe.matmul(banks(1)[:, a:b], K.const("head_ones"), bonus[:, a:b], start=True, stop=True)
            mm.then_inc(*K.up("bonus_summed"))

        @block.scalar
        def _(act):
            for i in range(4):
                d, out, bias = i % 2, (ld, iclr)[i // 2], ("decay_w0", "iclr_a0")[i // 2]
                act.wait_ge(*K.at("logits_ready", i))
                act.activation(out[:, d, :], banks(i), ACT.Sigmoid, bias=col(bias, 3 * d + pair)
                               ).then_inc(*K.up("sigmoid_ready"))
            act.wait_ge(*K.at("kk_raw", 0))
            act.activation(norm, kk, ACT.Square).then_inc(*K.up("kk_squared"))
            act.wait_ge(*K.at("norm_bounded", 0))
            act.activation(norm, norm, ACT.Sqrt).then_inc(*K.up("norm_ready"))
            for d in range(2):
                act.wait_ge(*K.at("sum_before", d))
                act.activation(decay_before[:, d, :], decay_before[:, d, :], ACT.Exp).then_inc(*K.up("before_ready"))
                act.activation(ld[:, d, :], L[:, d, :], ACT.Exp, scale=-1.0).then_inc(*K.up("inverse_ready"))
            for d in range(2):
                act.wait_ge(*K.at("inverse_ready", d))
                act.activation(L[:, d, :], L[:, d, :], ACT.Exp).then_inc(*K.up("decay_ready"))

        @block.vector
        def _(dve):
            dve.tensor_scalar(kk, k, col("k_k"), None, ALU.mult).then_inc(*K.up("kk_raw"))
            for d in range(2):
                dve.wait_ge(*K.at("sigmoid_ready", d))
                K.link(dve, dve.tensor_scalar(ld[:, d, :], ld[:, d, :], -DECAY_SCALE, None, ALU.mult), "dve_step")
                turn = slice(None) if d == 0 else slice(None, None, -1)
                K.link(dve, dve.tensor_tensor_scan(L[:, d, turn], K.reset[:, :], ld[:, d, turn], 0.0,
                                                   ALU.mult, ALU.add), "dve_step")
                dve.tensor_tensor(decay_before[:, d, :], L[:, d, :], ld[:, d, :], ALU.subtract
                                  ).then_inc(*K.up("sum_before"))
            dve.wait_ge(*K.at("kk_summed", 0))
            dve.wait_ge(*K.at("kk_squared", 0))
            dve.tensor_scalar(norm, banks(0), 1e-12, None, ALU.max).then_inc(*K.up("norm_bounded"))
            dve.wait_ge(*K.at("norm_ready", 0))
            K.link(dve, dve.reciprocal(norm, norm), "dve_step")
            K.link(dve, dve.tensor_tensor(kk, kk, norm, ALU.mult), "dve_step")
            for d in range(2):
                dve.wait_ge(*K.at("before_ready", d))
                dve.tensor_tensor(kr[:, d, :, 0, :], tiled(kk), tiled(decay_before[:, d, :]), ALU.mult)
            for d in range(2):
                dve.wait_ge(*K.at("sigmoid_ready", 2 + d))
                K.link(dve, dve.tensor_tensor(bk[:, d, 0, :], kk, iclr[:, d, :], ALU.mult), "dve_step")
                dve.wait_ge(*K.at("inverse_ready", d))
                dve.tensor_tensor(bk[:, d, 0, :], bk[:, d, 0, :], ld[:, d, :], ALU.mult)
            dve.wait_ge(*K.at("keys_summed", 0))
            for d in range(2):
                dve.tensor_tensor(bk[:, d, 1, :], bk[:, d, 1, :], ld[:, d, :], ALU.mult)
                dve.wait_ge(*K.at("decay_ready", d))
                dve.tensor_tensor(kr[:, d, :, 1, :], tiled(r), tiled(L[:, d, :]), ALU.mult)
                first = CH - 1 if d == 0 else 0
                dve.tensor_copy(pc[:, d, :], L[:, d, first:T2:CH])
            dve.wait_ge(*K.at("bonus_summed", 0))
            dve.tensor_copy(bonus, banks(1))

        @block.gpsimd
        def _(pool):
            pool.tensor_scalar(less, col("k_a"), -1.0, 1.0, ALU.mult, ALU.add).then_inc(*K.up("less_ready"))
            pool.wait_ge(*K.at("less_ready", 0))
            for d in range(2):
                pool.wait_ge(*K.at("sigmoid_ready", 2 + d))
                key = bk[:, d, 1, :]
                K.link(pool, pool.tensor_scalar(key, iclr[:, d, :], col("k_a"), less, ALU.mult, ALU.add), "pool_step")
                K.link(pool, pool.tensor_tensor(key, key, k, ALU.mult), "pool_step")
            K.link(pool, pool.tensor_tensor(bonus, bk[:, 0, 1, :], bk[:, 1, 1, :], ALU.add), "keys_summed")
            K.link(pool, pool.tensor_tensor(bonus, bonus, r, ALU.mult), "pool_step")
            pool.tensor_scalar(bonus, bonus, col("r_k"), None, ALU.mult).then_inc(*K.up("bonus_terms"))
    K.top = top


def rwkv_chunks(K, kr, bk, pc, v, step, carry, y):
    top = K.top
    K.top = K.ring_at
    ab, bd = (K.alloc(2, 2, 4 * P) for _ in range(2))
    ab = ab.rearrange("p s d (e a t) -> p s d e a t", e=2, a=2)
    bd = bd.rearrange("p s d (e a t) -> p s d e a t", e=2, a=2)
    corner = K.alloc(2, 2, 4, P)
    both = K.alloc(2, 2, 4 * P)
    assert K.top <= K.ring_end
    K.top = top
    prod = K.alloc(2, 4, P)
    x = K.alloc(2, 4, P)
    b_tok, k_tok, v_tok = K.alloc(2, 2, P), K.alloc(2, 2, P), K.alloc(2, P)
    kp, nu = K.alloc(2, 2, P), K.alloc(2, 2, P)
    TT = both[:, :, 0].rearrange("p s (u t) -> p s u t", u=4)
    T = both[:, :, 1].rearrange("p s (u t) -> p s u t", u=4)
    bank = lambda i: K.psum[:, i, :]
    four = lambda i: bank(i).rearrange("p (u t) -> p u t", u=4)
    ident4 = K.const("identity").rearrange("p (a b) -> p a b", a=1).to_broadcast([P, 4, P])
    ident2 = K.const("identity").rearrange("p (a b) -> p a b", a=1).to_broadcast([P, 2, P])
    heads2 = K.const("head_ones").rearrange("p (a b) -> p a b", a=1).to_broadcast([P, 2, P])
    units = [(d, e) for d in range(2) for e in range(2)]

    def level_mask(d, i):
        return K.level_masks[:, i, d, :].rearrange("p (a b) -> p a b", a=1).to_broadcast([P, 2, P])

    NL = len(LEVELS)

    def event(t, i):
        return (t // 2 * NL + i) * 2 + t % 2

    with K.stage() as block:
        @block.tensor
        def _(pe):
            def scores(t):
                s, tok = t % 2, slice(t * P, (t + 1) * P)
                if s == 1:
                    pe.wait_ge(*K.at("inverse_begun", t - 1))
                elif t:
                    pe.wait_ge(*K.at("steps_copied", t - 2))
                    pe.wait_ge(*K.at("own_copied", t - 1))
                for d, e in units:
                    rows = slice(64 * e, 64 * e + 64)
                    rhs = kr[rows, d, t, :, :].rearrange("p a b -> p (a b)")
                    pe.matmul(bank(e)[:, 256 * d:256 * d + 256], bk[rows, d, 0, tok], rhs, start=True, stop=True)
                    pe.matmul(bank(2 + e)[:, 256 * d:256 * d + 256], bk[rows, d, 1, tok], rhs, start=True, stop=True)
                    mm = pe.matmul(bank(4 + e)[:, P * d:P * d + P], kr[rows, d, t, 0, :], bk[rows, d, 0, tok],
                                   start=True, stop=True)
                mm.then_inc(*K.up("scores_done"))
                if s == 1:
                    pe.wait_ge(*K.at("x_ready", t - 1))
                elif t:
                    pe.wait_ge(*K.at("steps_copied", t - 1))
                for d in range(2):
                    pe.transpose(bank(6)[:, d * P:(d + 1) * P], bk[:, d, 0, tok], K.const("identity"))
                    pe.transpose(bank(6)[:, (2 + d) * P:(3 + d) * P], bk[:, d, 1, tok], K.const("identity"))
                    pe.transpose(bank(7)[:, d * P:(d + 1) * P], kr[:, d, t, 0, :], K.const("identity"))
                pe.transpose(bank(7)[:, 2 * P:3 * P], v[:, tok], K.const("identity")).then_inc(*K.up("tokens_turned"))
                pe.wait_ge(*K.at("masked", t))
                pe.wait_ge(*K.at("tokens_copied", t))
                for u, (d, e) in enumerate(units):
                    mm = pe.matmul(four(6)[:, u, :], bd[:, s, d, e, 0, :], v_tok[:, s, :], start=True, stop=True)
                mm.then_inc(*K.up("bv_ready"))

            def corners(t, i):
                s = t % 2
                pe.wait_ge(*K.at("corner_ready", event(t, i)))
                if i == 0:
                    pe.wait_ge(*K.at("inverse_begun", t))
                    if s == 0:
                        pe.wait_ge(*K.at("inverse_begun", t + 1))
                else:
                    pe.wait_ge(*K.at("inverse_grown", event(t, i - 1)))
                for u in range(4):
                    mm = pe.matmul(four(3 * s)[:, u, :], corner[:, s, i % 2, u, :], T[:, s, u, :], start=True, stop=True)
                mm.then_inc(*K.up("corner_product"))

            def growth(t, i):
                s = t % 2
                pe.wait_ge(*K.at("product_copied", event(t, i)))
                for u in range(4):
                    mm = pe.matmul(four(3 * s + 1)[:, u, :], prod[:, s, u, :], TT[:, s, u, :], start=True, stop=True)
                if i + 1 < NL:
                    for u in range(4):
                        mm = pe.matmul(four(3 * s + 2)[:, u, :], TT[:, s, u, :], prod[:, s, u, :],
                                       start=True, stop=True)
                mm.then_inc(*K.up("growth_ready"))

            def solve(t):
                s = t % 2
                pe.wait_ge(*K.at("inverse_grown", event(t, NL - 1)))
                pe.wait_ge(*K.at("x_ready", t))
                if s == 0:
                    pe.wait_ge(*K.at("x_ready", t + 1))
                for u in range(4):
                    mm = pe.matmul(four(6 + s)[:, u, :], TT[:, s, u, :], x[:, s, u, :], start=True, stop=True)
                mm.then_inc(*K.up("ku_ready"))

            def own(t):
                s = t % 2
                pe.wait_ge(*K.at("ku_copied", t))
                for d in range(2):
                    rhs = ab[:, s, d, :, 1, :]
                    pe.matmul(bank(2 * s)[:, 256 * d:256 * d + 256], kp[:, s, d, :], rhs, start=True, stop=True)
                    pe.matmul(bank(2 * s + 1)[:, 0:256], v_tok[:, s, :], bd[:, s, d, :, 1, :], start=d == 0, stop=False)
                    mm = pe.matmul(bank(2 * s + 1)[:, 0:256], nu[:, s, d, :], rhs, start=False, stop=d == 1)
                mm.then_inc(*K.up("own_ready"))

            def steps(t):
                s = t % 2
                if s == 0:
                    pe.wait_ge(*K.at("inverse_grown", event(t + 1, NL - 1)))
                for d in range(2):
                    for c in range(2):
                        rows, at, at2 = slice(64 * c, 64 * c + 64), slice(d * P, (d + 1) * P), slice((2 + d) * P, (3 + d) * P)
                        ps = bank(4 + 2 * s + c)
                        pe.matmul(ps[:, at], kp[rows, s, d, :], b_tok[rows, s, d, :], start=True, stop=True)
                        pe.matmul(ps[:, at2], k_tok[rows, s, d, :], v_tok[rows, s, :], start=True, stop=False)
                        mm = pe.matmul(ps[:, at2], b_tok[rows, s, d, :], nu[rows, s, d, :], start=False, stop=True)
                mm.then_inc(*K.up("steps_ready"))

            for t in range(0, TILES, 2):
                scores(t)
                scores(t + 1)
                for i in range(NL):
                    corners(t, i)
                    corners(t + 1, i)
                    growth(t, i)
                    growth(t + 1, i)
                solve(t)
                solve(t + 1)
                own(t)
                steps(t)
                pe.wait_ge(*K.at("ku_copied", t + 1))
                own(t + 1)
                steps(t + 1)

        @block.vector
        def _(dve):
            def begin(t):
                s = t % 2
                dve.wait_ge(*K.at("scores_done", t))
                if t >= 2:
                    dve.wait_ge(*K.at("steps_ready", t - s - 1))
                for e in range(2):
                    for src, dst in ((e, ab), (2 + e, bd)):
                        out = dst[:, s, :, e].rearrange("p d a t -> p d (a t)")
                        ins = dve.tensor_tensor(out, bank(src).rearrange("p (d n) -> p d n", d=2), K.order_masks,
                                                ALU.mult)
                K.link(dve, ins, "masked")
                for e in range(2):
                    mine = lambda m: m[:, s].rearrange("p (d e) t -> p d e t", d=2)[:, :, e, :]
                    dve.tensor_tensor(mine(T), bank(4 + e)[:, 0:256].rearrange("p (d t) -> p d t", d=2),
                                      K.first_masks[:, 0], ALU.mult)
                    ins = dve.tensor_tensor(mine(TT), ab[:, s, :, e, 0, :], K.first_masks[:, 1], ALU.mult)
                K.link(dve, ins, "dve_step")
                dve.tensor_tensor(T[:, s], T[:, s], ident4, ALU.add)
                dve.tensor_tensor(TT[:, s], TT[:, s], ident4, ALU.add).then_inc(*K.up("inverse_begun"))
                dve.wait_ge(*K.at("bv_ready", t))
                by_head = lambda m: m.rearrange("p (d e) n -> p d e n", d=2)
                for e in range(2):
                    ins = dve.tensor_copy(by_head(x[:, s])[:, :, e, 64:128],
                                          by_head(four(6))[:, :, e, 64 * e:64 * e + 64])
                ins.then_inc(*K.up("x_ready"))

            def grow(t, i):
                s = t % 2
                dve.wait_ge(*K.at("growth_ready", event(t, i)))
                if i + 1 < NL:
                    two = K.psum[:, 3 * s + 1:3 * s + 3, :]
                    dve.tensor_tensor(both[:, s], both[:, s], two, ALU.subtract).then_inc(*K.up("inverse_grown"))
                else:
                    dve.tensor_tensor(TT[:, s], TT[:, s], four(3 * s + 1), ALU.subtract).then_inc(*K.up("inverse_grown"))

            def copy_own(t):
                s = t % 2
                dve.wait_ge(*K.at("own_ready", t))
                for e in range(2):
                    rows = slice(64 * e, 64 * e + 64)
                    out = kr[rows, :, t, 1, :]
                    dve.tensor_tensor(out, out, bank(2 * s)[rows].rearrange("p (d n) -> p d n", d=2)[:, :, P * e:P * e + P],
                                      ALU.subtract)
                    ins = dve.tensor_copy(y[rows, t * P:(t + 1) * P], bank(2 * s + 1)[rows, P * e:P * e + P])
                ins.then_inc(*K.up("own_copied"))

            def copy_steps(t):
                s = t % 2
                dve.wait_ge(*K.at("steps_ready", t))
                at = [step[:, :, 2 * t + c, :] for c in range(2)]
                for c in range(2):
                    ps = bank(4 + 2 * s + c)
                    for d in range(2):
                        dve.scalar_tensor_tensor(carry[:, d, 2 * t + c, :], ps[:, (2 + d) * P:(3 + d) * P],
                                                 pc[:, d, 2 * t + c:2 * t + c + 1], K.const("head_ones"),
                                                 ALU.mult, ALU.mult)
                    ins = dve.tensor_tensor(at[c], ps[:, 0:256].rearrange("p (d n) -> p d n", d=2), heads2, ALU.mult)
                ins.then_inc(*K.up("dve_step"))
                dve.wait_ge(*K.now("dve_step"))
                for c in range(2):
                    ins = dve.tensor_tensor(at[c], ident2, at[c], ALU.subtract)
                ins.then_inc(*K.up("steps_copied"))

            for t in range(0, TILES, 2):
                begin(t)
                begin(t + 1)
                for i in range(NL):
                    grow(t, i)
                    grow(t + 1, i)
                copy_own(t)
                copy_steps(t)
                copy_own(t + 1)
                copy_steps(t + 1)

        @block.scalar
        def _(act):
            def copy_tokens(t):
                s = t % 2
                act.wait_ge(*K.at("tokens_turned", t))
                if t >= 2:
                    act.wait_ge(*K.at("steps_ready", t - s - 1))
                act.copy(b_tok[:, s], bank(6)[:, 0:2 * P].rearrange("p (d n) -> p d n", d=2))
                act.copy(k_tok[:, s], bank(6)[:, 2 * P:4 * P].rearrange("p (d n) -> p d n", d=2))
                act.copy(x[:, s, :, 0:64], bank(7)[:, 0:256].rearrange("p (u n) -> p u n", u=4))
                act.copy(v_tok[:, s], bank(7)[:, 2 * P:3 * P]).then_inc(*K.up("tokens_copied"))

            for t in range(0, TILES, 2):
                copy_tokens(t)
                copy_tokens(t + 1)
                for i in range(NL):
                    for tile in (t, t + 1):
                        act.wait_ge(*K.at("corner_product", event(tile, i)))
                        act.copy(prod[:, tile % 2], four(3 * (tile % 2))).then_inc(*K.up("product_copied"))
                for s in range(2):
                    act.wait_ge(*K.at("ku_ready", t + s))
                    ku = bank(6 + s).rearrange("p (u w n) -> p u w n", u=4, w=2)
                    parts = lambda m: m[:, s].rearrange("p d (e n) -> p (d e) n", e=2)
                    act.copy(parts(kp), ku[:, :, 0, :])
                    act.mul(parts(nu), ku[:, :, 1, :], -1.0).then_inc(*K.up("ku_copied"))

        @block.gpsimd
        def _(pool):
            for t in range(0, TILES, 2):
                for i in range(NL):
                    for tile in (t, t + 1):
                        s = tile % 2
                        if i == 0:
                            pool.wait_ge(*K.at("masked", tile))
                        if i >= 2:
                            pool.wait_ge(*K.at("corner_product", event(tile, i - 2)))
                        for d in range(2):
                            ins = pool.tensor_tensor(corner[:, s, i % 2, 2 * d:2 * d + 2, :], ab[:, s, d, :, 0, :],
                                                     level_mask(d, i), ALU.mult)
                        ins.then_inc(*K.up("corner_ready"))
    K.top = top


def rwkv_scan(K, kr, pc, step, carry, y, first_out):
    order = [list(range(NCH)), list(range(CTX // CH - 1, -1, -1)) + list(range(NCH - 1, CTX // CH - 1, -1))]
    before = {c: [(d, order[d][order[d].index(c) - 1]) for d in range(2) if order[d].index(c) > 0]
              for c in range(first_out, NCH)}
    due = {}
    for c in before:
        due.setdefault(max(order[d].index(prior) for d, prior in before[c]), []).append(c)
    with K.stage() as block:
        @block.tensor
        def _(pe):
            def outputs(c):
                at = K.psum[:, 4 + c // 8, (c % 8) * CH:(c % 8 + 1) * CH]
                for n, (d, prior) in enumerate(before[c]):
                    mm = pe.matmul(at, carry[:, d, prior, :], kr[:, d, c // 2, 1, (c % 2) * CH:(c % 2 + 1) * CH],
                                   start=n == 0, stop=n == len(before[c]) - 1)
                return mm

            for c in due.get(0, []):
                outputs(c)
            for j in range(1, NCH - 1):
                for d in range(2):
                    if j >= 2:
                        pe.wait_ge(*K.at("state_ready", 2 * (j - 2) + d))
                    pe.matmul(K.psum[:, 2 * (j % 2) + d, 0:P], step[:, d, order[d][j], :], carry[:, d, order[d][j - 1], :],
                              start=True, stop=True).then_inc(*K.up("state_moved"))
                if j >= 2:
                    for c in due.get(j - 1, []):
                        mm = outputs(c)
            pe.wait_ge(*K.at("state_ready", 2 * (NCH - 3) + 1))
            for c in due[NCH - 2]:
                mm = outputs(c)
            mm.then_inc(*K.up("outputs_ready"))

        @block.vector
        def _(dve):
            for j in range(1, NCH - 1):
                for d in range(2):
                    c = order[d][j]
                    dve.wait_ge(*K.at("state_moved", 2 * (j - 1) + d))
                    dve.scalar_tensor_tensor(carry[:, d, c, :], K.psum[:, 2 * (j % 2) + d, 0:P], pc[:, d, c:c + 1],
                                             carry[:, d, c, :], ALU.mult, ALU.add).then_inc(*K.up("state_ready"))
            dve.wait_ge(*K.at("outputs_ready", 0))
            a = first_out * CH
            for lo, hi in ((a, 512), (512, T2)):
                out = y[:, lo:hi]
                dve.tensor_tensor(out, out, K.psum[:, 4:6, :].rearrange("p a b -> p (a b)")[:, lo:hi], ALU.add)


def rwkv_finish(K, layer, pair, y, v, bonus, gate, out, a):
    top = K.top
    n = T2 - a
    tok = slice(a, T2)
    centred, sq, rstd = K.alloc(n), K.alloc(n), K.alloc(n)
    col = lambda name: K.col(f"{name}{layer}")[:, pair:pair + 1]
    banks = lambda i: K.psum[:, 2 * i:2 * i + 2, :].rearrange("p a b -> p (a b)")[:, 0:n]
    cuts = [(lo, min(lo + 512, n)) for lo in range(0, n, 512)]
    with K.stage() as block:
        @block.tensor
        def _(pe):
            for lo, hi in cuts:
                mm = pe.matmul(banks(0)[:, lo:hi], K.const("head_ones"), y[:, a + lo:a + hi], start=True, stop=True)
            mm.then_inc(*K.up("mean_ready"))
            pe.wait_ge(*K.at("deviation_squared", 0))
            for lo, hi in cuts:
                mm = pe.matmul(banks(1)[:, lo:hi], K.const("head_ones"), sq[:, lo:hi], start=True, stop=True)
            mm.then_inc(*K.up("variance_ready"))

        @block.vector
        def _(dve):
            dve.wait_ge(*K.at("mean_ready", 0))
            dve.scalar_tensor_tensor(centred, banks(0), -1.0 / HD, y[:, tok], ALU.mult, ALU.add
                                     ).then_inc(*K.up("centred"))
            dve.wait_ge(*K.at("std_ready", 0))
            K.link(dve, dve.reciprocal(rstd, rstd), "dve_step")
            K.link(dve, dve.scalar_tensor_tensor(centred, centred, col("gn_g"), rstd, ALU.mult, ALU.mult), "dve_step")
            dve.wait_ge(*K.at("bonus_ready", 0))
            K.link(dve, dve.scalar_tensor_tensor(centred, centred, col("gn_b"), bonus[:, tok], ALU.add, ALU.add),
                   "dve_step")
            dve.tensor_tensor(out[:, tok], centred, gate, ALU.mult)

        @block.scalar
        def _(act):
            act.wait_ge(*K.at("centred", 0))
            act.activation(sq, centred, ACT.Square).then_inc(*K.up("deviation_squared"))
            act.wait_ge(*K.at("variance_ready", 0))
            act.activation(rstd, banks(1), ACT.Sqrt, scale=1.0 / HD, bias=K.const("eps_gn")).then_inc(*K.up("std_ready"))

        @block.gpsimd
        def _(pool):
            pool.tensor_tensor(bonus[:, tok], bonus[:, tok], v[:, tok], ALU.mult).then_inc(*K.up("bonus_ready"))
    K.top = top


def layer_norm(K, layer, x, n):
    top = K.top
    sq, mean, rstd = K.alloc(2, n), K.alloc(n), K.alloc(n)
    banks = lambda i: K.psum[:, 2 * i:2 * i + 2, :].rearrange("p a b -> p (a b)")[:, 0:n]
    cuts = [(lo, min(lo + 512, n)) for lo in range(0, n, 512)]
    g, b = K.col(f"ln_g{layer}"), K.col(f"ln_b{layer}")
    with K.stage() as block:
        @block.tensor
        def _(pe):
            for k in range(KT):
                for lo, hi in cuts:
                    mm = pe.matmul(banks(0)[:, lo:hi], K.const("ones"), x[:, k, lo:hi], start=k == 0, stop=k == KT - 1)
            mm.then_inc(*K.up("mean_ready"))
            for k in range(KT):
                pe.wait_ge(*K.at("square_ready", k))
                for lo, hi in cuts:
                    mm = pe.matmul(banks(1)[:, lo:hi], K.const("ones"), sq[:, k % 2, lo:hi], start=k == 0, stop=k == KT - 1)
                mm.then_inc(*K.up("square_summed"))

        @block.vector
        def _(dve):
            dve.wait_ge(*K.at("mean_ready", 0))
            K.link(dve, dve.tensor_scalar(mean, banks(0), -1.0 / D, None, ALU.mult), "dve_step")
            for k in range(KT):
                dve.tensor_tensor(x[:, k, :], x[:, k, :], mean, ALU.add).then_inc(*K.up("centred"))
            dve.wait_ge(*K.at("std_ready", 0))
            K.link(dve, dve.reciprocal(rstd, rstd), "dve_step")
            for k in range(KT):
                dve.scalar_tensor_tensor(x[:, k, :], x[:, k, :], g[:, k:k + 1], rstd, ALU.mult, ALU.mult
                                         ).then_inc(*K.up("scaled"))

        @block.scalar
        def _(act):
            for k in range(KT):
                act.wait_ge(*K.at("centred", k))
                if k >= 2:
                    act.wait_ge(*K.at("square_summed", k - 2))
                act.activation(sq[:, k % 2, :], x[:, k, :], ACT.Square).then_inc(*K.up("square_ready"))
            act.wait_ge(*K.at("square_summed", KT - 1))
            act.activation(rstd, banks(1), ACT.Sqrt, scale=1.0 / D, bias=K.const("eps_ln")).then_inc(*K.up("std_ready"))
            for k in range(KT):
                act.wait_ge(*K.at("scaled", k))
                act.activation(x[:, k, :], x[:, k, :], ACT.Identity, bias=b[:, k:k + 1])
    K.top = top


def gated_residual(x, mod, tile, a):
    def evacuate(K, eng, ps):
        x_new = x
        K.link(eng, eng.tensor_scalar(x_new, x_new, ALPHA, None, ALU.mult), "dve_step")
        for (lo, hi), which in (((0, CTX), 1), ((CTX, T2), 0)):
            if hi > a:
                ins = eng.scalar_tensor_tensor(x_new[:, lo - a:hi - a], ps[:, lo - a:hi - a],
                                               mod[:, 16 + tile, which:which + 1], x_new[:, lo - a:hi - a],
                                               ALU.mult, ALU.add)
        return ins
    return evacuate


def second_layer(K, layer, x, cond, mods):
    top = K.top
    final = layer == 1
    a = CTX if final else 0
    n = T2 - a
    mod = mods[layer]
    conv, gates = K.alloc(10, T2), K.alloc(8, T2)
    q, nq = K.alloc(3, T2), K.alloc(2, T2)
    mark = K.top
    kg, nk, v_tok = K.alloc(T2), K.alloc(2, T2), K.alloc(TILES, 384)
    inner = K.top
    h = Split(K, KT, T2)
    full = q[:, 0:2, :]

    def low(eng, k):
        feed_low(K, eng, k, h.lo[:, k, :], full[:, k % 2, :], h.hi[:, k, :])

    def modulate(dve):
        for k in range(KT):
            if k >= 2:
                dve.wait_ge(*K.at("lo_odd" if k % 2 else "lo_even", k // 2 - 1))
            dve.tensor_scalar(full[:, k % 2, LAT], x[:, k, LAT], mod[:, 8 + k, 0:1], mod[:, k, 0:1],
                              ALU.mult, ALU.add)
            dve.tensor_scalar(full[:, k % 2, 0:CTX], x[:, k, 0:CTX], mod[:, 8 + k, 1:2], mod[:, k, 1:2],
                              ALU.mult, ALU.add).then_inc(*K.up("modulated"))
            if k % 2:
                low(dve, k - 1)

    def round_modulated(act):
        for k in range(KT):
            act.wait_ge(*K.at("modulated", k))
            act.copy(h.hi[:, k, :], full[:, k % 2, :]).then_inc(*K.up("tile_hi"))

    def odd_lows(pool):
        for k in range(1, KT, 2):
            low(pool, k)
    feed = Feed(K, KT, dve=modulate, act=round_modulated, pool=odd_lows)
    whole = [h.pair(k) for k in range(KT)]
    asked = [tuple(x[:, a:T2] for x in h.pair(k)) for k in range(KT)]
    taps = K.col(f"rwkv_conv{layer}")
    jobs = []

    def feature(src, m, engine, evacuate):
        i = len(jobs)
        jobs.append(Job(i // 2, P * (i % 2), P, 256, src, m, engine, evacuate))
    for i in range(10):
        feature(whole, T2, "dve", centred_evacuation(conv[:, i, :], taps[:, 3 * i:3 * i + 3]))
    for i in range(3):
        feature(asked, n, "act", act_to(gates[:, i, a:T2], ACT.Silu))
    for i in range(3):
        feature(asked, n, "dve", copy_to(q[:, i, a:T2]))
    feature(whole, T2, "dve", copy_to(kg))
    for i in range(3):
        feature(asked, n, "act", act_to(gates[:, 3 + i, a:T2], ACT.Silu))
    for i in range(2):
        feature(asked, n, "dve", copy_to(nq[:, i, a:T2]))
    for i in range(2):
        feature(whole, T2, "dve", copy_to(nk[:, i, :]))
    for i in range(2):
        feature(asked, n, "act", act_to(gates[:, 6 + i, a:T2], ACT.Silu))
    for t in range(TILES):
        jobs.append(Job(13, 0, 256, 256, whole, T2, "act" if t % 2 else "dve", copy_to(v_tok[:, t, 0:256]),
                        tokens=block_of(t)))
    for t in range(TILES):
        jobs.append(Job(14, 0, P, P, whole, T2, "act" if t % 2 else "dve", copy_to(v_tok[:, t, 256:384]),
                        tokens=block_of(t)))
    project(K, jobs, 15, feed, ahead=0 if final else RING)

    K.top = inner
    cos, sin, turn = K.alloc(S), K.alloc(S), K.alloc(P)
    bias, mask = K.alloc(4, 16, 64), K.alloc(64)
    load(K, [(cos, K.dram["rope_cos"]), (sin, K.dram["rope_sin"]), (turn, K.dram["rope_turn"]),
             (bias.rearrange("p a b c -> p (a b c)"), K.dram["window_bias"][layer]), (mask, K.dram["window_mask"])])
    head_norm(K, [(q[:, i, a:T2], K.col(f"gqa_q_norm{layer}")) for i in range(3)] + [(kg, K.col(f"gqa_k_norm{layer}"))])
    rope(K, [q[:, i, :] for i in range(3)] + [kg], cos, sin, turn)
    with K.stage() as block:
        @block.vector
        def _(dve):
            every = mask.rearrange("p (a b) -> p a b", a=1).to_broadcast([P, 64, 64])
            rows = bias.rearrange("p a b c -> p (a b) c")
            dve.tensor_tensor(rows, rows, every, ALU.add)
    units = []
    for half in range(2):
        rows = slice(64 * half, 64 * half + 64)
        for t in range(TILES):
            tok = slice(t * P, (t + 1) * P)
            if t * P < a:
                continue
            in_ctx = (t + 1) * P <= CTX
            keys, blocks = slice(0, CTX if in_ctx else T2), range(CTX // P if in_ctx else TILES)
            for i in range(3):
                units.append(Unit(half, q[rows, i, tok], kg[rows, keys], [v_tok[:, b, 256:384] for b in blocks],
                                  q[rows, i, tok]))
            for i in range(2):
                window = None
                if not in_ctx:
                    r0 = 2 * (t - CTX // P)
                    window = bias[:, 2 * i + half, 7 - r0:15 - r0, :].rearrange("p a b -> p (a b)")
                units.append(Unit(half, nq[rows, i, tok], nk[rows, i, keys],
                                  [v_tok[:, b, P * i:P * i + P] for b in blocks], nq[rows, i, tok], bias=window))
    attention(K, units, None if final else Modulation(K, 1, cond, mods[1], 0, 12, len(units) - 1), ahead=0)

    with K.stage() as block:
        @block.vector
        def _(dve):
            for i in range(3):
                dve.tensor_tensor(q[:, i, a:T2], q[:, i, a:T2], gates[:, 3 + i, a:T2], ALU.mult)
            for i in range(2):
                dve.tensor_tensor(nq[:, i, a:T2], nq[:, i, a:T2], gates[:, 6 + i, a:T2], ALU.mult)

        @block.scalar
        def _(act):
            act.activation(conv[0:64, 9, :], conv[0:64, 9, :], ACT.Tanh)
    spare = gates[:, 3:8, :].rearrange("p a b -> p (a b)")
    step = spare[:, 0:2 * NCH * P].rearrange("p (d c n) -> p d c n", d=2, c=NCH)
    pc = spare[:, 2 * NCH * P:2 * NCH * P + 2 * NCH].rearrange("p (d c) -> p d c", d=2)
    K.top = mark
    K.reset = K.alloc(T2)
    K.order_masks, K.first_masks = K.alloc(2, 2 * P), K.alloc(2, 2, P)
    K.level_masks, lora = K.alloc(len(LEVELS), 2, P), K.alloc(RH * P)
    load(K, [(K.reset, K.dram["reset"]), (K.order_masks.rearrange("p a b -> p (a b)"), K.dram["order_masks"]),
             (K.first_masks.rearrange("p a b c -> p (a b c)"), K.dram["first_masks"]),
             (K.level_masks.rearrange("p a b c -> p (a b c)"), K.dram["level_masks"]), (lora, K.dram["lora"][layer])])
    kr, bk = K.alloc(2, TILES, 2, P), K.alloc(2, 2, T2)
    carry, bonus = K.alloc(2, NCH, P), K.alloc(T2)
    for pair in range(RH):
        r, k, v = conv[:, pair, :], conv[:, 3 + pair, :], conv[:, 6 + pair, :]
        y = k
        rwkv_prepare(K, layer, pair, r, k, conv[:, 9, :], lora, kr, bk, pc, bonus,
                     carry.rearrange("p a b c -> p (a b c)"))
        rwkv_chunks(K, kr, bk, pc, v, step, carry, y)
        rwkv_scan(K, kr, pc, step, carry, y, a // CH)
        rwkv_finish(K, layer, pair, y, v, bonus, gates[:, pair, a:T2], r, a)
    K.top = mark
    mixed = Split(K, KT, n)
    feed = split_tiles(K, [conv[:, i, a:T2] for i in range(3)] + [q[:, i, a:T2] for i in range(3)]
                + [nq[:, i, a:T2] for i in range(2)], mixed)
    src = [mixed.pair(i) for i in range(KT)]
    jobs = [Job(d // 2, P * (d % 2), P, 256, src, n, "dve", gated_residual(x[:, d, a:T2], mod, d, a)) for d in range(KT)]
    project(K, jobs, 4, feed)
    K.top = inner
    layer_norm(K, layer, x[:, :, a:T2], n)
    K.top = top


def chunk_plan():
    full = [(k * P, P) for k in range(KT)]
    plan = []

    def add(names, layer, cols, rows=None):
        plan.append((names, layer, cols, rows or full))

    def both(a, b, n=P):
        return [(a, n), (b, n)]

    def ffn_chunks(which, layer):
        for f in range(FT):
            add([f"ffn{which}_w_gate", f"ffn{which}_w_up"], layer, [[(f * P, P)], [(f * P, P)]])
        for d in range(KT):
            for half in range(2):
                add([f"ffn{which}_w_down"], layer, [[(d * P, P)]],
                    [((half * (FT // 2) + f) * P, P) for f in range(FT // 2)])

    def span(name, layer, start, stop, step=256, rows=None):
        for c in range(start, stop, step):
            add([name], layer, [[(c, min(step, stop - c))]], rows)

    w = ML_H * ML_D
    ffn_chunks(1, 0)
    span("a_w_in", 0, 0, 2 * w, 192)
    span("a_w_in", 0, 3 * w, 4 * w, 192)
    span("a_w_in", 0, 2 * w, 3 * w)
    span("a_w_in", 0, 4 * w + 8, 4 * w + 8 + 256)
    span("a_w_in", 0, 4 * w, 4 * w + 8)
    span("w_mem_kv", 0, 0, 512)
    span("w_mod_2", 0, 0, 512)
    span("a_w_out", 0, 0, D, P, [(96 * i, 96) for i in range(8)] + [(w + P * i, P) for i in range(2)])
    ffn_chunks(2, 0)
    span("w_kv", None, 0, 1536)
    ffn_chunks(1, 1)
    span("b_w_q", 0, 0, D)
    span("w_mod_2", 0, 512, 2560)
    span("w_mem_kv", 1, 0, 512)
    span("w_mod_2", 0, 2560, 3072)
    span("b_w_out", 0, 0, D)
    ffn_chunks(2, 1)
    second_plan(add, span)
    return plan


def second_plan(add, span):
    tiles = lambda at, n: [[(at + P * i, P)] for i in range(n)]
    paired = lambda at: [[(at + HD * i, HD), (at + HD * (i + 3), HD)] for i in range(3)]
    mixed = [[(P * i, P)] for i in range(3)] + paired(384) + tiles(768, 2)
    for layer in range(2):
        order = (tiles(0, 10) + tiles(1280, 3) + paired(1664) + tiles(2048, 1) + paired(2304)
                 + tiles(2688, 2) + tiles(2944, 2) + tiles(3456, 2))
        for i in range(0, len(order), 2):
            add(["w_in_2"], layer, [order[i] + order[i + 1]])
        add(["w_in_2"], layer, [[(3200, 256)]])
        add(["w_in_2"], layer, [[(2176, P)]])
        if layer == 0:
            span("w_mod_2", 1, 0, 3 * D)
        span("w_out_2", layer, 0, D, rows=mixed)


def chunk_width(chunk):
    names, layer, cols, rows = chunk
    return len(rows) * sum(n for part in cols for _, n in part)


def build(nc, dram, out, cols, n_cols, consts, n_consts):
    plan = [("weights", i, chunk_width(c)) for i, c in enumerate(chunk_plan())]
    with ExitStack() as ctx:
        K = Core(nc, ctx, dram, cols, consts, plan)
        K.cols_sb, K.consts_sb = K.alloc(n_cols), K.alloc(n_consts)
        x = K.alloc(KT, T2)
        x_T = x[:, :, LAT]
        cond = K.alloc(KT, 2)
        mods = [K.alloc(24, 2) for _ in range(2)]
        top = K.top
        load(K, [(K.cols_sb, dram["columns"]), (K.consts_sb, dram["constants"]),
                 (x_T, dram["x_T"]),
                 (cond.rearrange("p a b -> p (a b)"), dram["conditions"])])
        spare = x[:, :, 0:CTX]
        with K.stage() as block:
            @block.scalar
            def _(act):
                act.activation(cond, cond, ACT.Silu)
        ffn(K, x_T, K.col("ffn1_norm0"), spare)
        mlstm_layer(K, x_T, cond, mods[0])
        k_T, v = K.alloc(6, S), K.alloc(3, S // P, 256)
        ffn(K, x_T, K.col("ffn2_norm0"), spare)
        shared_keys(K, x_T, k_T, v)
        ffn(K, x_T, K.col("ffn1_norm1"), spare)
        dilated_layer(K, x_T, k_T, v, cond, mods[0])
        ffn(K, x_T, K.col("ffn2_norm1"), spare)
        K.top = top
        load(K, [(x[:, :, 0:CTX], dram["ctx_T"])])
        second_layer(K, 0, x, cond, mods)
        second_layer(K, 1, x, cond, mods)
        with K.stage() as block:
            @block.sync
            def _(sp):
                sp.dma_start(out, x_T).then_inc(*K.up("result_stored", 16))
                sp.wait_ge(*K.at("result_stored", 0, 16))


def host_columns(inputs):
    import numpy as np

    blocks = {}

    def per_feature(name, values):
        blocks[name] = values.reshape(-1, P).T

    for i in range(2):
        for name in ("ffn1_norm", "ffn2_norm", "mix_norm", "mem_norm"):
            per_feature(f"{name}{i}", inputs[name][i])
        for name in ("mem_q_norm", "mem_k_norm"):
            per_feature(f"{name}{i}", np.tile(inputs[name][i], 2))
    per_feature("kv_norm", inputs["kv_norm"])
    per_feature("b_q_norm", np.tile(inputs["b_q_norm"][0], 2))
    per_feature("kv_k_norm", np.tile(inputs["kv_k_norm"], 2))

    def rows96(a):
        full = np.zeros((P, a.shape[1]), a.dtype)
        full[0:96] = a
        return full
    for i in range(2):
        per_feature(f"b_mod{i}", inputs["b_mod_2"][i])
        blocks[f"rwkv_conv{i}"] = inputs["rwkv_conv_2"][i].reshape(3, 10, P).transpose(2, 1, 0).reshape(P, 30)
        per_feature(f"decay_w0{i}", inputs["decay_w0_2"][i])
        per_feature(f"iclr_a0{i}", inputs["iclr_a0_2"][i])
        for name in ("k_k", "k_a", "r_k", "gn_g", "gn_b"):
            per_feature(f"{name}{i}", inputs[f"rwkv_{name}_2"][i].reshape(-1))
        for name in ("gqa_q_norm", "gqa_k_norm"):
            per_feature(f"{name}{i}", np.tile(inputs[f"{name}_2"][i], 2))
        for name in ("ln_g", "ln_b"):
            per_feature(f"{name}{i}", inputs[f"{name}_2"][i])
    conv = inputs["a_conv"][0].reshape(4, 16, 96)
    blocks["a_conv"] = rows96(conv.transpose(2, 1, 0).reshape(96, 64))
    blocks["a_h_norm"] = rows96(inputs["a_h_norm"][0].reshape(8, 96).T)
    blocks["a_gate_bias"] = np.tile(inputs["a_gate_bias"], (P, 1))
    return blocks


def shape_constants():
    import numpy as np

    f = np.float32
    s, t = np.arange(P)[:, None], np.arange(P)[None, :]
    core = {
        "eps_rms": np.full((P, 1), RMS_EPS, f), "eps_ln": np.full((P, 1), LN_EPS, f),
        "eps_gn": np.full((P, 1), GN_EPS, f),
        "identity": np.eye(P, dtype=f), "ones": np.ones((P, P), f),
        "head_ones": (s // HD == t // HD).astype(f),
        "upto": (s <= t).astype(f),
        "causal_add": np.where(t <= s, 0, -1e30).astype(f),
    }
    return core


def dilated_tables():
    import math

    import numpy as np

    q = np.arange(P)[:, None]
    k2, k = np.arange(2 * P)[None, :], np.arange(P)[None, :]
    m0 = q + P - k2
    m1 = q - k
    m2 = q // 4 - k // 4
    ok2 = (m2 >= 0) & (q % 4 == k % 4)
    dist = np.concatenate([m0, 4 * m1, 16 * m2], 1)
    ok = np.concatenate([(m0 >= 0) & (m0 <= P), m1 >= 0, ok2], 1)
    dist = np.where(ok, dist, 0)
    d_f = np.maximum(dist, 1).astype(np.float32)
    large = 16 + (np.log(d_f / np.float32(16)) / np.float32(math.log(128)) * np.float32(16)).astype(np.int32)
    bucket = np.where(dist < 16, dist, np.minimum(large, 31))
    return bucket, np.where(ok, 0, -1e30).astype(np.float32)


def second_arrays(inputs):
    import numpy as np

    f = np.float32
    t = np.arange(S)
    inv_freq = f(10000.0) ** (-np.arange(16, dtype=f) / f(16))
    ang_r, ang_c = (t // 64).astype(f)[:, None] * inv_freq, (t % 64).astype(f)[:, None] * inv_freq
    ang = np.tile(np.concatenate([ang_r, ang_r, ang_c, ang_c], -1).T, (2, 1))
    turn = np.zeros((P, P), f)
    for m in range(P):
        turn[m + 16 if m % 32 < 16 else m - 16, m] = -1 if m % 32 < 16 else 1

    parity, c = np.arange(P)[:, None, None] // 64, np.arange(P)[:, None, None] % 64
    slot, kc = np.arange(16)[None, :, None], np.arange(64)[None, None, :]
    start = np.clip(c - 8, 0, 48)
    inside = (kc >= start) & (kc < start + 16)
    dr, dc = np.clip(slot - parity, 0, 14), np.where(inside, kc - c + 15, 0)
    window = inputs["na_rpb_2"][:, :, dr, dc].transpose(0, 2, 1, 3, 4)

    s, u = np.arange(P)[:, None], np.arange(P)[None, :]
    chunk = s // CH == u // CH
    before = [s < u, s > u]
    order = np.stack([np.stack([chunk & before[d], chunk & (before[d] | (s == u))]) for d in range(2)])
    pairs = np.stack([np.stack([(s // 2 == u // 2) & before[1 - d] for d in range(2)]),
                      np.stack([(s // 2 == u // 2) & before[d] for d in range(2)])])
    levels = np.stack([np.stack([(s // n == u // n) & (s // (n // 2) != u // (n // 2)) & before[d] for d in range(2)])
                       for n in LEVELS])
    flat = lambda m: np.ascontiguousarray(np.moveaxis(m, -2, 0).reshape(P, -1).astype(f))
    lora = np.concatenate([inputs["decay_w2_2"].reshape(2, 64, 384), inputs["iclr_a2_2"].reshape(2, 64, 384)], 1)
    return {
        "rope_cos": np.cos(ang).astype(f), "rope_sin": np.sin(ang).astype(f), "rope_turn": turn,
        "window_bias": np.ascontiguousarray(window.reshape(2, P, 4096)),
        "window_mask": np.where(inside[:, 0, :], 0, -1e30).astype(f),
        "reset": np.tile((np.arange(T2) % CH != 0).astype(f), (P, 1)),
        "order_masks": flat(order), "first_masks": -flat(pairs), "level_masks": flat(levels),
        "lora": np.ascontiguousarray(lora),
    }


def kernel(**inputs):
    import numpy as np
    import concourse.bacc as bacc
    from concourse.bass_utils import run_bass_kernel_spmd

    inputs = {name: np.asarray(a) for name, a in inputs.items()}
    plan = chunk_plan()
    weights = np.zeros((len(plan), P, CHUNK), np.float32)
    for i, (names, layer, cols, rows) in enumerate(plan):
        width = sum(n for part in cols for _, n in part)
        for k, row in enumerate(rows):
            to = 0
            for r, nr in row if isinstance(row, list) else [row]:
                at = k * width
                for name, part in zip(names, cols):
                    w = inputs[name] if layer is None else inputs[name][layer]
                    for c, n in part:
                        weights[i, to:to + nr, at:at + n] = w[r:r + nr, c:c + n]
                        at += n
                to += nr

    def joined(blocks):
        where, at = {}, 0
        for name, a in blocks.items():
            where[name] = (at, a.shape[1])
            at += a.shape[1]
        return where, np.ascontiguousarray(np.concatenate(list(blocks.values()), 1))

    def feature_major(a):
        n = a.shape[0]
        return np.ascontiguousarray(a.T.reshape(KT, P, n).transpose(1, 0, 2))

    cols_at, columns = joined(host_columns(inputs))
    consts_at, constants = joined(shape_constants())
    bucket, mask = dilated_tables()
    group_of = np.repeat(np.arange(3), [2 * P, P, P])
    bias = np.stack([inputs["rel_bias"][bucket, group_of[None, :] * 4 + h] for h in range(4)], 1)
    arrays = {
        "weights": weights, "columns": columns, "constants": constants,
        "x_T": feature_major(inputs["x"][0]), "mem_T": feature_major(inputs["mem"][0]).reshape(P, KT * M),
        "ctx_T": feature_major(inputs["ctx_2"][0]),
        "conditions": feature_major(np.stack([inputs["c_2"][0], inputs["c_ctx_2"]])).reshape(P, KT * 2),
        **second_arrays(inputs),
        "dilated_bias": np.ascontiguousarray(bias.reshape(P, 2048)), "dilated_mask": mask,
    }
    nc = bacc.Bacc("TRN2", target_bir_lowering=False, num_devices=1)
    dram = {n: nc.dram_tensor(n, a.shape, mybir.dt.float32, kind="ExternalInput").ap() for n, a in arrays.items()}
    out = nc.dram_tensor("out", (P, KT * S), mybir.dt.float32, kind="ExternalOutput").ap()
    build(nc, dram, out, cols_at, columns.shape[1], consts_at, constants.shape[1])
    r = run_bass_kernel_spmd(nc, [arrays], core_ids=[0])
    got = r.results[0]["out"].reshape(P, KT, S)
    return np.ascontiguousarray(got.transpose(2, 1, 0).reshape(1, S, D))
```
